# Optimizing a Trainium2 kernel written in Bass

```python
import math
import jax, jax.numpy as jnp
from jax import lax
import numpy as np

D_MODEL = 1024
BATCH = 1
SEQ = 512
DEPTH = 1

D_MIX = D_MODEL
D_RWKV = D_MIX // 2
D_S5 = D_MIX - D_RWKV
RWKV_HEAD = 64
N_RWKV_HEADS = D_RWKV // RWKV_HEAD
LORA_W = 64
LORA_A = 64
LORA_G = 128
S5_CH = 16
N_S5_GROUPS = D_S5 // S5_CH
S5_STATE = 64
D_FF = ((8 * D_MODEL // 3 + 255) // 256) * 256
D_SHIFT = 3 * D_RWKV + LORA_W + LORA_A + LORA_G
D_IN = D_SHIFT + D_S5
NORM_EPS = 1e-6
LNX_EPS = 64e-5
DT_MIN = 1e-3
DT_MAX = 1e-1


def rms_norm(x, eps=NORM_EPS):
    xf = x.astype(jnp.float32)
    y = xf * lax.rsqrt(jnp.mean(xf * xf, axis=-1, keepdims=True) + eps)
    return y.astype(x.dtype)

def modulate(h, shift, scale):
    return h * (1.0 + scale[:, None, :]) + shift[:, None, :]

def rwkv7_time_mix(z, w0, w2, a0, a2, g2, k_k, k_a, r_k, lnx_w, lnx_b):
    out_dtype = z.dtype
    z = z.astype(jnp.float32)
    bsz, seq = z.shape[0], z.shape[1]
    H, N = N_RWKV_HEADS, RWKV_HEAD
    o = 0
    r = z[..., o:o + D_RWKV]; o += D_RWKV
    k = z[..., o:o + D_RWKV]; o += D_RWKV
    v = z[..., o:o + D_RWKV]; o += D_RWKV
    w_lo = z[..., o:o + LORA_W]; o += LORA_W
    a_lo = z[..., o:o + LORA_A]; o += LORA_A
    g_lo = z[..., o:o + LORA_G]

    w = -jax.nn.softplus(-(w0 + jnp.tanh(w_lo) @ w2)) - 0.5
    decay = jnp.exp(-jnp.exp(w))
    a = jax.nn.sigmoid(a0 + a_lo @ a2)
    g = jax.nn.sigmoid(g_lo) @ g2
    kk = (k * k_k).reshape(bsz, seq, H, N)
    kk = kk / jnp.maximum(jnp.linalg.norm(kk, axis=-1, keepdims=True), 1e-12)
    k = k * (1.0 + (a - 1.0) * k_a)

    heads = lambda t: t.reshape(bsz, seq, H, N)
    r_h, k_h, v_h, w_h, a_h = heads(r), heads(k), heads(v), heads(decay), heads(a)
    tm = lambda t: jnp.transpose(t, (1, 0, 2, 3))
    xs = (tm(r_h), tm(w_h), tm(k_h), tm(v_h), tm(-kk), tm(kk * a_h))

    def step(S, inp):
        r_t, w_t, k_t, v_t, a_t, b_t = inp
        sa = jnp.einsum("bhvk,bhk->bhv", S, a_t)
        S = S * w_t[:, :, None, :] + sa[..., None] * b_t[:, :, None, :] + v_t[..., None] * k_t[:, :, None, :]
        y = jnp.einsum("bhvk,bhk->bhv", S, r_t)
        return S, y

    S0 = jnp.zeros((bsz, H, N, N), jnp.float32)
    _, y = lax.scan(step, S0, xs)
    y = jnp.transpose(y, (1, 0, 2, 3))

    mu = jnp.mean(y, axis=-1, keepdims=True)
    var = jnp.mean(jnp.square(y - mu), axis=-1, keepdims=True)
    y = (y - mu) * lax.rsqrt(var + LNX_EPS) * lnx_w.reshape(H, N) + lnx_b.reshape(H, N)
    y = y + jnp.sum(r_h * k_h * r_k, axis=-1, keepdims=True) * v_h
    return (y.reshape(bsz, seq, D_RWKV) * g).astype(out_dtype)

def _ssm_combine(e1, e2):
    ar1, ai1, br1, bi1 = e1
    ar2, ai2, br2, bi2 = e2
    ar = ar2 * ar1 - ai2 * ai1
    ai = ar2 * ai1 + ai2 * ar1
    br = ar2 * br1 - ai2 * bi1 + br2
    bi = ar2 * bi1 + ai2 * br1 + bi2
    return ar, ai, br, bi

def s5_mix(u, a_re, a_im, log_dt, b_re, b_im, c_re, c_im, d_skip, w_glu, b_glu, gain):
    out_dtype = u.dtype
    u = u.astype(jnp.float32)
    bsz, seq = u.shape[0], u.shape[1]
    G, P = N_S5_GROUPS, S5_STATE
    ug = u.reshape(bsz, seq, G, S5_CH)

    dt = jnp.exp(log_dt)[:, None]
    mag = jnp.exp(dt * a_re)
    abar_re = mag * jnp.cos(dt * a_im)
    abar_im = mag * jnp.sin(dt * a_im)
    den = a_re * a_re + a_im * a_im
    p, q = abar_re - 1.0, abar_im
    coef_re = (p * a_re + q * a_im) / den
    coef_im = (q * a_re - p * a_im) / den
    bbar_re = coef_re[..., None] * b_re - coef_im[..., None] * b_im
    bbar_im = coef_re[..., None] * b_im + coef_im[..., None] * b_re

    bu_re = jnp.einsum("gpc,btgc->tbgp", bbar_re, ug)
    bu_im = jnp.einsum("gpc,btgc->tbgp", bbar_im, ug)
    a_seq_re = jnp.broadcast_to(abar_re[None, None], (seq, 1, G, P))
    a_seq_im = jnp.broadcast_to(abar_im[None, None], (seq, 1, G, P))
    _, _, s_re, s_im = lax.associative_scan(_ssm_combine, (a_seq_re, a_seq_im, bu_re, bu_im), axis=0)

    y = (jnp.einsum("gcp,tbgp->btgc", c_re, s_re) - jnp.einsum("gcp,tbgp->btgc", c_im, s_im)
         + d_skip * ug).reshape(bsz, seq, D_S5)
    zz = jax.nn.gelu(y)
    out = zz * jax.nn.sigmoid(zz @ w_glu + b_glu)
    return (rms_norm(out) * gain).astype(out_dtype)

def first_inputs(seed: int = 0) -> dict:
    key = jax.random.key(seed)
    ks = jax.random.split(key, 40)
    L = DEPTH
    nrm = lambda k, shape, s: jax.random.normal(k, shape, jnp.float32) * s
    uni = lambda k, shape, lo, hi: jax.random.uniform(k, shape, jnp.float32, lo, hi)
    H, N, G, P = N_RWKV_HEADS, RWKV_HEAD, N_S5_GROUPS, S5_STATE
    return {
        "x": nrm(ks[0], (BATCH, SEQ, D_MODEL), 1.0),
        "c": nrm(ks[1], (BATCH, D_MODEL), 1.0),
        "w_ada": nrm(ks[2], (L, D_MODEL, 6 * D_MODEL), D_MODEL ** -0.5),
        "b_ada": nrm(ks[3], (L, 6 * D_MODEL), 0.01),
        "w_in": nrm(ks[4], (L, D_MODEL, D_IN), D_MODEL ** -0.5),
        "mu_shift": uni(ks[5], (L, D_SHIFT), 0.0, 1.0),
        "rw_w0": uni(ks[6], (L, D_RWKV), -6.0, 1.0),
        "rw_w2": nrm(ks[7], (L, LORA_W, D_RWKV), 0.5 * LORA_W ** -0.5),
        "rw_a0": nrm(ks[8], (L, D_RWKV), 0.1),
        "rw_a2": nrm(ks[9], (L, LORA_A, D_RWKV), 0.5 * LORA_A ** -0.5),
        "rw_g2": nrm(ks[10], (L, LORA_G, D_RWKV), LORA_G ** -0.5),
        "rw_k_k": 0.85 + nrm(ks[11], (L, D_RWKV), 0.05),
        "rw_k_a": 1.0 + nrm(ks[12], (L, D_RWKV), 0.05),
        "rw_r_k": nrm(ks[13], (L, H, N), 0.1),
        "rw_lnx_w": 1.0 + nrm(ks[14], (L, D_RWKV), 0.05),
        "rw_lnx_b": nrm(ks[15], (L, D_RWKV), 0.01),
        "s5_a_re": -0.5 + nrm(ks[16], (L, G, P), 0.01),
        "s5_a_im": math.pi * jnp.arange(P, dtype=jnp.float32)[None, None, :] + nrm(ks[17], (L, G, P), 0.01),
        "s5_log_dt": uni(ks[18], (L, G), math.log(DT_MIN), math.log(DT_MAX)),
        "s5_b_re": nrm(ks[19], (L, G, P, S5_CH), (2 * S5_CH) ** -0.5),
        "s5_b_im": nrm(ks[20], (L, G, P, S5_CH), (2 * S5_CH) ** -0.5),
        "s5_c_re": nrm(ks[21], (L, G, S5_CH, P), (2 * P) ** -0.5),
        "s5_c_im": nrm(ks[22], (L, G, S5_CH, P), (2 * P) ** -0.5),
        "s5_d": nrm(ks[23], (L, G, S5_CH), 1.0),
        "s5_w_glu": nrm(ks[24], (L, D_S5, D_S5), D_S5 ** -0.5),
        "s5_b_glu": nrm(ks[25], (L, D_S5), 0.01),
        "s5_gain": 1.0 + nrm(ks[26], (L, D_S5), 0.05),
        "w_out": nrm(ks[27], (L, D_MIX, D_MODEL), D_MIX ** -0.5),
        "ffn_w_gate": nrm(ks[28], (L, D_MODEL, D_FF), D_MODEL ** -0.5),
        "ffn_w_up": nrm(ks[29], (L, D_MODEL, D_FF), D_MODEL ** -0.5),
        "ffn_w_down": nrm(ks[30], (L, D_FF, D_MODEL), D_FF ** -0.5),
        "final_gain": 1.0 + nrm(ks[31], (D_MODEL,), 0.05),
    }

def first_block(x, c, w_ada, b_ada, w_in, mu_shift, rw_w0, rw_w2, rw_a0, rw_a2, rw_g2,
              rw_k_k, rw_k_a, rw_r_k, rw_lnx_w, rw_lnx_b, s5_a_re, s5_a_im, s5_log_dt,
              s5_b_re, s5_b_im, s5_c_re, s5_c_im, s5_d, s5_w_glu, s5_b_glu, s5_gain,
              w_out, ffn_w_gate, ffn_w_up, ffn_w_down, final_gain):
    c_act = jax.nn.silu(c)
    for l in range(DEPTH):
        ada = c_act @ w_ada[l] + b_ada[l]
        sh_m, sc_m, g_m, sh_f, sc_f, g_f = jnp.split(ada, 6, axis=-1)

        h = modulate(rms_norm(x), sh_m, sc_m)
        proj = h @ w_in[l]
        z = proj[..., :D_SHIFT]
        u = proj[..., D_SHIFT:]
        z_prev = jnp.pad(z[:, :-1], ((0, 0), (1, 0), (0, 0)))
        z = z + mu_shift[l] * (z_prev - z)
        y_rwkv = rwkv7_time_mix(z, rw_w0[l], rw_w2[l], rw_a0[l], rw_a2[l], rw_g2[l],
                                rw_k_k[l], rw_k_a[l], rw_r_k[l], rw_lnx_w[l], rw_lnx_b[l])
        y_s5 = s5_mix(u, s5_a_re[l], s5_a_im[l], s5_log_dt[l], s5_b_re[l], s5_b_im[l],
                      s5_c_re[l], s5_c_im[l], s5_d[l], s5_w_glu[l], s5_b_glu[l], s5_gain[l])
        mix = jnp.concatenate([y_rwkv, y_s5], axis=-1) @ w_out[l]
        x = x + g_m[:, None, :] * mix

        h = modulate(rms_norm(x), sh_f, sc_f)
        ffn = (jax.nn.silu(h @ ffn_w_gate[l]) * (h @ ffn_w_up[l])) @ ffn_w_down[l]
        x = x + g_f[:, None, :] * ffn
    return rms_norm(x) * final_gain


DEPTH_2 = 2

GROUP_WIDTH = D_MODEL // 2
D_MIX_2 = 3 * GROUP_WIDTH
BLOCK = 128
RMS_EPS = 1e-6
NEG_INF = -1e30

MLA_HEADS = 8
MLA_NOPE_DIM = 64
MLA_ROPE_DIM = 32
MLA_QK_DIM = MLA_NOPE_DIM + MLA_ROPE_DIM
MLA_V_DIM = 64
MLA_Q_LORA = 256
MLA_KV_LORA = 128
ROPE_THETA = 10000.0

CONV_DIM = GROUP_WIDTH
CONV_WIDTH = 3

SWA_HEADS = 8
SWA_KV_HEADS = 2
SWA_GROUP = SWA_HEADS // SWA_KV_HEADS
SWA_HEAD_DIM = 64
SWA_WINDOW = 128

IN_SPLITS = (
    MLA_Q_LORA, MLA_KV_LORA, MLA_ROPE_DIM, GROUP_WIDTH,
    CONV_DIM, CONV_DIM, CONV_DIM, GROUP_WIDTH,
    SWA_HEADS * SWA_HEAD_DIM, SWA_KV_HEADS * SWA_HEAD_DIM,
    SWA_KV_HEADS * SWA_HEAD_DIM, GROUP_WIDTH,
)
IN_COLS = sum(IN_SPLITS)


def rms_norm_2(x, g):
    xf = x.astype(jnp.float32)
    y = xf * lax.rsqrt(jnp.mean(xf * xf, axis=-1, keepdims=True) + RMS_EPS)
    return (y * g.astype(jnp.float32)).astype(x.dtype)

def apply_rope(x, pos):
    half = x.shape[-1] // 2
    inv_freq = jnp.power(jnp.float32(ROPE_THETA), -jnp.arange(half, dtype=jnp.float32) / half)
    ang = pos[:, None] * inv_freq[None, :]
    cos = jnp.cos(ang)[:, None, :]
    sin = jnp.sin(ang)[:, None, :]
    xf = x.astype(jnp.float32)
    x1, x2 = xf[..., :half], xf[..., half:]
    out = jnp.concatenate([x1 * cos - x2 * sin, x2 * cos + x1 * sin], axis=-1)
    return out.astype(x.dtype)

def mla_mixer(q_lat, kv_lat, k_rope, q_a_norm, w_qb, kv_a_norm, w_kvb, q_norm, k_norm):
    b, s, _ = q_lat.shape
    q = (rms_norm_2(q_lat, q_a_norm) @ w_qb).reshape(b, s, MLA_HEADS, MLA_QK_DIM)
    kv = (rms_norm_2(kv_lat, kv_a_norm) @ w_kvb).reshape(b, s, MLA_HEADS, MLA_NOPE_DIM + MLA_V_DIM)
    k_nope, v = kv[..., :MLA_NOPE_DIM], kv[..., MLA_NOPE_DIM:]
    k_pe = jnp.broadcast_to(k_rope[:, :, None, :], (b, s, MLA_HEADS, MLA_ROPE_DIM))
    k = jnp.concatenate([k_nope, k_pe], axis=-1)
    q = rms_norm_2(q, q_norm)
    k = rms_norm_2(k, k_norm)
    pos = jnp.arange(s, dtype=jnp.float32)
    q = jnp.concatenate([q[..., :MLA_NOPE_DIM], apply_rope(q[..., MLA_NOPE_DIM:], pos)], axis=-1)
    k = jnp.concatenate([k[..., :MLA_NOPE_DIM], apply_rope(k[..., MLA_NOPE_DIM:], pos)], axis=-1)
    scale = MLA_QK_DIM ** -0.5
    nb = s // BLOCK
    q_blocks = q.reshape(b, nb, BLOCK, MLA_HEADS, MLA_QK_DIM).transpose(1, 0, 2, 3, 4)
    starts = jnp.arange(nb, dtype=jnp.int32) * BLOCK
    key_pos = jnp.arange(s, dtype=jnp.int32)

    def attend_block(args):
        qb, start = args
        sc = jnp.einsum('bqhd,bkhd->bhqk', qb, k, preferred_element_type=jnp.float32) * scale
        q_pos = start + jnp.arange(BLOCK, dtype=jnp.int32)
        causal = key_pos[None, :] <= q_pos[:, None]
        sc = jnp.where(causal[None, None], sc, NEG_INF)
        p = jax.nn.softmax(sc, axis=-1).astype(v.dtype)
        return jnp.einsum('bhqk,bkhd->bqhd', p, v)

    o = lax.map(attend_block, (q_blocks, starts))
    return o.transpose(1, 0, 2, 3, 4).reshape(b, s, MLA_HEADS * MLA_V_DIM)

def short_conv_mixer(h, b_gate, c_gate, conv_w):
    u = c_gate * h
    y = lax.conv_general_dilated(
        u, conv_w[:, None, :].astype(u.dtype), window_strides=(1,),
        padding=[(CONV_WIDTH - 1, 0)], dimension_numbers=('NWC', 'WIO', 'NWC'),
        feature_group_count=CONV_DIM)
    return b_gate * y

def _band(t):
    b, s, kv, d = t.shape
    nb = s // BLOCK
    tp = jnp.concatenate([jnp.zeros((b, BLOCK, kv, d), t.dtype), t], axis=1)
    tp = tp.reshape(b, nb + 1, BLOCK, kv, d)
    return jnp.concatenate([tp[:, :-1], tp[:, 1:]], axis=2)

def swa_mixer(q, k, v, q_norm, k_norm, sinks):
    b, s, _ = q.shape
    nb = s // BLOCK
    q = rms_norm_2(q.reshape(b, s, SWA_HEADS, SWA_HEAD_DIM), q_norm)
    k = rms_norm_2(k.reshape(b, s, SWA_KV_HEADS, SWA_HEAD_DIM), k_norm)
    v = v.reshape(b, s, SWA_KV_HEADS, SWA_HEAD_DIM)
    qb = q.reshape(b, nb, BLOCK, SWA_KV_HEADS, SWA_GROUP, SWA_HEAD_DIM)
    kb, vb = _band(k), _band(v)
    sc = jnp.einsum('bnqkgd,bnskd->bnkgqs', qb, kb,
                    preferred_element_type=jnp.float32) * (SWA_HEAD_DIM ** -0.5)
    q_idx = jnp.arange(BLOCK, dtype=jnp.int32)[:, None]
    k_idx = jnp.arange(2 * BLOCK, dtype=jnp.int32)[None, :]
    dist = BLOCK + q_idx - k_idx
    key_pos = (jnp.arange(nb, dtype=jnp.int32)[:, None] - 1) * BLOCK + k_idx
    valid = ((dist >= 0) & (dist < SWA_WINDOW))[None] & (key_pos >= 0)[:, None, :]
    slopes = jnp.exp2(-8.0 * jnp.arange(1, SWA_HEADS + 1, dtype=jnp.float32) / SWA_HEADS)
    slopes = slopes.reshape(SWA_KV_HEADS, SWA_GROUP)
    sc = sc - slopes[None, None, :, :, None, None] * dist.astype(jnp.float32)[None, None, None, None]
    sc = jnp.where(valid[None, :, None, None], sc, NEG_INF)
    sink = jnp.broadcast_to(
        sinks.astype(jnp.float32).reshape(SWA_KV_HEADS, SWA_GROUP)[None, None, :, :, None, None],
        sc.shape[:-1] + (1,))
    p = jax.nn.softmax(jnp.concatenate([sc, sink], axis=-1), axis=-1)[..., :-1].astype(v.dtype)
    o = jnp.einsum('bnkgqs,bnskd->bnqkgd', p, vb)
    return o.reshape(b, s, SWA_HEADS * SWA_HEAD_DIM)

def hybrid_layer(x, norm_g, w_in, mla_q_a_norm, mla_w_qb, mla_kv_a_norm, mla_w_kvb,
                 mla_q_norm, mla_k_norm, conv_w, swa_q_norm, swa_k_norm, swa_sinks, w_out):
    h = rms_norm_2(x, norm_g)
    proj = h @ w_in
    offsets = [int(o) for o in np.cumsum(IN_SPLITS)[:-1]]
    (q_lat, kv_lat, k_rope, g_mla,
     c_h, c_b, c_c, g_conv,
     s_q, s_k, s_v, g_swa) = jnp.split(proj, offsets, axis=-1)
    y_mla = mla_mixer(q_lat, kv_lat, k_rope, mla_q_a_norm, mla_w_qb, mla_kv_a_norm,
                      mla_w_kvb, mla_q_norm, mla_k_norm) * jax.nn.silu(g_mla)
    y_conv = short_conv_mixer(c_h, c_b, c_c, conv_w) * jax.nn.silu(g_conv)
    y_swa = swa_mixer(s_q, s_k, s_v, swa_q_norm, swa_k_norm, swa_sinks) * jax.nn.silu(g_swa)
    y = jnp.concatenate([y_mla, y_conv, y_swa], axis=-1) @ w_out
    return x + y

def second_inputs(seed: int = 0) -> dict:
    key = jax.random.key(seed)
    ks = jax.random.split(key, 14)
    f32 = jnp.float32

    def nrm(k, shape, scale):
        return jax.random.normal(k, shape, f32) * scale

    def gain(k, n):
        return 1.0 + 0.02 * jax.random.normal(k, (DEPTH_2, n), f32)

    return {
        "x": jax.random.normal(ks[0], (BATCH, SEQ, D_MODEL), f32),
        "norm_g": gain(ks[1], D_MODEL),
        "w_in": nrm(ks[2], (DEPTH_2, D_MODEL, IN_COLS), D_MODEL ** -0.5),
        "mla_q_a_norm": gain(ks[3], MLA_Q_LORA),
        "mla_w_qb": nrm(ks[4], (DEPTH_2, MLA_Q_LORA, MLA_HEADS * MLA_QK_DIM), MLA_Q_LORA ** -0.5),
        "mla_kv_a_norm": gain(ks[5], MLA_KV_LORA),
        "mla_w_kvb": nrm(ks[6], (DEPTH_2, MLA_KV_LORA, MLA_HEADS * (MLA_NOPE_DIM + MLA_V_DIM)), MLA_KV_LORA ** -0.5),
        "mla_q_norm": gain(ks[7], MLA_QK_DIM),
        "mla_k_norm": gain(ks[8], MLA_QK_DIM),
        "conv_w": nrm(ks[9], (DEPTH_2, CONV_WIDTH, CONV_DIM), CONV_WIDTH ** -0.5),
        "swa_q_norm": gain(ks[10], SWA_HEAD_DIM),
        "swa_k_norm": gain(ks[11], SWA_HEAD_DIM),
        "swa_sinks": nrm(ks[12], (DEPTH_2, SWA_HEADS), 0.5),
        "w_out": nrm(ks[13], (DEPTH_2, D_MIX_2, D_MODEL), D_MIX_2 ** -0.5),
    }

def second_block(x, norm_g, w_in, mla_q_a_norm, mla_w_qb, mla_kv_a_norm, mla_w_kvb,
              mla_q_norm, mla_k_norm, conv_w, swa_q_norm, swa_k_norm, swa_sinks, w_out):
    for l in range(DEPTH_2):
        x = hybrid_layer(x, norm_g[l], w_in[l], mla_q_a_norm[l], mla_w_qb[l], mla_kv_a_norm[l],
                         mla_w_kvb[l], mla_q_norm[l], mla_k_norm[l], conv_w[l], swa_q_norm[l],
                         swa_k_norm[l], swa_sinks[l], w_out[l])
    return x


def setup_inputs(seed=0):
    out = dict(first_inputs(seed))
    for name, value in second_inputs(seed + 1).items():
        if name != "x":
            out[name + "_2"] = value
    return out


def reference(
    x, c, w_ada, b_ada, w_in, mu_shift, rw_w0, rw_w2, rw_a0, rw_a2, rw_g2, rw_k_k, rw_k_a,
    rw_r_k, rw_lnx_w, rw_lnx_b, s5_a_re, s5_a_im, s5_log_dt, s5_b_re, s5_b_im, s5_c_re, s5_c_im,
    s5_d, s5_w_glu, s5_b_glu, s5_gain, w_out, ffn_w_gate, ffn_w_up, ffn_w_down, final_gain,
    norm_g_2, w_in_2, mla_q_a_norm_2, mla_w_qb_2, mla_kv_a_norm_2, mla_w_kvb_2, mla_q_norm_2,
    mla_k_norm_2, conv_w_2, swa_q_norm_2, swa_k_norm_2, swa_sinks_2, w_out_2,
):
    x = first_block(
        x, c, w_ada, b_ada, w_in, mu_shift, rw_w0, rw_w2, rw_a0, rw_a2, rw_g2, rw_k_k, rw_k_a,
        rw_r_k, rw_lnx_w, rw_lnx_b, s5_a_re, s5_a_im, s5_log_dt, s5_b_re, s5_b_im, s5_c_re,
        s5_c_im, s5_d, s5_w_glu, s5_b_glu, s5_gain, w_out, ffn_w_gate, ffn_w_up, ffn_w_down,
        final_gain,
    )
    return second_block(
        x, norm_g_2, w_in_2, mla_q_a_norm_2, mla_w_qb_2, mla_kv_a_norm_2, mla_w_kvb_2,
        mla_q_norm_2, mla_k_norm_2, conv_w_2, swa_q_norm_2, swa_k_norm_2, swa_sinks_2, w_out_2,
    )


_drawn_inputs = setup_inputs


def setup_inputs(seed=0):
    import zlib

    import numpy as np

    out = dict(_drawn_inputs(seed))
    spreads = {}
    factors = {'b_ada': 2.753,
     'rw_a0': 4.243,
     'rw_lnx_w': 3.896,
     'rw_lnx_b': 8.0,
     's5_a_re': 8.0,
     's5_b_glu': 8.0,
     'norm_g_2': 2.782,
     'mla_q_a_norm_2': 8.0,
     'mla_kv_a_norm_2': 8.0,
     'mla_q_norm_2': 8.0,
     'mla_k_norm_2': 8.0,
     'swa_q_norm_2': 8.0,
     'swa_k_norm_2': 8.0,
     'swa_sinks_2': 4.698}
    for name, (base, spread) in spreads.items():
        noise = np.random.default_rng([zlib.crc32(name.encode()), seed]).standard_normal(out[name].shape)
        drawn = base * np.exp(spread * noise) if base else spread * noise
        out[name] = __import__('jax').numpy.asarray(drawn.astype(out[name].dtype))
    for name, factor in factors.items():
        out[name] = (out[name] * factor).astype(out[name].dtype)
    return out
```

```python
import math

import numpy as np
import concourse.bass as bass
from concourse import mybir
from contextlib import ExitStack

F32 = mybir.dt.float32
ALU = mybir.AluOpType
ACT = mybir.ActivationFunctionType
AX = mybir.AxisListType

T = 512
NT = 8
DFF_T = 22
RING = 8
UNITS = 234


class Tok:
    __slots__ = ("queue", "signals", "value")

    def __init__(self, queue):
        self.queue, self.signals, self.value = queue, False, None


class Queue:

    def __init__(self, name):
        self.name, self.items, self.sem, self.last = name, [], None, None

    def do(self, fn, *after):
        tok = Tok(self)
        waits = []
        for a in flat(after):
            a.signals = True
            waits.append(a)
        self.items.append((fn, waits, tok))
        self.last = tok
        return tok


class DmaTok(Tok):
    __slots__ = ("dsem",)


def flat(x):
    if x is None:
        return []
    if isinstance(x, Tok):
        return [x]
    out = []
    for y in x:
        out += flat(y)
    return out


class DmaSem:

    def __init__(self, prog, name):
        self.name, self.count, self.sem = name, 0, None
        prog.dsems.append(self)


class Prog:
    def __init__(self):
        self.pe, self.act, self.dve, self.pool, self.sp = (Queue(n) for n in ("pe", "act", "dve", "pool", "sp"))
        self.dsems = []

    def dsem(self, name):
        return DmaSem(self, name)

    def dma(self, queue, out, in_, dsem, *after):
        tok = DmaTok(queue)
        dsem.count += 16
        tok.dsem, tok.value = dsem, dsem.count
        waits = []
        for a in flat(after):
            a.signals = True
            waits.append(a)
        queue.items.append((lambda e: e.dma_start(out, in_), waits, tok))
        return tok

    def number(self):
        for q in (self.pe, self.act, self.dve, self.pool, self.sp):
            n = 0
            for _, _, tok in q.items:
                if not isinstance(tok, DmaTok) and tok.signals:
                    n += 1
                    tok.value = n

    def issue(self, q, eng):
        seen = {}
        for fn, waits, tok in q.items:
            for w in waits:
                sem = w.dsem.sem if isinstance(w, DmaTok) else w.queue.sem
                name = w.dsem.name if isinstance(w, DmaTok) else w.queue.name
                if seen.get(name, 0) < w.value:
                    eng.wait_ge(sem, w.value)
                    seen[name] = w.value
            ins = fn(eng)
            if isinstance(tok, DmaTok):
                ins.then_inc(tok.dsem.sem, 16)
            elif tok.signals:
                ins.then_inc(q.sem, 1)


class Banks:

    def __init__(self, aps):
        self.aps = aps
        self.free = [(i, []) for i in range(len(aps))]

    def take(self):
        i, toks = self.free.pop(0)
        return i, self.aps[i], toks

    def give(self, i, *toks):
        self.free.append((i, flat(toks)))


PCOLS = {}


def _pcols():
    at = 0
    for name, n in [("b_ada", 48), ("mu", 14), ("w0", 4), ("a0", 4), ("k_k", 4), ("k_a", 4), ("r_k", 4),
                    ("lnw", 4), ("lnb", 4), ("s5d", 4), ("bglu", 4), ("gain", 4), ("fgain", 8), ("c", 8),
                    ("are", 16), ("aim", 16), ("ldt", 16),
                    ("ng0", 8), ("ng1", 8), ("qan0", 2), ("qan1", 2), ("kvan0", 1), ("kvan1", 1),
                    ("qn0", 1), ("qn1", 1), ("kn0", 1), ("kn1", 1), ("cw0", 12), ("cw1", 12),
                    ("sqn0", 1), ("sqn1", 1), ("skn0", 1), ("skn1", 1), ("sink0", 8), ("sink1", 8)]:
        PCOLS[name] = (at, n)
        at += n
    return at


NPC = _pcols()
CC = {}


def _ccols():
    at = 0
    for name, n in [("ident", 128), ("ones", 128), ("blk", 128), ("caus", 128), ("scan", 512),
                    ("I64", 64), ("m2L", 64), ("m2U", 64), ("mSU", 64), ("mIU", 64), ("lvl", 320), ("k", 8)]:
        CC[name] = (at, n)
        at += n
    return at


NCC = _ccols()
C2 = {"alibi": (0, 2048), "ropec": (2048, 512), "ropes": (2560, 512), "rot": (3072, 32)}
NC2 = 3104
EPS6, EPSLN, TENLN2, C1E24, HPI = range(5)


def constants():
    c = np.zeros((128, NCC), np.float32)

    def put(name, a):
        s, n = CC[name]
        c[:, s:s + n] = a
    i = np.arange(128)
    put("ident", np.eye(128))
    put("ones", 1.0)
    put("blk", (i[:, None] // 64) == (i[None, :] // 64))
    put("caus", np.where(i[None, :] > i[:, None], -1e30, 0.0))
    put("scan", (np.arange(512) % 64 != 0)[None, :].astype(np.float32))
    a, b = (i % 64)[:, None], np.arange(64)[None, :]
    put("I64", a == b)
    put("m2L", (a // 2 == b // 2) & (a > b))
    put("m2U", (a // 2 == b // 2) & (a < b))
    put("mSU", a < b)
    put("mIU", a <= b)
    lv = [((a // (2 * m)) == (b // (2 * m))) & ((a // m) < (b // m)) for m in (2, 4, 8, 16, 32)]
    put("lvl", np.concatenate(lv, 1))
    put("k", np.array([1e-6, 64e-5, 10 * math.log(2), 1e-24 * 2 ** 20, math.pi / 2, 0, 0, 0])[None, :])
    d = np.zeros((128, NC2), np.float32)
    q, k = i[:, None], np.arange(256)[None, :]
    dist = 128 + q - k
    ok = (dist >= 0) & (dist < 128)
    al = []
    for h in (0, 4, 1, 5, 2, 6, 3, 7):
        slope = np.float32(2.0 ** (-(h + 1)))
        al.append(np.where(ok, -slope * dist.astype(np.float32), np.float32(-1e30)))
    d[:, 0:2048] = np.concatenate(al, 1)
    half = 16
    inv = np.power(np.float32(10000.0), -np.arange(half, dtype=np.float32) / half).astype(np.float32)
    ang = (np.arange(512, dtype=np.float32)[:, None] * inv[None, :]).astype(np.float32)
    cos, sin = np.cos(ang).T, np.sin(ang).T
    rc = np.ones((128, 512), np.float32)
    rs = np.zeros((128, 512), np.float32)
    rc[64:80], rc[80:96] = cos, cos
    rs[64:80], rs[80:96] = sin, sin
    d[:, 2048:2560], d[:, 2560:3072] = rc, rs
    rot = np.zeros((32, 32), np.float32)
    for j in range(16):
        rot[j + 16, j] = -1.0
        rot[j, j + 16] = 1.0
    d[64:96, 3072:3104] = rot
    return c, d


class Kern:
    def __init__(self, nc, d, out, dumps=None):
        self.nc, self.d, self.out, self.dumps = nc, d, out, dumps or {}
        self.P = Prog()
        self.order = []

    def tt(self, q, out, a, b, op, *after):
        if q is self.P.pool:
            after += (q.last,)
        return q.do(lambda e: e.tensor_tensor(out=out, in0=a, in1=b, op=op), *after)

    def ts(self, q, out, a, s1, op0, s2, op1, *after):
        if q is self.P.pool:
            after += (q.last,)
        if s2 is None:
            return q.do(lambda e: e.tensor_scalar(out=out, in0=a, scalar1=s1, scalar2=None, op0=op0), *after)
        return q.do(lambda e: e.tensor_scalar(out=out, in0=a, scalar1=s1, scalar2=s2, op0=op0, op1=op1), *after)

    def stt(self, out, a, s, b, op0, op1, *after):
        return self.P.dve.do(lambda e: e.scalar_tensor_tensor(out=out, in0=a, scalar=s, in1=b, op0=op0, op1=op1), *after)

    def af(self, out, a, f, *after, bias=None, scale=1.0, acc=None):
        def fn(e):
            kw = {}
            if bias is not None:
                kw["bias"] = bias
            if acc is not None:
                kw["accum_out"] = acc
            return e.activation(out, a, f, scale=scale, **kw)
        return self.P.act.do(fn, *after)

    def cp(self, q, out, a, *after):
        if q is self.P.act:
            return q.do(lambda e: e.activation(out, a, ACT.Copy), *after)
        return q.do(lambda e: e.tensor_copy(out, a), *after)

    def mm(self, out, lhsT, rhs, start, stop, *after):
        return self.P.pe.do(lambda e: e.matmul(out, lhsT, rhs, start=start, stop=stop, skip_group_check=True), *after)

    def tr(self, out, in_, *after):
        idn = self.C("ident")
        return self.P.pe.do(lambda e: e.transpose(out, in_, idn), *after)

    def C(self, name):
        s, n = CC[name]
        return self.cst[:, s:s + n]

    def kc(self, i):
        s, _ = CC["k"]
        return self.cst[:, s + i:s + i + 1]

    def pc(self, name, i=0, n=1):
        s, _ = PCOLS[name]
        return self.par[:, s + i:s + i + n]

    def wblock(self, key):
        b = len(self.order)
        self.order.append(key)
        u, j = divmod(b, 8)
        if j == 0:
            self.wtok = self.wdma[u]
        slot = u % RING
        return self.ring[:, slot * 1024 + j * 128:slot * 1024 + (j + 1) * 128], self.wtok

    def wused(self, tok):
        b = len(self.order)
        if b % 8 == 0:
            u = b // 8 - 1 + RING
            if u < self.units:
                self.load_unit(u, tok)

    def load_unit(self, u, *after):
        slot = u % RING
        self.wdma[u] = self.P.dma(self.P.sp, self.ring[:, slot * 1024:(slot + 1) * 1024],
                                  self.d["ws"][u, :, :], self.wsem[slot], *after)

    def dense(self, keys, rhs, out, M=128, *after, start=True, stop=True):
        n = len(keys)
        for i, (key, r) in enumerate(zip(keys, rhs)):
            w, wt = self.wblock(key)
            t = self.mm(out, w[:, 0:M], r, start and i == 0, stop and i == n - 1, wt, *(after if i == 0 else ()))
            self.wused(t)
        return t

    def dump(self, name, ap, *after):
        if name in self.dumps:
            s = self.P.dsem("dump_" + name)
            t = self.P.dma(self.P.sp, self.dumps[name], ap, s, *after)
            self.final.append(t)

    def rsqrt(self, out, src, eps, scale, *after, bias=None):
        t = self.af(out, src, ACT.Ln, *after, bias=eps, scale=scale)
        return self.af(out, out, ACT.Exp, t, scale=-0.5, bias=bias)

    def build(self, stop=None):
        nc, P = self.nc, self.P
        self.final = []
        ctx = ExitStack()
        with ctx:
            self.cst = ctx.enter_context(nc.sbuf_tensor("cst", [128, NCC], F32))
            self.par = ctx.enter_context(nc.sbuf_tensor("par", [128, NPC], F32))
            self.X = ctx.enter_context(nc.sbuf_tensor("X", [128, NT, T], F32))
            self.H = ctx.enter_context(nc.sbuf_tensor("H", [128, NT, T], F32))
            self.ring = ctx.enter_context(nc.sbuf_tensor("ring", [128, RING * 1024], F32))
            self.ada = ctx.enter_context(nc.sbuf_tensor("ada", [128, 48], F32))
            self.AF = (nc.sbuf_bytes_remaining - 64) // 4
            self.ar = ctx.enter_context(nc.sbuf_tensor("arena", [128, self.AF], F32))
            banks = [ctx.enter_context(nc.psum_tensor(f"b{i}", [128, 512], F32)) for i in range(8)]
            self.banks = Banks(banks)
            self.units = self.d["ws"].shape[0]
            self.wsem = [P.dsem(f"w{i}") for i in range(RING)]
            self.wdma = {}
            self.body(stop)
            assert stop or len(self.order) == 8 * self.units, (len(self.order), self.units)
            P.number()
            for q in (P.pe, P.act, P.dve, P.pool, P.sp):
                q.sem = ctx.enter_context(nc.semaphore("s_" + q.name))
            for s in P.dsems:
                s.sem = ctx.enter_context(nc.semaphore("d_" + s.name))
            block = ctx.enter_context(nc.Block())

            @block.sync
            def _(e):
                P.issue(P.sp, e)
                for s in P.dsems:
                    if s.count:
                        e.wait_ge(s.sem, s.count)

            @block.gpsimd
            def _(e):
                P.issue(P.pool, e)

            @block.scalar
            def _(e):
                P.issue(P.act, e)

            @block.vector
            def _(e):
                P.issue(P.dve, e)

            @block.tensor
            def _(e):
                P.issue(P.pe, e)
        return self.order

    def region(self, kb, *shape):
        n = int(np.prod(shape))
        s = int(kb * 256)
        assert s + n <= self.AF, (kb, shape, self.AF)
        a = self.ar[:, s:s + n]
        if len(shape) == 1:
            return a
        names = "abcdef"[:len(shape)]
        return a.rearrange(f"p ({' '.join(names)}) -> p {' '.join(names)}", **{x: y for x, y in zip(names[1:], shape[1:])})

    def run(self, *gens):
        gens = [[g, w, 0] for g, w in gens]
        while gens:
            for x in list(gens):
                for _ in range(x[1]):
                    try:
                        next(x[0])
                    except StopIteration:
                        gens.remove(x)
                        break

    def body(self, stop):
        P = self.P
        sp = P.sp
        s0 = P.dsem("in0")
        t_par = P.dma(sp, self.par[:, :], self.d["par"], s0)
        t_cst = P.dma(sp, self.cst[:, :], self.d["cst"], s0)
        self.t_in = t_cst
        s1 = P.dsem("in1")
        self.t_x = P.dma(sp, self.X[:, :, :], self.d["xT"], s1)
        for u in range(RING):
            self.load_unit(u)
        self.block1(stop)
        if stop and stop.startswith("b1"):
            return
        self.layers(stop)

    def ada_tiles(self, a, b):
        i, ps, fr = self.banks.take()
        for n in range(a, b):
            rhs = [self.cact[:, k:k + 1] for k in range(8)]
            t = self.dense([("ada", n, k) for k in range(8)], rhs, ps[:, n - a:n - a + 1], 128, self.t_cact, fr)
            fr = ()
            yield
        t = self.tt(self.P.dve, self.ada[:, a:b], ps[:, 0:b - a], self.pc("b_ada", a, b - a), ALU.add, t)
        self.banks.give(i, t)
        self.t_ada = t

    def norm_mod(self, src, dst, t_src, gain, shift=None, feats=1024, tmp=None, tmp_free=()):
        P = self.P
        n = len(src)
        i, ps, fr = self.banks.take()
        mms = []
        for k in range(n):
            sq = tmp[:, k % 2, :]
            w = mms[k - 2] if k >= 2 else tmp_free
            if k % 2:
                t = self.af(sq, src[k], ACT.Square, t_src[k], w)
            else:
                t = self.tt(P.pool, sq, src[k], src[k], ALU.mult, t_src[k], w)
            mms.append(self.mm(ps[:, :], self.C("ones"), sq, k == 0, k == n - 1, t, fr if k == 0 else ()))
        r = tmp[:, 2, :]
        t = self.rsqrt(r, ps[:, :], self.kc(EPS6), 1.0 / feats, mms[-1], tmp_free)
        self.banks.give(i, t)
        outs = []
        for k in range(n):
            if shift is None:
                outs.append(self.stt(dst[k], src[k], gain[k], r, ALU.mult, ALU.mult, t))
            else:
                u = self.stt(dst[k], src[k], gain[k], r, ALU.mult, ALU.mult, t)
                outs.append(self.af(dst[k], dst[k], ACT.Identity, u, bias=shift[k]))
        return outs

    def block1(self, stop):
        P = self.P
        dve, act, pool, sp = P.dve, P.act, P.pool, P.sp
        R = self.region
        self.cact = R(140, 8)
        self.small = R(136, 2, 512)
        s = P.dsem("small")
        self.t_small = P.dma(sp, self.small, self.d["small"], s)
        t = self.af(self.cact, self.pc("c", 0, 8), ACT.Silu, self.t_in)
        self.t_cact = t
        s = P.dsem("s5w")
        self.s5p = R(124, 4, 256)
        self.t_s5p = P.dma(sp, self.s5p, self.d["s5p"], s)
        self.run((self.ada_tiles(0, 16), 1), (self.s5_tables(), 3))
        t_ada = self.t_ada
        one_sc = R(140.5, 8)
        t1 = self.ts(dve, one_sc, self.ada[:, 8:16], 1.0, ALU.add, None, None, t_ada)
        X = [self.X[:, k, :] for k in range(8)]
        Hs = [self.H[:, k, :] for k in range(8)]
        t_h = self.norm_mod(X, Hs, [self.t_x] * 8, [one_sc[:, k:k + 1] for k in range(8)],
                            [self.ada[:, k:k + 1] for k in range(8)], tmp=R(126, 3, 512),
                            tmp_free=[t1, self.t_tab])
        self.dump("h", self.H[:, :, :], t_h)
        if stop == "b1h":
            return
        U = R(110, 4, 8, 64)
        self.U = U
        self.t_u = []
        for n in range(4):
            i, ps, fr = self.banks.take()
            t = self.dense([("in", 14 + n, k) for k in range(8)], Hs, ps[:, :], 128, t_h, self.t_tab, fr)
            t = self.cp(dve, U[:, n, :, :], ps[:, :].rearrange("p (j t) -> p t j", t=8), t)
            self.banks.give(i, t)
            self.t_u.append(t)
        self.dump("u", R(110, 2048), self.t_u)
        self.run((self.in_proj(Hs), 1), (self.s5_apply(), 4))
        self.dump("zs", R(0, 14 * 512), self.t_z)
        self.dump("ys5", R(28, 2048), self.t_os)
        if stop == "b1s5":
            return
        self.run((self.rwkv(stop), 6), (self.ada_tiles(16, 48), 1))
        self.dump("yr", self.region(0, 2048), self.t_yr)
        if stop == "b1rw":
            return
        YR, OS = R(0, 4, 512), R(28, 4, 512)
        ys = [YR[:, k, :] for k in range(4)] + [OS[:, k, :] for k in range(4)]
        t_x1 = []
        for n in range(8):
            i, ps, fr = self.banks.take()
            t = self.dense([("out", n, k) for k in range(8)], ys, ps[:, :], 128, self.t_yr, self.t_os, fr)
            t = self.stt(X[n], ps[:, :], self.ada[:, 16 + n:17 + n], X[n], ALU.mult, ALU.add, t, self.t_ada, self.t_x)
            self.banks.give(i, t)
            t_x1.append(t)
        self.dump("x1", self.X[:, :, :], t_x1)
        if stop == "b1x":
            return
        self.load_layer_tables(t_x1)
        one_sc = R(100, 8)
        t1 = self.ts(dve, one_sc, self.ada[:, 32:40], 1.0, ALU.add, None, None, self.t_ada, t_x1)
        t_h = self.norm_mod(X, Hs, t_x1, [one_sc[:, k:k + 1] for k in range(8)],
                            [self.ada[:, 24 + k:25 + k] for k in range(8)], tmp=R(102, 3, 512), tmp_free=[t1])
        G = R(40, DFF_T, 512)
        SB = R(84, 2, 512)
        t_g, sil = [], {}
        for n in range(DFF_T):
            i, ps, fr = self.banks.take()
            t = self.dense([("gate", n, k) for k in range(8)], Hs, ps[:, :], 128, t_h, fr)
            ta = self.af(SB[:, n % 2, :], ps[:, :], ACT.Silu, t, t_g[n - 2] if n >= 2 else t_x1)
            self.banks.give(i, ta)
            i, ps, fr = self.banks.take()
            t = self.dense([("up", n, k) for k in range(8)], Hs, ps[:, :], 128, fr)
            t = self.tt(dve, G[:, n, :], ps[:, :], SB[:, n % 2, :], ALU.mult, t, ta)
            self.banks.give(i, t)
            t_g.append(t)
        t_x2 = []
        for n in range(8):
            i, ps, fr = self.banks.take()
            t = self.dense([("down", n, k) for k in range(DFF_T)], [G[:, k, :] for k in range(DFF_T)],
                           ps[:, :], 128, t_g, fr)
            t = self.stt(X[n], ps[:, :], self.ada[:, 40 + n:41 + n], X[n], ALU.mult, ALU.add, t)
            self.banks.give(i, t)
            t_x2.append(t)
        self.t_ff = t_x2[-1]
        self.t_X = self.norm_mod(X, X, t_x2, [self.pc("fgain", k) for k in range(8)], tmp=R(102, 3, 512))
        self.dump("x2", self.X[:, :, :], self.t_X)

    def s5_tables(self):
        P = self.P
        dve, act, pool, sp = P.dve, P.act, P.pool, P.sp
        R = self.region
        V = lambda out, a, b, op, *w: self.tt(dve, out, a, b, op, *w)
        S = lambda out, a, s1, o1, s2, o2, *w: self.ts(dve, out, a, s1, o1, s2, o2, *w)
        sm = R(141, 24, 16)
        dt, xr, mag, xi, kf, r, sn, cs, den, pr_, cr, ci, t1, t2, t3, t4, cc, sg = (sm[:, i, :] for i in range(18))
        PR, PI = R(28, 16, 9), R(29, 16, 9)
        are, aim, ldt = self.pc("are", 0, 16), self.pc("aim", 0, 16), self.pc("ldt", 0, 16)
        a = self.af(dt, ldt, ACT.Exp, self.t_in)
        a = V(xr, dt, are, ALU.mult, a)
        b = V(xi, dt, aim, ALU.mult)
        a = self.af(mag, xr, ACT.Exp, a)
        M = 12582912.0
        b = S(kf, xi, 1.0 / (2 * math.pi), ALU.mult, M, ALU.add, b)
        b = S(kf, kf, -M, ALU.add, None, None, b)
        c1 = 6.28125
        c2 = float(np.float32(np.round((2 * math.pi - c1) * 2 ** 22) / 2 ** 22))
        c3 = float(np.float32(2 * math.pi - c1 - c2))
        b = self.stt(r, kf, -c1, xi, ALU.mult, ALU.add, b)
        b = self.stt(r, kf, -c2, r, ALU.mult, ALU.add, b)
        b = self.stt(r, kf, -c3, r, ALU.mult, ALU.add, b)
        PIF = 3.14159250
        c = S(cc, r, math.pi / 2, ALU.add, None, None, b)
        d_ = S(t1, cc, math.pi, ALU.is_gt, -2 * math.pi, ALU.mult, c)
        c = V(cc, cc, t1, ALU.add, d_)
        c = S(cc, cc, PIF, ALU.min, -PIF, ALU.max, c)
        b = S(r, r, PIF, ALU.min, -PIF, ALU.max, b)
        yield
        b = self.af(sn, r, ACT.Sin, b)
        c = self.af(cs, cc, ACT.Sin, c)
        c = V(PR[:, :, 1], mag, cs, ALU.mult, c, a)
        b = V(PI[:, :, 1], mag, sn, ALU.mult, b)
        b = dve.do(lambda e: e.memset(PR[:, :, 0], 1.0))
        b = dve.do(lambda e: e.memset(PI[:, :, 0], 0.0))
        yield
        t = V(t1, are, are, ALU.mult)
        u = V(t2, aim, aim, ALU.mult)
        t = V(den, t1, t2, ALU.add, t, u)
        t = dve.do(lambda e: e.reciprocal(den, den), t)
        w = S(pr_, PR[:, :, 1], -1.0, ALU.add, None, None, c)
        x1 = V(t1, pr_, are, ALU.mult, w)
        x2 = V(t2, PI[:, :, 1], aim, ALU.mult, b)
        x3 = V(t3, PI[:, :, 1], are, ALU.mult)
        x4 = V(t4, pr_, aim, ALU.mult)
        x1 = V(t1, t1, t2, ALU.add, x1, x2)
        x3 = V(t3, t3, t4, ALU.subtract, x3, x4)
        x1 = V(cr, t1, den, ALU.mult, x1, t)
        x3 = V(ci, t3, den, ALU.mult, x3)
        yield
        def bc(ap, n):
            return ap.unsqueeze(2).broadcast_to((128, 16, n))

        q1, q2 = sm[:, 20, :], sm[:, 21, :]
        tm = R(30, 4, 16, 4)
        last = x3
        for lo, n in ((1, 1), (2, 2), (4, 4)):
            ar_, ai_ = bc(PR[:, :, lo], n), bc(PI[:, :, lo], n)
            br_, bi_ = PR[:, :, 1:1 + n], PI[:, :, 1:1 + n]
            y = [V(tm[:, i, :, 0:n], p, q_, ALU.mult, last)
                 for i, (p, q_) in enumerate(((br_, ar_), (bi_, ai_), (br_, ai_), (bi_, ar_)))]
            y1 = V(PR[:, :, lo + 1:lo + 1 + n], tm[:, 0, :, 0:n], tm[:, 1, :, 0:n], ALU.subtract, y)
            last = V(PI[:, :, lo + 1:lo + 1 + n], tm[:, 2, :, 0:n], tm[:, 3, :, 0:n], ALU.add, y1)
            yield
        P8R, P8I = R(33.5, 8, 16), R(34, 8, 16)
        self.P8R, self.P8I = P8R, P8I
        t = self.cp(dve, P8R[:, 0, :], PR[:, :, 8], last)
        t = self.cp(dve, P8I[:, 0, :], PI[:, :, 8], t)
        tm2 = R(31, 4, 4, 16)
        for lo, n in ((1, 1), (2, 2), (4, 4)):
            def bb(ap):
                return ap.unsqueeze(1).broadcast_to((128, n, 16))
            ar_, ai_ = bb(P8R[:, lo - 1, :]), bb(P8I[:, lo - 1, :])
            br_, bi_ = P8R[:, 0:n, :], P8I[:, 0:n, :]
            y = [V(tm2[:, i, 0:n, :], p, q_, ALU.mult, t)
                 for i, (p, q_) in enumerate(((br_, ar_), (bi_, ai_), (br_, ai_), (bi_, ar_)))]
            y1 = V(P8R[:, lo:lo + n, :], tm2[:, 0, 0:n, :], tm2[:, 1, 0:n, :], ALU.subtract, y)
            t = V(P8I[:, lo:lo + n, :], tm2[:, 2, 0:n, :], tm2[:, 3, 0:n, :], ALU.add, y1)
            yield
        t_p8 = t
        BB = R(16, 2, 16, 16)
        self.BB = BB
        bt = R(18, 2, 16, 16)
        bre, bim, cre, cim = (self.s5p[:, i, :].rearrange("p (g c) -> p g c", g=16) for i in range(4))
        crb, cib = bc(cr, 16), bc(ci, 16)
        y1 = V(bt[:, 0], crb, bre, ALU.mult, x1, x3, self.t_s5p)
        y2 = V(bt[:, 1], cib, bim, ALU.mult)
        y = V(BB[:, 0], bt[:, 0], bt[:, 1], ALU.subtract, y1, y2)
        y1 = V(bt[:, 0], crb, bim, ALU.mult, y)
        y2 = V(bt[:, 1], cib, bre, ALU.mult)
        t_bb = V(BB[:, 1], bt[:, 0], bt[:, 1], ALU.add, y1, y2)
        yield
        W = R(76, 2, 16, 9, 16)
        self.W = W
        wt = R(36, 2, 16, 9, 16)

        def b4(ap, n):
            return ap.unsqueeze(3).broadcast_to((128, 16, n, 16))

        def c4(ap, n):
            return ap.unsqueeze(2).broadcast_to((128, 16, n, 16))
        VT = R(0, 2, 16, 8, 16)
        vt = R(62, 16, 8, 16)
        t = None
        tws = []
        for ri in range(2):
            (pa, ca), (pb_, cb) = (((PR, cre), (PI, cim)) if ri == 0 else ((PI, cre), (PR, cim)))
            for g in range(0, 16, 4):
                gs = slice(g, g + 4)
                w1 = V(wt[:, 0, gs], pa[:, gs].unsqueeze(3).broadcast_to((128, 4, 9, 16)),
                       ca[:, gs].unsqueeze(2).broadcast_to((128, 4, 9, 16)), ALU.mult, last, t)
                w2 = V(wt[:, 1, gs], pb_[:, gs].unsqueeze(3).broadcast_to((128, 4, 9, 16)),
                       cb[:, gs].unsqueeze(2).broadcast_to((128, 4, 9, 16)), ALU.mult, t)
                if ri == 0:
                    t = V(W[:, 0, gs], wt[:, 0, gs], wt[:, 1, gs], ALU.subtract, w1, w2)
                else:
                    t = self.stt(W[:, 1, gs].rearrange("p g d c -> p (g d c)"),
                                 wt[:, 0, gs].rearrange("p g d c -> p (g d c)"), -1.0,
                                 wt[:, 1, gs].rearrange("p g d c -> p (g d c)"), ALU.mult, ALU.subtract, w1, w2)
                tws.append(t)
                yield
        self.t_w = tws
        tv = {}
        t = t_bb
        for ri in range(2):
            br_, bi_ = BB[:, 0], BB[:, 1]
            (pa, ca), (pb_, cb) = (((PR, br_), (PI, bi_)) if ri == 0 else ((PR, bi_), (PI, br_)))
            for g in range(0, 16, 4):
                gs = slice(g, g + 4)
                w1 = V(VT[:, ri, gs], pa[:, gs, 0:8].unsqueeze(3).broadcast_to((128, 4, 8, 16)),
                       ca[:, gs].unsqueeze(2).broadcast_to((128, 4, 8, 16)), ALU.mult, t)
                w2 = V(vt[:, gs], pb_[:, gs, 0:8].unsqueeze(3).broadcast_to((128, 4, 8, 16)),
                       cb[:, gs].unsqueeze(2).broadcast_to((128, 4, 8, 16)), ALU.mult, t)
                t = V(VT[:, ri, gs], VT[:, ri, gs], vt[:, gs], ALU.subtract if ri == 0 else ALU.add, w1, w2)
                tv[ri, g] = t
                yield
        KS = R(94, 32, 240)
        t_z = pool.do(lambda e: e.memset(KS[0:16, :, 0:112], 0.0))
        t_ks = []
        for g4 in range(8):
            i, ps, fr = self.banks.take()
            for gp in range(4 * (g4 // 2), 4 * (g4 // 2) + 4):
                par = 64 * (g4 % 2)
                o = ps[0:16, (gp % 4) * 128:(gp % 4) * 128 + 128]
                for ri in range(2):
                    t = self.mm(o, BB[par:par + 64, ri, gp, :],
                                W[par:par + 64, ri, gp, 0:8, :].rearrange("p d c -> p (d c)"),
                                ri == 0, ri == 1, t_bb, tws, fr)
            g0 = 8 * (g4 // 2) + g4 % 2
            t = self.cp(act, KS[0:16, g0:g0 + 7:2, 112:240], ps[0:16, :].rearrange("p (g d) -> p g d", g=4), t)
            self.banks.give(i, t)
            t_ks.append(t)
            yield
        kd = self.d["kpad"]
        sk = P.dsem("kpad")
        t = P.dma(sp, kd.rearrange("g c n -> c g n"), KS[0:16, :, :], sk, t_ks, t_z)
        TT = R(44, 32, 128)
        self.TT = TT
        st = P.dsem("tt")
        for dl in range(8):
            t_tt = P.dma(sp, TT[16 * dl:16 * dl + 16, :, :],
                         kd[:, :, 16 * dl:16 * dl + 128].rearrange("g c n -> c g n"), st, t, tws[-1], tv[1, 12])
        self.t_tt = t_tt
        VM = R(60, 16, 2, 128)
        self.VM = VM
        t_vm = []
        for g in range(0, 16, 2):
            i, ps, fr = self.banks.take()
            for gg in (g, g + 1):
                for ri in range(2):
                    o = ((gg - g) * 2 + ri) * 128
                    t = self.tr(ps[:, o:o + 128], VT[:, ri, gg].rearrange("p d c -> p (d c)"), tv[1, 12], fr)
            t = self.cp(act if g % 4 else dve, VM[:, g:g + 2].rearrange("p a b c -> p (a b c)"), ps[:, :], t)
            self.banks.give(i, t)
            t_vm.append(t)
            yield
        self.t_vm = t_vm
        self.t_tab = [t_vm, t_p8, t_tt, t_ks]
        self.t_tab_mm = t_vm[-1]

    def in_proj(self, Hs):
        P = self.P
        ZB = self.region(0, 14, 512)
        self.ZB = ZB
        TMP = self.region(126, 2, 516)
        omm = self.region(141, 14)
        t_o = self.ts(P.dve, omm, self.pc("mu", 0, 14), -1.0, ALU.mult, 1.0, ALU.add, self.t_tab, self.t_u)
        z = [P.pool.do(lambda e, j=j: e.memset(TMP[:, j, 0:1], 0.0), self.t_tab, self.t_u) for j in range(2)]
        self.t_z = []
        for m, n in enumerate([12, 13, 4, 5, 6, 7, 0, 1, 2, 3, 8, 9, 10, 11]):
            i, ps, fr = self.banks.take()
            t = self.dense([("in", n, k) for k in range(8)], Hs, ps[:, :], 128, fr)
            tmp = TMP[:, m % 2, :]
            ta = self.af(tmp[:, 1:513], ps[:, :], ACT.Copy, t, self.t_z[m - 2] if m >= 2 else z,
                         scale=self.pc("mu", n))
            tb = self.stt(ZB[:, n, :], ps[:, :], omm[:, n:n + 1], tmp[:, 0:512], ALU.mult, ALU.add, ta, t_o, z)
            self.banks.give(i, tb)
            self.t_z.append(tb)
            yield
        self.t_hfree = t

    def s5_apply(self):
        P = self.P
        dve, act, pool, sp = P.dve, P.act, P.pool, P.sp
        R = self.region
        U, TT, VM, W = self.U, self.TT, self.VM, self.W
        UG = R(36, 32, 64)
        ud = self.d["ud"]
        s = P.dsem("ud")
        t = P.dma(sp, ud.rearrange("(gt g) c t j -> (g c) gt (t j)", gt=4),
                  U.rearrange("p a t j -> p a (t j)"), s, self.t_u)
        s = P.dsem("ug")
        for dl in range(8):
            t_ug = P.dma(sp, UG[16 * dl:16 * dl + 16, :, :], ud[:, :, 7 - dl, :].rearrange("g c j -> c g j"),
                         s, t, self.t_w, self.t_tab)
        yield
        S = R(94, 2, 16, 64)
        t_e = []
        for ri in range(2):
            for h in range(2):
                i, ps, fr = self.banks.take()
                for g in range(16 * h, 16 * h + 16):
                    gp, par = g // 2, 64 * (g % 2)
                    t = self.mm(ps[par:par + 64, (gp - 8 * h) * 64:(gp - 8 * h) * 64 + 64],
                                VM[:, gp, ri, par:par + 64], UG[:, g, :], True, True, t_ug, self.t_vm, fr)
                t = self.cp(act, S[:, ri, 8 * h:8 * h + 8, :].rearrange("p a j -> p (a j)"), ps[:, :], t)
                self.banks.give(i, t)
                t_e.append(t)
                yield
        Sv = S.rearrange("p r g (b i) -> p r g b i", i=8)
        T1, T2 = R(102, 2, 16, 8), R(103, 2, 16, 8)
        P8R, P8I = self.P8R, self.P8I
        V = lambda out, a, b, op, *w: self.tt(dve, out, a, b, op, *w)

        def cstep(dst, src, wr, wi, T1, T2, *w):
            a = V(T1[:, 0], src[:, 0], wr, ALU.mult, *w)
            a = V(T1[:, 1], src[:, 1], wr, ALU.mult)
            b = V(T2[:, 0], src[:, 1], wi, ALU.mult)
            c = V(T2[:, 1], src[:, 0], wi, ALU.mult)
            a = V(dst[:, 0], dst[:, 0], T1[:, 0], ALU.add, a)
            b = V(dst[:, 1], dst[:, 1], T1[:, 1], ALU.add)
            a = V(dst[:, 0], dst[:, 0], T2[:, 0], ALU.subtract, a, c)
            b = V(dst[:, 1], dst[:, 1], T2[:, 1], ALU.add, b)
            return b
        t = t_e
        w8r = P8R[:, 0, :].unsqueeze(2).broadcast_to((128, 16, 8))
        w8i = P8I[:, 0, :].unsqueeze(2).broadcast_to((128, 16, 8))
        for k in range(1, 8):
            t = cstep(Sv[:, :, :, :, k], Sv[:, :, :, :, k - 1], w8r, w8i, T1, T2, t)
            yield
        for b in range(1, 8):
            t = cstep(Sv[:, :, :, b, 7], Sv[:, :, :, b - 1, 7], P8R[:, 7, :], P8I[:, 7, :],
                      T1[:, :, :, 0], T2[:, :, :, 0], t)
        yield
        for k in range(7):
            wr = P8R[:, k, :].unsqueeze(2).broadcast_to((128, 16, 7))
            wi = P8I[:, k, :].unsqueeze(2).broadcast_to((128, 16, 7))
            X1, X2 = R(102, 2, 16, 7), R(103, 2, 16, 7)
            t = cstep(Sv[:, :, :, 1:8, k], Sv[:, :, :, 0:7, 7], wr, wi, X1, X2, t)
            yield
        t_s = t
        YG = UG
        t_yg = []
        for q in range(4):
            i, ps, fr = self.banks.take()
            for gp in range(8 * (q // 2), 8 * (q // 2) + 8):
                g, par = 2 * gp + q % 2, 64 * (q % 2)
                o = (gp % 8) * 64
                self.mm(ps[:, o:o + 64], TT[:, g, :], UG[:, g, :], True, False, self.t_tt, t_ug, fr)
                for ri in range(2):
                    t = self.mm(ps[:, o + 1:o + 64], W[par:par + 64, ri, gp, 1:9, :].rearrange("p d c -> p (d c)"),
                                S[par:par + 64, ri, gp, 0:63], False, ri == 1, t_s)
            g0 = 16 * (q // 2) + q % 2
            t = self.cp(act, YG[:, g0:g0 + 15:2, :], ps[:, :].rearrange("p (g j) -> p g j", g=8), t)
            self.banks.give(i, t)
            t_yg.append(t)
            yield
        yd = self.d["yd"]
        s = P.dsem("yd")
        for tau in range(8):
            t = P.dma(sp, yd[:, :, tau, :].rearrange("g c j -> c g j"), YG[16 * tau:16 * tau + 16, :, :], s, t_yg)
        YS = R(118, 4, 512)
        s = P.dsem("ys")
        t_ys = P.dma(sp, YS, yd.rearrange("(gt g) c t j -> (g c) gt (t j)", gt=4), s, t)
        yield
        Z = R(44, 4, 512)
        t_z = []
        for n in range(4):
            t = self.stt(YS[:, n, :], U[:, n].rearrange("p t j -> p (t j)"), self.pc("s5d", n), YS[:, n, :],
                         ALU.mult, ALU.add, t_ys)
            t = self.af(Z[:, n, :], YS[:, n, :], ACT.Gelu_apprx_tanh, t, t_yg)
            t_z.append(t)
        yield
        OZ = R(52, 4, 512)
        t_oz = []
        for n in range(4):
            i, ps, fr = self.banks.take()
            t = self.dense([("glu", n, k) for k in range(4)], [Z[:, k, :] for k in range(4)], ps[:, :], 128, t_z, fr)
            t = self.af(YS[:, n, :], ps[:, :], ACT.Sigmoid, t, bias=self.pc("bglu", n))
            self.banks.give(i, t)
            t = self.tt(dve, OZ[:, n, :], Z[:, n, :], YS[:, n, :], ALU.mult, t)
            t_oz.append(t)
            yield
        OS = R(28, 4, 512)
        dst = [OS[:, n, :].rearrange("p (j t) -> p t j", t=8) for n in range(4)]
        tmp = R(104, 3, 512)
        t_r = self.norm_r([OZ[:, n, :] for n in range(4)], t_oz, 512, tmp)
        rr = tmp[:, 2, :].rearrange("p (t j) -> p t j", t=8)
        self.t_os = [self.stt(dst[n], OZ[:, n, :].rearrange("p (t j) -> p t j", t=8), self.pc("gain", n), rr,
                              ALU.mult, ALU.mult, t_r) for n in range(4)]

    def norm_r(self, src, t_src, feats, tmp, tmp_free=()):
        P = self.P
        i, ps, fr = self.banks.take()
        mms = []
        n = len(src)
        for k in range(n):
            sq = tmp[:, k % 2, :]
            w = mms[k - 2] if k >= 2 else tmp_free
            t = self.tt(P.pool, sq, src[k], src[k], ALU.mult, t_src[k], w)
            mms.append(self.mm(ps[:, :], self.C("ones"), sq, k == 0, k == n - 1, t, fr if k == 0 else ()))
        t = self.rsqrt(tmp[:, 2, :], ps[:, :], self.kc(EPS6), 1.0 / feats, mms[-1], tmp_free)
        self.banks.give(i, t)
        return t

    def rwkv(self, stop):
        P = self.P
        dve, act, pool = P.dve, P.act, P.pool
        R = self.region
        ZB = self.ZB
        CE = math.exp(-0.5)
        V = lambda out, a, b, op, *w: self.tt(dve, out, a, b, op, *w)
        G = lambda out, a, b, op, *w: self.tt(pool, out, a, b, op, *w)
        tz, to, hf = self.t_z, self.t_os, self.t_hfree
        SG, AS = self.H[:, 0:4, :], self.H[:, 4:8, :]
        w2, g2 = self.small[:, 0, :], self.small[:, 1, :]
        t = self.af(ZB[0:64, 12, :], ZB[0:64, 12, :], ACT.Tanh, tz)
        t_gl = self.af(ZB[:, 13, :], ZB[:, 13, :], ACT.Sigmoid, tz)
        t_sg, t_as = [], []
        for n in range(4):
            i, ps, fr = self.banks.take()
            m = self.mm(ps[:, :], w2[0:64, n * 128:n * 128 + 128], ZB[0:64, 12, :], True, True, t, fr, self.t_small)
            x = self.af(SG[:, n, :], ps[:, :], ACT.Sigmoid, m, hf, bias=self.pc("w0", n))
            self.banks.give(i, x)
            t_sg.append(x)
            i, ps, fr = self.banks.take()
            m = self.mm(ps[:, :], w2[64:128, n * 128:n * 128 + 128], ZB[64:128, 12, :], True, True, fr)
            x = self.af(AS[:, n, :], ps[:, :], ACT.Sigmoid, m, hf, bias=self.pc("a0", n))
            self.banks.give(i, x)
            t_as.append(x)
            yield
        omk = R(141.5, 4)
        t_omk = self.ts(dve, omk, self.pc("k_a", 0, 4), -1.0, ALU.mult, 1.0, ALU.add, to)
        AR = R(36, 4, 8, 2, 64)
        B = R(52, 4, 512)
        GC = R(142, 4, 8)
        E = R(68, 8, 512)
        t_ar, t_b, t_k, t_bv = [], [], [], []
        last_e = [to, None]
        RK, KK = [ZB[:, n, :] for n in range(4)], [ZB[:, 4 + n, :] for n in range(4)]
        VV = [ZB[:, 8 + n, :] for n in range(4)]
        v8 = lambda ap: ap.rearrange("p (c t) -> p c t", t=64)
        for n in range(4):
            o = 0
            cs, gam, ig, gp, x, y, z_, q = (R(68 + 16 * (n % 2), 8, 512)[:, i, :] for i in range(8))
            le = last_e[n % 2] if n >= 2 else to
            t = dve.do(lambda e, cs=cs, n=n: e.tensor_tensor_scan(out=cs, data0=self.C("scan"), data1=SG[:, n, :],
                       initial=0.0, op0=ALU.mult, op1=ALU.add), t_sg[n], le)
            tg = self.af(gam, cs, ACT.Exp, t, le, scale=-CE)
            ti = self.af(ig, cs, ACT.Exp, t, scale=CE)
            tp = G(gp, cs, SG[:, n, :], ALU.subtract, t, t_sg[n], le)
            tp = self.af(gp, gp, ACT.Exp, tp, scale=-CE)
            t_gc = self.cp(dve, GC[:, n, :], v8(gam)[:, :, 63], tg, to)
            t1 = self.ts(pool, x, KK[n], self.pc("k_k", n), ALU.mult, None, None, tz, le)
            t2 = G(y, x, x, ALU.mult, t1)
            i, ps, fr = self.banks.take()
            m = self.mm(ps[:, :], self.C("blk"), y, True, True, t2, fr)
            c = self.ts(dve, z_, ps[:, :], 2.0 ** 20, ALU.mult, 1e-24 * 2 ** 20, ALU.max, m, le)
            self.banks.give(i, c)
            c = self.af(z_, z_, ACT.Ln, c)
            c = self.af(z_, z_, ACT.Exp, c, scale=-0.5, bias=self.kc(TENLN2))
            tkk = V(x, x, z_, ALU.mult, c, t1)
            ta = self.stt(AR[:, n, :, 0, :], v8(x), -1.0, v8(gp), ALU.mult, ALU.mult, tkk, tp)
            tb = G(y, x, AS[:, n, :], ALU.mult, tkk, m, t_as[n])
            tb = V(B[:, n, :], y, ig, ALU.mult, tb, ti)
            yield
            t3 = self.ts(pool, q, AS[:, n, :], self.pc("k_a", n), ALU.mult, omk[:, n:n + 1], ALU.add, t_as[n], t_omk, le)
            t3 = G(KK[n], KK[n], q, ALU.mult, t3, t1)
            t4 = self.stt(q, RK[n], self.pc("r_k", n), KK[n], ALU.mult, ALU.mult, t3)
            i, ps, fr = self.banks.take()
            m = self.mm(ps[:, :], self.C("blk"), q, True, True, t4, fr)
            t5 = V(z_, VV[n], ps[:, :], ALU.mult, m, tkk)
            self.banks.give(i, t5)
            BVn = self.H[:, n, :]
            t6 = self.cp(pool, BVn, z_, t5, t, tp)
            tr_ = V(AR[:, n, :, 1, :], v8(RK[n]), v8(gam), ALU.mult, tg, t4)
            tk = G(KK[n], KK[n], ig, ALU.mult, t4, ti)
            t_ar += [ta, tr_]
            t_b.append(tb)
            t_k.append(tk)
            t_bv.append(t6)
            last_e[n % 2] = [t6, tk, tr_, tb, ta, t_gc, m]
            yield
        ew = [t_ar, t_b, t_k, t_bv, last_e]
        self.dump("ar", R(36, 4096), ew)
        M, LT, LL, PP, MT, KA, BR, KR = (R(68 + 8 * i, 4, 512) for i in range(8))
        mk = lambda name: self.C(name).unsqueeze(1).broadcast_to((128, 8, 64))
        h8 = lambda ap: ap.rearrange("p (h t) -> p h t", t=64)
        tM, tMT, tLT, tKA, tBR, tKR = {}, {}, {}, {}, {}, {}
        for pp in range(2):
            for hp in (0, 64):
                i, ps, fr = self.banks.take()
                for p in range(2 * pp, 2 * pp + 2):
                    for n in range(4):
                        for par in range(2):
                            c, o = 2 * p + par, (p % 2) * 256 + n * 64
                            t = self.mm(ps[64 * par:64 * par + 64, o:o + 64], AR[hp:hp + 64, n, c, 0, :],
                                        B[hp:hp + 64, n, c * 64:c * 64 + 64], True, True, ew, fr)
                dst = M[:, 2 * pp:2 * pp + 2, :].rearrange("p q (n a t) -> p q n a t", a=2, t=64)[:, :, :, hp // 64, :]
                m4 = lambda name: self.C(name).unsqueeze(1).unsqueeze(1).broadcast_to((128, 2, 4, 64))
                t = V(dst, ps[:, :].rearrange("p (q n t) -> p q n t", q=2, t=64), m4("m2L"), ALU.mult, t)
                self.banks.give(i, t)
            for p in range(2 * pp, 2 * pp + 2):
                tM[p] = G(h8(M[:, p, :]), h8(M[:, p, :]), mk("I64"), ALU.add, t)
            yield
        for p in range(4):
            ks = []
            for hp in (0, 64):
                for which in (0, 1):
                    i, ps, fr = self.banks.take()
                    for n in range(4):
                        for par in range(2):
                            c = 2 * p + par
                            l = (B[hp:hp + 64, n, :] if which == 0 else KK[n][hp:hp + 64, :])[:, c * 64:c * 64 + 64]
                            t = self.mm(ps[64 * par:64 * par + 64, n * 128:n * 128 + 128], l,
                                        AR[hp:hp + 64, n, c, :, :].rearrange("p a t -> p (a t)"), True, True, ew, fr)
                    pv = ps[:, :].rearrange("p (n a t) -> p n a t", a=2, t=64)
                    n4 = lambda z: z[:, p, :].rearrange("p (n a t) -> p n a t", a=2, t=64)[:, :, hp // 64, :]
                    mk4 = lambda name: self.C(name).unsqueeze(1).broadcast_to((128, 4, 64))
                    a = V(n4(LT if which == 0 else KA), pv[:, :, 0, :], mk4("mSU"), ALU.mult, t)
                    b = V(n4(BR if which == 0 else KR), pv[:, :, 1, :], mk4("mIU"), ALU.mult)
                    self.banks.give(i, b)
                    ks.append(b)
                    if which == 0:
                        tLT[p, hp] = a
                yield
            tLT[p] = tLT[p, 64]
            t = G(h8(MT[:, p, :]), h8(LT[:, p, :]), mk("m2U"), ALU.mult, tLT[p])
            tMT[p] = G(h8(MT[:, p, :]), h8(MT[:, p, :]), mk("I64"), ALU.add, t)
            tKA[p] = ks[-1]
        t_gram = ks[-1]
        VTk, BTk = self.H[:, 4:8, :], R(60, 4, 512)
        t_tok = []

        def tok_tr(src, dst, *w):
            out = []
            for p in range(4):
                i, ps, fr = self.banks.take()
                for n in range(4):
                    t = self.tr(ps[:, n * 128:n * 128 + 128], src[n][:, p * 128:p * 128 + 128], w, fr)
                t = self.cp(act, dst[:, p, :], ps[:, :], t)
                self.banks.give(i, t)
                out.append(t)
            return out, t
        self.tv_, _ = tok_tr(VV, VTk, t_gram)
        yield
        self.tb_, _ = tok_tr([B[:, n, :] for n in range(4)], BTk, t_gram)
        yield
        KTk = R(16, 4, 512)
        self.tk_, _ = tok_tr(KK, KTk, t_gram, self.tv_)
        yield
        for l in range(5):
            lv = self.cst[:, CC["lvl"][0] + 64 * l:CC["lvl"][0] + 64 * l + 64].unsqueeze(1).broadcast_to((128, 8, 64))
            tP, tL = {}, {}
            for p in range(4):
                tL[p] = G(h8(LL[:, p, :]), h8(LT[:, p, :]), lv, ALU.mult, tMT[p])
            for p in range(4):
                i, ps, fr = self.banks.take()
                for h in range(8):
                    for par in (0, 64):
                        r, c = slice(par, par + 64), slice(h * 64, h * 64 + 64)
                        t = self.mm(ps[r, c], LL[r, p, c], M[r, p, c], True, True, tL[p], tM[p], fr)
                tP[p] = self.cp(act, PP[:, p, :], ps[:, :], t)
                self.banks.give(i, tP[p])
                yield
            for p in range(4):
                iM, pM, fM = self.banks.take() if l < 4 else (None, None, None)
                iT, pT, fT = self.banks.take()
                for h in range(8):
                    for par in (0, 64):
                        r, c = slice(par, par + 64), slice(h * 64, h * 64 + 64)
                        if l < 4:
                            tm = self.mm(pM[r, c], MT[r, p, c], PP[r, p, c], True, True, tP[p], fM)
                        tt_ = self.mm(pT[r, c], PP[r, p, c], MT[r, p, c], True, True, tP[p], fT)
                if l < 4:
                    tM[p] = V(M[:, p, :], M[:, p, :], pM[:, :], ALU.add, tm, tM[p])
                    self.banks.give(iM, tM[p])
                tMT[p] = V(MT[:, p, :], MT[:, p, :], pT[:, :], ALU.add, tt_, tMT[p])
                self.banks.give(iT, tMT[p])
                yield
        self.dump("mt", R(100, 2048), list(tMT.values()))
        ST, XX, UU, TS = R(76, 4, 128), R(80, 2, 512), R(84, 2, 512), R(90, 4, 64)
        Y = R(0, 4, 512)
        t0 = [tMT[3], self.tk_, self.tb_, self.tv_]
        tST = [dve.do(lambda e: e.memset(ST, 0.0), t0)]
        tS0 = tST[0]
        t_y, t_xf, t_uf = [], {}, {}
        for c in range(8):
            p, par = c // 2, 64 * (c % 2)
            r = slice(par, par + 64)
            i, ps, fr = self.banks.take()
            for h in range(8):
                hs = slice(h * 64, h * 64 + 64)
                self.mm(ps[r, hs], KA[r, p, hs], VTk[r, p, hs], h == 0, False, t0, fr)
            for n in range(4):
                t = self.mm(ps[r, n * 128:n * 128 + 128], AR[:, n, c, 0, :], ST[:, n, :], False, True, tST)
            tx = self.cp(act, XX[r, c // 2 % 2, :], ps[r, :], t, t_xf.get(c - 4), tS0)
            self.banks.give(i, tx)
            i, ps, fr = self.banks.take()
            for h in range(8):
                hs = slice(h * 64, h * 64 + 64)
                t = self.mm(ps[r, hs], MT[r, p, hs], XX[r, c // 2 % 2, hs], True, True, tx, fr)
            t_xf[c] = t
            tu = self.cp(act, UU[r, c // 2 % 2, :], ps[r, :], t, t_uf.get(c - 4), tS0)
            self.banks.give(i, tu)
            i, ps, fr = self.banks.take()
            for h in range(8):
                n, hp = h // 2, slice(64 * (h % 2), 64 * (h % 2) + 64)
                hs = slice(h * 64, h * 64 + 64)
                o = ps[hp, n * 64:n * 64 + 64]
                self.mm(o, KTk[r, p, hs], VTk[r, p, hs], h < 2, False, fr)
            for h in range(8):
                n, hp = h // 2, slice(64 * (h % 2), 64 * (h % 2) + 64)
                hs = slice(h * 64, h * 64 + 64)
                t = self.mm(ps[hp, n * 64:n * 64 + 64], BTk[r, p, hs], UU[r, c // 2 % 2, hs], False, True, tu)
            ty = []
            for hp in (0, 64):
                ty.append(V(TS[hp:hp + 64], ps[hp:hp + 64, 0:256].rearrange("p (n v) -> p n v", v=64),
                            ST[hp:hp + 64, :, hp:hp + 64], ALU.add, t, tST))
            self.banks.give(i, ty)
            i, ps, fr = self.banks.take()
            for n in range(4):
                self.mm(ps[:, n * 64:n * 64 + 64], ST[:, n, :], AR[:, n, c, 1, :], n == 0, False, fr)
            for h in range(8):
                n, hp = h // 2, slice(64 * (h % 2), 64 * (h % 2) + 64)
                hs = slice(h * 64, h * 64 + 64)
                o = ps[hp, n * 64:n * 64 + 64]
                self.mm(o, VTk[r, p, hs], KR[r, p, hs], False, False)
                t = self.mm(o, UU[r, c // 2 % 2, hs], BR[r, p, hs], False, True)
            t_uf[c] = t
            tST = [V(ST[hp:hp + 64, :, hp:hp + 64], TS[hp:hp + 64],
                     GC[hp:hp + 64, :, c].unsqueeze(2).broadcast_to((64, 4, 64)), ALU.mult, ty, t) for hp in (0, 64)]
            t = self.cp(act, Y[:, :, c * 64:c * 64 + 64], ps[:, 0:256].rearrange("p (n v) -> p n v", v=64), t, t0)
            self.banks.give(i, t)
            t_y.append(t)
            yield
        self.dump("y0", R(0, 2048), t_y)
        self.t_yr = []
        D = [(R(92, 512), R(94, 512), R(96, 512)), (R(68, 512), R(70, 512), R(72, 512))]
        le = [t_y, t_y]
        nb = []
        for n in range(4):
            a, b, c = D[n % 2]
            y = Y[:, n, :]
            i, ps, fr = self.banks.take()
            m = self.mm(ps[:, :], self.C("blk"), y, True, True, t_y, fr)
            t1 = self.stt(y, ps[:, :], -1.0 / 64, y, ALU.mult, ALU.add, m)
            self.banks.give(i, t1)
            t2 = self.af(a, y, ACT.Square, t1, le[n % 2])
            i, ps, fr = self.banks.take()
            m = self.mm(ps[:, :], self.C("blk"), a, True, True, t2, fr)
            t2 = self.rsqrt(b, ps[:, :], self.kc(EPSLN), 1.0 / 64, m, le[n % 2])
            self.banks.give(i, t2)
            t3 = self.stt(y, y, self.pc("lnw", n), b, ALU.mult, ALU.mult, t2, t1)
            t3 = self.stt(y, y, self.pc("lnb", n), self.H[:, n, :], ALU.add, ALU.add, t3)
            i, ps, fr = self.banks.take()
            m = self.mm(ps[:, :], g2[:, n * 128:n * 128 + 128], ZB[:, 13, :], True, True, t_gl, fr)
            t3 = V(y, y, ps[:, :], ALU.mult, m, t3)
            self.banks.give(i, t3)
            le[n % 2] = t3
            self.t_yr.append(t3)
            yield

    def load_layer_tables(self, *after):
        P, R = self.P, self.region
        self.c2 = R(24, NC2)
        self.lw = [R(108, 2560), R(118, 2560)]
        s = P.dsem("c2")
        self.t_c2 = P.dma(P.sp, self.c2, self.d["cst2"], s, *after)
        s = P.dsem("lw")
        for l in range(2):
            self.t_lw = P.dma(P.sp, self.lw[l], self.d["lw"][l], s, *after)

    def layers(self, stop):
        P, R = self.P, self.region
        X = [self.X[:, k, :] for k in range(8)]
        Hs = [self.H[:, k, :] for k in range(8)]
        t_end = [self.t_X, self.t_ff]
        for l in range(2):
            self.l = l
            t_h = self.norm_mod(X, Hs, self.t_X, [self.pc(f"ng{l}", k) for k in range(8)],
                                tmp=R(136, 3, 512), tmp_free=t_end)
            self.layer_proj(l, Hs, t_h, t_end)
            self.run((self.attention(l), 3), (self.conv(l, Hs), 1))
            Y = [self.G[:, k, :] for k in range(12)]
            self.dump("Y12" if l == 0 else "", self.G, self.t_y)
            t_X = []
            so = P.dsem("out") if l == 1 else None
            for n in range(8):
                i, ps, fr = self.banks.take()
                t = self.dense([(f"o{l}", n, k) for k in range(12)], Y, ps[:, :], 128, self.t_y, fr)
                u = self.tt(P.dve, X[n], ps[:, :], X[n], ALU.add, t)
                self.banks.give(i, u)
                t_X.append(u)
                if l == 1:
                    P.dma(P.sp, self.out[:, n, :], X[n], so, u)
            self.t_X = t_X
            t_end = [t_X, t]
            self.dump("l0" if l == 0 else "", self.X[:, :, :], t_X)
            if stop == "l0":
                return

    def layer_proj(self, l, Hs, t_h, t_end):
        P, R = self.P, self.region
        act, dve = P.act, P.dve
        self.G = R(0, 12, 512)
        self.L = R(37, 3, 512)
        self.KR, self.QR = R(75, 2, 512), R(79, 2, 512)
        self.SQ, self.SK, self.SV = R(95, 4, 512), R(103, 512), R(105, 4, 128)
        name = f"l{l}"

        def proj(n, M=128, rows=slice(0, 128)):
            i, ps, fr = self.banks.take()
            t = self.dense([(name, n, k) for k in range(8)], Hs, ps[rows, :], M, t_h, fr)
            return i, ps, t
        self.t_l = []
        for n in range(3):
            i, ps, t = proj(n)
            t = self.cp(act, self.L[:, n, :], ps[:, :], t, t_end)
            self.banks.give(i, t)
            self.t_l.append(t)
        i, ps, t = proj(3, 32, slice(64, 96))
        ta = self.cp(act, self.KR[64:96, 0, :], ps[64:96, :], t, t_end)
        tb = self.cp(act, self.KR[64:96, 1, :], ps[64:96, :], t)
        self.banks.give(i, ta, tb)
        self.t_rope = tb
        self.t_sq = []
        for n in range(4):
            i, ps, t = proj(24 + n)
            t = self.cp(act, self.SQ[:, n, :], ps[:, :], t, t_end)
            self.banks.give(i, t)
            self.t_sq.append(t)
        i, ps, t = proj(28)
        self.t_sk = self.cp(act, self.SK, ps[:, :], t, t_end)
        self.banks.give(i, self.t_sk)
        i, ps, fr = self.banks.take()
        for k in range(8):
            w, wt = self.wblock((name, 29, k))
            for q in range(4):
                t = self.mm(ps[:, q * 128:q * 128 + 128], Hs[k][:, q * 128:q * 128 + 128], w,
                            k == 0 and q == 0, k == 7, wt, fr)
            self.wused(t)
        self.t_sv = self.cp(act, self.SV.rearrange("p q v -> p (q v)"), ps[:, :], t, t_end)
        self.banks.give(i, self.t_sv)
        self.t_g = {}
        for n in range(4):
            for m, src in ((n, 4 + n), (8 + n, 30 + n)):
                i, ps, t = proj(src)
                t = self.af(self.G[:, m, :], ps[:, :], ACT.Silu, t, t_end)
                self.banks.give(i, t)
                self.t_g[m] = t
        self.t_y = []
        self.t_end = t_end

    def conv(self, l, Hs):
        P, R = self.P, self.region
        act, dve = P.act, P.dve
        name = f"l{l}"
        CH, CU, YC = R(87, 512), R(144, 516), R(136, 4, 512)

        def proj(n):
            i, ps, fr = self.banks.take()
            t = self.dense([(name, n, k) for k in range(8)], Hs, ps[:, :], 128, fr)
            return i, ps, t
        t0 = dve.do(lambda e: e.memset(CU[:, 0:2], 0.0), self.t_end)
        CH = R(147, 512)
        t_y, t_u = t0, t0
        raw = []
        for j in range(4):
            i, ps, t = proj(8 + j)
            ta = self.cp(act, CH, ps[:, :], t, t_u)
            self.banks.give(i, ta)
            yield
            i, ps, t = proj(16 + j)
            t_u = self.tt(dve, CU[:, 2:514], ps[:, :], CH, ALU.mult, t, ta, t_y)
            self.banks.give(i, t_u)
            y = YC[:, j, :]
            a = self.ts(dve, y, CU[:, 0:512], self.pc(f"cw{l}", j), ALU.mult, None, None, t_u)
            a = self.stt(y, CU[:, 1:513], self.pc(f"cw{l}", 4 + j), y, ALU.mult, ALU.add, a)
            t_y = self.stt(y, CU[:, 2:514], self.pc(f"cw{l}", 8 + j), y, ALU.mult, ALU.add, a)
            yield
            i, ps, t = proj(12 + j)
            b = self.tt(dve, y, y, ps[:, :], ALU.mult, t, t_y)
            self.banks.give(i, b)
            yield
            i, ps, t = proj(20 + j)
            c = self.cp(dve, self.G[:, 4 + j, :], ps[:, :], t)
            self.banks.give(i, c)
            raw.append((b, c))
            yield
        for j in range(4):
            t = self.af(self.G[:, 4 + j, :], self.G[:, 4 + j, :], ACT.Silu, raw[j][1])
            self.t_y.append(self.tt(P.pool, self.G[:, 4 + j, :], self.G[:, 4 + j, :], YC[:, j, :], ALU.mult, t, raw[j][0]))

    def head_norm(self, l, raw, dst, gain, k, t_raw, t_free):
        P = self.P
        TM = self.region(128, 4, 512)
        sq, rr = TM[0:96, 2 * k, :], TM[0:96, 2 * k + 1, :]
        fr0 = self.hn_free.get(k)
        t = self.tt(P.pool, sq, raw, raw, ALU.mult, t_raw, fr0)
        i, ps, fr = self.banks.take()
        m = self.mm(ps[0:96, :], self.C("ones")[0:96, 0:96], sq, True, True, t, fr)
        t = self.rsqrt(rr, ps[0:96, :], self.kc(EPS6)[0:96], 1.0 / 96, m, fr0)
        self.banks.give(i, t)
        t1 = self.stt(dst, raw, gain[0:96], rr, ALU.mult, ALU.mult, t, t_free)
        i, ps, fr = self.banks.take()
        c2 = self.c2
        m2 = self.mm(ps[64:96, :], c2[64:96, 3072:3104], dst[64:96, :], True, True, t1, fr, self.t_c2)
        a = self.tt(P.pool, sq[64:96], dst[64:96], c2[64:96, 2048:2560], ALU.mult, t1, m)
        b = self.tt(P.dve, rr[64:96], ps[64:96, :], c2[64:96, 2560:3072], ALU.mult, m2, t1)
        self.banks.give(i, b)
        c = self.tt(P.pool, dst[64:96], sq[64:96], rr[64:96], ALU.add, a, b)
        self.hn_free[k] = [c, t1]
        return c, t1

    def mla(self, l):
        P, R = self.P, self.region
        act, dve, pool = P.act, P.dve, P.pool
        L, lw = self.L, self.lw[l]
        self.hn_free = {0: self.t_end, 1: self.t_end}
        tmp = R(128, 3, 512)
        t = self.norm_r([L[:, 0, :], L[:, 1, :]], self.t_l[0:2], 256, tmp, self.t_end)
        tq = [self.stt(L[:, k, :], L[:, k, :], self.pc(f"qan{l}", k), tmp[:, 2, :], ALU.mult, ALU.mult, t) for k in range(2)]
        t = self.norm_r([L[:, 2, :]], self.t_l[2:3], 128, tmp, tq)
        tkv = self.stt(L[:, 2, :], L[:, 2, :], self.pc(f"kvan{l}"), tmp[:, 2, :], ALU.mult, ALU.mult, t)
        self.hn_free = {0: [tkv], 1: [tkv]}
        yield
        MV = R(87, 4, 512)
        t_mv = []
        for q in range(4):
            i, ps, fr = self.banks.take()
            t = self.mm(ps[:, :], L[:, 2, q * 128:q * 128 + 128], lw[:, 2048:2560], True, True, tkv, self.t_lw, fr)
            t = self.cp(act, MV[:, q, :], ps[:, :], t, self.t_end)
            self.banks.give(i, t)
            t_mv.append(t)
            yield
        KH, QH, PB, PT = R(43, 2, 512), R(47, 2, 512), R(51, 4, 512), R(59, 2, 4, 512)
        ST = R(149.5, 2, 4, 4)
        sc = 96.0 ** -0.5
        raw_free = {}
        t_sc, t_pt, t_pv = {}, {}, {}
        for h in range(8):
            b = h % 2
            i, ps, fr = self.banks.take()
            t = self.mm(ps[0:64, :], lw[:, 1536 + 64 * h:1600 + 64 * h], L[:, 2, :], True, True, tkv, fr)
            t = self.cp(act, self.KR[0:64, b, :], ps[0:64, :], t, raw_free.get((0, b), self.t_end))
            self.banks.give(i, t)
            tK, u = self.head_norm(l, self.KR[0:96, b, :], KH[0:96, b, :], self.pc(f"kn{l}"), 0,
                                   [t, self.t_rope], [t_sc.get(h - 2), self.t_end])
            raw_free[0, b] = u
            yield
            i, ps, fr = self.banks.take()
            self.mm(ps[0:96, :], lw[:, 96 * h:96 * h + 96], L[:, 0, :], True, False, tq, fr)
            t = self.mm(ps[0:96, :], lw[:, 768 + 96 * h:864 + 96 * h], L[:, 1, :], False, True)
            t = self.cp(act, self.QR[0:96, b, :], ps[0:96, :], t, raw_free.get((1, b), self.t_end))
            self.banks.give(i, t)
            tQ, u = self.head_norm(l, self.QR[0:96, b, :], QH[0:96, b, :], self.pc(f"qn{l}"), 1,
                                   t, [t_sc.get(h - 2), self.t_end])
            raw_free[1, b] = u
            yield
            mx, nm, rs, rc = (ST[:, b, k, :] for k in range(4))
            hold, tm = [], []
            for q in range(4):
                n = 128 * (q + 1)
                i, ps, fr = self.banks.take()
                t = self.mm(ps[:, 0:n], QH[0:96, b, q * 128:q * 128 + 128], KH[0:96, b, 0:n], True, True, tK, tQ, fr)
                hold.append((i, ps))
                t_sc[h] = t
                t = self.tt(dve, ps[:, n - 128:n], ps[:, n - 128:n], self.C("caus"), ALU.add, t)
                tm.append(dve.do(lambda e, o=mx[:, q:q + 1], a=ps[:, 0:n]: e.tensor_reduce(out=o, in_=a, op=ALU.max, axis=AX.X),
                                 t, t_pt.get(h - 2)))
            t = self.ts(dve, nm, mx, -sc, ALU.mult, None, None, tm)
            yield
            te = []
            for q in range(4):
                n = 128 * (q + 1)
                i, ps = hold[q]
                e_ = self.af(PB[:, q, 0:n], ps[:, 0:n], ACT.Exp, t, t_pt.get(h - 1, self.t_end), bias=nm[:, q:q + 1],
                             scale=sc, acc=rs[:, q:q + 1])
                self.banks.give(i, e_)
                te.append(e_)
            t = dve.do(lambda e, rc=rc, rs=rs: e.reciprocal(rc, rs), te)
            tp = [self.ts(pool, PB[:, q, 0:128 * q + 128], PB[:, q, 0:128 * q + 128], rc[:, q:q + 1], ALU.mult,
                          None, None, t, te[q]) for q in range(4)]
            yield
            t_pt[h] = []
            ev = []
            for j in range(4):
                i, ps, fr = self.banks.take()
                for q in range(j, 4):
                    t = self.tr(ps[:, q * 128:q * 128 + 128], PB[:, q, j * 128:j * 128 + 128], tp[q], fr)
                e_ = self.cp(act if j == 3 else dve, PT[:, b, j, j * 128:512], ps[:, j * 128:512], t,
                             t_pv.get(h - 2, self.t_end))
                self.banks.give(i, e_)
                ev.append(e_)
                t_pt[h].append(t)
            yield
            i, ps, fr = self.banks.take()
            r = slice(64 * b, 64 * b + 64)
            for j in range(4):
                t = self.mm(ps[r, j * 128:512], MV[:, j, 64 * h:64 * h + 64], PT[:, b, j, j * 128:512],
                            j == 0, j == 3, ev, t_mv, fr)
            t_pv[h] = t
            g = self.G[r, h // 2, :]
            t = self.tt(dve, g, ps[r, :], g, ALU.mult, t, self.t_g[h // 2])
            self.banks.give(i, t)
            self.t_y.append(t)
            yield
        self.t_mla = [t_sc[7], t_pt[7], t_pv[7], t]

    def attention(self, l):
        yield from self.mla(l)
        yield from self.swa(l)

    def swa(self, l):
        P, R = self.P, self.region
        act, dve, pool = P.act, P.dve, P.pool
        SQ, SK, SV = self.SQ, self.SK, self.SV
        tmp = [(R(43, 512), R(45, 512)), (R(47, 512), R(49, 512))]
        le = [self.t_mla, self.t_mla]
        tn = []
        for n in range(5):
            s = SQ[:, n, :] if n < 4 else SK
            a, b = tmp[n % 2]
            t = self.tt(pool, a, s, s, ALU.mult, self.t_sq[n] if n < 4 else self.t_sk, le[n % 2])
            i, ps, fr = self.banks.take()
            m = self.mm(ps[:, :], self.C("blk"), a, True, True, t, fr)
            t = self.rsqrt(b, ps[:, :], self.kc(EPS6), 1.0 / 64, m, le[n % 2])
            self.banks.give(i, t)
            t = self.stt(s, s, self.pc(f"sqn{l}" if n < 4 else f"skn{l}"), b, ALU.mult, ALU.mult, t)
            le[n % 2] = [t, m]
            tn.append(t)
            yield
        Z, PT = R(51, 8, 256), R(59, 2, 2, 512)
        ST = R(150, 5, 8)
        mx, nm, rs, es, rc = (ST[:, k, :] for k in range(5))
        al = self.c2[:, 0:2048].rearrange("p (h k) -> p h k", h=8)
        sink = self.pc(f"sink{l}", 0, 8)
        t_tr, t_pv = [self.t_mla], [self.t_mla]
        for n in range(4):
            lo = 128 if n == 0 else 0
            w = 256 - lo
            k0 = (n - 1) * 128 + lo
            tz = []
            for g in range(2):
                for jj in range(2):
                    i, ps, fr = self.banks.take()
                    for x in range(2):
                        j = 2 * jj + x
                        t = self.mm(ps[:, x * 256 + lo:x * 256 + 256], SQ[64 * g:64 * g + 64, j, n * 128:n * 128 + 128],
                                    SK[64 * g:64 * g + 64, k0:k0 + w], True, True, tn, fr)
                    h0 = 4 * jj + g
                    t = self.stt(Z[:, h0:h0 + 3:2, lo:256], ps[:, :].rearrange("p (x k) -> p x k", x=2)[:, :, lo:256],
                                 0.125, al[:, h0:h0 + 3:2, lo:256], ALU.mult, ALU.add, t, self.t_c2, t_tr)
                    self.banks.give(i, t)
                    tz.append(t)
                yield
            t = dve.do(lambda e, lo=lo: e.tensor_reduce(out=mx, in_=Z[:, :, lo:256], op=ALU.max, axis=AX.X), tz)
            t = self.tt(dve, mx, mx, sink, ALU.max, t)
            ta = self.ts(dve, nm, mx, -1.0, ALU.mult, None, None, t)
            tb = self.tt(dve, es, sink, mx, ALU.subtract, t)
            te = [self.af(Z[:, h, lo:256], Z[:, h, lo:256], ACT.Exp, ta, tz, bias=nm[:, h:h + 1], acc=rs[:, h:h + 1])
                  for h in range(8)]
            tb = self.af(es, es, ACT.Exp, tb)
            yield
            t = self.tt(dve, rc, rs, es, ALU.add, te, tb)
            t = dve.do(lambda e: e.reciprocal(rc, rc), t)
            tp = self.tt(pool, Z[:, :, lo:256], Z[:, :, lo:256], rc.unsqueeze(2).broadcast_to((128, 8, w)), ALU.mult, t, te)
            yield
            ev, t_tr = {}, []
            for g in range(2):
                for kb in range(lo // 128, 2):
                    i, ps, fr = self.banks.take()
                    for j in range(4):
                        t = self.tr(ps[:, j * 128:j * 128 + 128], Z[:, 2 * j + g, kb * 128:kb * 128 + 128], tp, fr)
                    t_tr.append(t)
                    e_ = self.cp(act if kb else dve, PT[:, g, kb, :], ps[:, :], t, t_pv)
                    self.banks.give(i, e_)
                    ev[g, kb] = e_
                yield
            i, ps, fr = self.banks.take()
            for g in range(2):
                kbs = range(lo // 128, 2)
                for kb in kbs:
                    t = self.mm(ps[64 * g:64 * g + 64, :], SV[:, n - 1 + kb, 64 * g:64 * g + 64], PT[:, g, kb, :],
                                kb == kbs[0], kb == 1, list(ev.values()), self.t_sv, fr)
            t_pv = [t]
            gt = self.G[:, 8:12, n * 128:n * 128 + 128]
            t = self.tt(dve, gt, ps[:, :].rearrange("p (j q) -> p j q", j=4), gt, ALU.mult, t,
                        [self.t_g[8 + j] for j in range(4)])
            self.banks.give(i, t)
            self.t_y.append(t)
            yield


def _cols(a, n):
    return np.asarray(a, np.float32).reshape(n, 128).T


def _pad(a, rows):
    out = np.zeros((rows,) + a.shape[1:], np.float32)
    out[:a.shape[0]] = a
    return out


SW = [0, 4, 1, 5, 2, 6, 3, 7]


def _heads(a, axis):
    a = np.moveaxis(a, axis, 0)
    a = a.reshape((8, 64) + a.shape[1:])[SW].reshape((512,) + a.shape[1:])
    return np.moveaxis(a, 0, axis)


def _weights(inp):
    W = {"ada": inp["w_ada"][0], "in": inp["w_in"][0], "glu": inp["s5_w_glu"][0], "out": inp["w_out"][0],
         "gate": inp["ffn_w_gate"][0], "up": inp["ffn_w_up"][0], "down": inp["ffn_w_down"][0]}
    for l in range(2):
        w = inp["w_in_2"][l]
        o = np.cumsum([0, 256, 128, 32, 512, 512, 512, 512, 512, 512, 128, 128, 512])
        part = [w[:, o[i]:o[i + 1]] for i in range(12)]
        rope = np.zeros((1024, 128), np.float32)
        rope[:, :32] = part[2]
        W[f"l{l}"] = np.concatenate([part[0], part[1], rope, part[3], part[4], part[5], part[6], part[7],
                                     _heads(part[8], 1), part[9], part[10], _heads(part[11], 1)], 1)
        wo = inp["w_out_2"][l]
        W[f"o{l}"] = np.concatenate([wo[:1024], _heads(wo[1024:], 0)], 0)
    return W


def _arrays(inp):
    f = lambda n: np.asarray(inp[n], np.float32)
    par = np.zeros((128, NPC), np.float32)

    def put(name, a):
        s, n = PCOLS[name]
        par[:a.shape[0], s:s + n] = a
    put("b_ada", _cols(f("b_ada")[0], 48))
    put("mu", _cols(f("mu_shift")[0], 14))
    for name, src in (("w0", "rw_w0"), ("a0", "rw_a0"), ("k_k", "rw_k_k"), ("k_a", "rw_k_a"), ("lnw", "rw_lnx_w"),
                      ("lnb", "rw_lnx_b"), ("bglu", "s5_b_glu"), ("gain", "s5_gain")):
        put(name, _cols(f(src)[0], 4))
    put("r_k", _cols(f("rw_r_k")[0].reshape(512), 4))
    put("s5d", _cols(f("s5_d")[0].reshape(512), 4))
    put("fgain", _cols(f("final_gain"), 8))
    put("c", _cols(f("c")[0], 8))
    put("are", f("s5_a_re")[0].reshape(16, 128).T)
    put("aim", f("s5_a_im")[0].reshape(16, 128).T)
    put("ldt", np.repeat(f("s5_log_dt")[0].reshape(16, 2), 64, axis=1).T)
    for l in range(2):
        put(f"ng{l}", _cols(f("norm_g_2")[l], 8))
        put(f"qan{l}", _cols(f("mla_q_a_norm_2")[l], 2))
        put(f"kvan{l}", _cols(f("mla_kv_a_norm_2")[l], 1))
        put(f"qn{l}", f("mla_q_norm_2")[l][:, None])
        put(f"kn{l}", f("mla_k_norm_2")[l][:, None])
        put(f"cw{l}", np.concatenate([_cols(f("conv_w_2")[l][w], 4) for w in range(3)], 1))
        put(f"sqn{l}", np.tile(f("swa_q_norm_2")[l], 2)[:, None])
        put(f"skn{l}", np.tile(f("swa_k_norm_2")[l], 2)[:, None])
        put(f"sink{l}", np.broadcast_to(f("swa_sinks_2")[l][SW][None, :], (128, 8)))
    cst, cst2 = constants()
    b = lambda a: a.reshape(16, 128, 16).transpose(1, 0, 2).reshape(128, 256)
    bt = lambda a: b(a.transpose(0, 2, 1))
    s5p = np.stack([b(f("s5_b_re")[0]), b(f("s5_b_im")[0]), bt(f("s5_c_re")[0]), bt(f("s5_c_im")[0])], 1)
    small = np.stack([np.concatenate([f("rw_w2")[0], f("rw_a2")[0]], 0), f("rw_g2")[0]], 1)
    lw = []
    for l in range(2):
        qb, kvb = f("mla_w_qb_2")[l], f("mla_w_kvb_2")[l].reshape(128, 8, 128)
        lw.append(np.concatenate([qb[0:128], qb[128:256], kvb[:, :, :64].reshape(128, 512),
                                  kvb[:, :, 64:].reshape(128, 512)], 1))
    xT = f("x")[0].T.reshape(8, 128, 512).transpose(1, 0, 2)
    out = {"par": par, "cst": cst, "cst2": cst2, "s5p": s5p, "small": small, "lw": np.stack(lw), "xT": xT}
    return {k: np.ascontiguousarray(v) for k, v in out.items()}


def _program(nc, stop=None, dump_shapes=None):
    shapes = {"par": [128, NPC], "cst": [128, NCC], "cst2": [128, NC2], "s5p": [128, 4, 256],
              "small": [128, 2, 512], "lw": [2, 128, 2560], "xT": [128, 8, 512], "ws": [UNITS, 128, 1024]}
    d = {n: nc.dram_tensor("in_" + n, s, F32, kind="ExternalInput").ap() for n, s in shapes.items()}
    for n, s in (("kpad", [32, 16, 240]), ("ud", [32, 16, 8, 64]), ("yd", [32, 16, 8, 64])):
        d[n] = nc.dram_tensor("scr_" + n, s, F32).ap()
    out = nc.dram_tensor("outT", [128, 8, 512], F32, kind="ExternalOutput").ap()
    dumps = {n: nc.dram_tensor("dump_" + n, s, F32, kind="ExternalOutput").ap() for n, s in (dump_shapes or {}).items()}
    return Kern(nc, d, out, dumps).build(stop)


def _stream(W, order):
    ws = np.zeros((UNITS, 128, 8, 128), np.float32)
    for b, (name, n, k) in enumerate(order):
        ws[b // 8, :, b % 8, :] = W[name][k * 128:k * 128 + 128, n * 128:n * 128 + 128]
    return ws.reshape(UNITS, 128, 1024)


def kernel(**inputs):
    import concourse.bacc as _bacc
    from concourse.bass_utils import run_bass_kernel_spmd as _run

    nc = _bacc.Bacc("TRN2", target_bir_lowering=False, num_devices=1, dynamic_dma_scratch_size=1024)
    order = _program(nc)
    inp = {k: np.asarray(v) for k, v in inputs.items()}
    arrays = {"in_" + k: v for k, v in _arrays(inp).items()}
    arrays["in_ws"] = _stream(_weights(inp), order)
    r = _run(nc, [arrays], core_ids=[0])
    got = r.results[0]["outT"]
    return np.ascontiguousarray(got.transpose(2, 1, 0).reshape(1, 512, 1024))
```

```python
import math

import numpy as np
import concourse.bass as bass
from concourse import mybir
from contextlib import ExitStack

F32 = mybir.dt.float32
F32R = mybir.dt.float32r
ALU = mybir.AluOpType
ACT = mybir.ActivationFunctionType
AX = mybir.AxisListType

T = 512
NT = 8
DFF_T = 22
RING = 4
UNITS = 234
SBUF = 229344
WHOLE = set(range(16)) | set(range(36, 68))


class Tok:
    __slots__ = ("queue", "signals", "value")

    def __init__(self, queue):
        self.queue, self.signals, self.value = queue, False, None


class Queue:

    def __init__(self, name):
        self.name, self.items, self.sem, self.last = name, [], None, None

    def do(self, fn, *after):
        tok = Tok(self)
        waits = []
        for a in flat(after):
            a.signals = True
            waits.append(a)
        self.items.append((fn, waits, tok))
        self.last = tok
        return tok


class DmaTok(Tok):
    __slots__ = ("dsem",)


def flat(x):
    if x is None:
        return []
    if isinstance(x, Tok):
        return [x]
    out = []
    for y in x:
        out += flat(y)
    return out


class DmaSem:

    def __init__(self, prog, name):
        self.name, self.count, self.sem = name, 0, None
        prog.dsems.append(self)


class Prog:
    def __init__(self):
        self.pe, self.act, self.dve, self.pool, self.sp = (Queue(n) for n in ("pe", "act", "dve", "pool", "sp"))
        self.dsems = []

    def dsem(self, name):
        return DmaSem(self, name)

    def dma(self, queue, out, in_, dsem, *after):
        tok = DmaTok(queue)
        dsem.count += 16
        tok.dsem, tok.value = dsem, dsem.count
        waits = []
        for a in flat(after):
            a.signals = True
            waits.append(a)
        queue.items.append((lambda e: e.dma_start(out, in_), waits, tok))
        return tok

    def number(self):
        for q in (self.pe, self.act, self.dve, self.pool, self.sp):
            n = 0
            for _, _, tok in q.items:
                if not isinstance(tok, DmaTok) and tok.signals:
                    n += 1
                    tok.value = n

    def issue(self, q, eng):
        seen = {}
        for fn, waits, tok in q.items:
            for w in waits:
                sem = w.dsem.sem if isinstance(w, DmaTok) else w.queue.sem
                name = w.dsem.name if isinstance(w, DmaTok) else w.queue.name
                if seen.get(name, 0) < w.value:
                    eng.wait_ge(sem, w.value)
                    seen[name] = w.value
            ins = fn(eng)
            if isinstance(tok, DmaTok):
                ins.then_inc(tok.dsem.sem, 16)
            elif tok.signals:
                ins.then_inc(q.sem, 1)


class Banks:

    def __init__(self, aps):
        self.aps = aps
        self.free = [(i, []) for i in range(len(aps))]

    def take(self):
        i, toks = self.free.pop(0)
        return i, self.aps[i], toks

    def give(self, i, *toks):
        self.free.append((i, flat(toks)))


PCOLS = {}


def _pcols():
    at = 0
    for name, n in [("b_ada", 48), ("mu", 14), ("w0", 4), ("a0", 4), ("k_k", 4), ("k_a", 4), ("r_k", 4),
                    ("lnw", 4), ("lnb", 4), ("s5d", 4), ("bglu", 4), ("gain", 4), ("fgain", 8), ("c", 8),
                    ("are", 16), ("aim", 16), ("ldt", 16),
                    ("ng0", 8), ("ng1", 8), ("qan0", 2), ("qan1", 2), ("kvan0", 1), ("kvan1", 1),
                    ("qn0", 1), ("qn1", 1), ("kn0", 1), ("kn1", 1), ("cw0", 12), ("cw1", 12),
                    ("sqn0", 1), ("sqn1", 1), ("skn0", 1), ("skn1", 1), ("sink0", 8), ("sink1", 8),
                    ("gr0", 64), ("gr1", 64)]:
        PCOLS[name] = (at, n)
        at += n
    return at


NPC = _pcols()
CC = {}


def _ccols():
    at = 0
    for name, n in [("ident", 128), ("ones", 128), ("blk", 128), ("caus", 128), ("scan", 512),
                    ("I64", 64), ("m2L", 64), ("m2U", 64), ("mSU", 64), ("mIU", 64), ("lvl", 320), ("k", 8)]:
        CC[name] = (at, n)
        at += n
    return at


NCC = _ccols()
NC2 = 2176
EPS6, EPSLN, TENLN2, C1E24, HPI = range(5)


def constants():
    c = np.zeros((128, NCC), np.float32)

    def put(name, a):
        s, n = CC[name]
        c[:, s:s + n] = a
    i = np.arange(128)
    put("ident", np.eye(128))
    put("ones", 1.0)
    put("blk", (i[:, None] // 64) == (i[None, :] // 64))
    put("caus", np.where(i[None, :] > i[:, None], -1e30, 0.0))
    put("scan", (np.arange(512) % 64 != 0)[None, :].astype(np.float32))
    a, b = (i % 64)[:, None], np.arange(64)[None, :]
    put("I64", a == b)
    put("m2L", (a // 2 == b // 2) & (a > b))
    put("m2U", (a // 2 == b // 2) & (a < b))
    put("mSU", a < b)
    put("mIU", a <= b)
    lv = [((a // (2 * m)) == (b // (2 * m))) & ((a // m) < (b // m)) for m in (2, 4, 8, 16, 32)]
    put("lvl", np.concatenate(lv, 1))
    put("k", np.array([1e-6, 64e-5, 10 * math.log(2), 1e-24 * 2 ** 20, math.pi / 2, 0, 0, 0])[None, :])
    d = np.zeros((128, NC2), np.float32)
    q, k = i[:, None], np.arange(256)[None, :]
    dist = 128 + q - k
    ok = (dist >= 0) & (dist < 128)
    al = []
    for h in (0, 4, 1, 5, 2, 6, 3, 7):
        slope = np.float32(2.0 ** (-(h + 1)))
        al.append(np.where(ok, -slope * dist.astype(np.float32), np.float32(-1e30)))
    d[:, 0:2048] = np.concatenate(al, 1)
    half = 16
    inv = np.power(np.float32(10000.0), -np.arange(half, dtype=np.float32) / half).astype(np.float32)
    ang = (np.arange(512, dtype=np.float32)[:, None] * inv[None, :]).astype(np.float32)
    by_token = lambda a: a.reshape(4, 128, 16).transpose(1, 0, 2).reshape(128, 64)
    d[:, 2048:2112], d[:, 2112:2176] = by_token(np.cos(ang)), by_token(np.sin(ang))
    return c, d


class Kern:
    def __init__(self, nc, d, out, dumps=None):
        self.nc, self.d, self.out, self.dumps = nc, d, out, dumps or {}
        self.P = Prog()
        self.order = []

    def tt(self, q, out, a, b, op, *after):
        if q is self.P.pool:
            after += (q.last,)
        return q.do(lambda e: e.tensor_tensor(out=out, in0=a, in1=b, op=op), *after)

    def ts(self, q, out, a, s1, op0, s2, op1, *after):
        if q is self.P.pool:
            after += (q.last,)
        if s2 is None:
            return q.do(lambda e: e.tensor_scalar(out=out, in0=a, scalar1=s1, scalar2=None, op0=op0), *after)
        return q.do(lambda e: e.tensor_scalar(out=out, in0=a, scalar1=s1, scalar2=s2, op0=op0, op1=op1), *after)

    def stt(self, out, a, s, b, op0, op1, *after):
        return self.P.dve.do(lambda e: e.scalar_tensor_tensor(out=out, in0=a, scalar=s, in1=b, op0=op0, op1=op1), *after)

    def af(self, out, a, f, *after, bias=None, scale=1.0, acc=None):
        def fn(e):
            kw = {}
            if bias is not None:
                kw["bias"] = bias
            if acc is not None:
                kw["accum_out"] = acc
            return e.activation(out, a, f, scale=scale, **kw)
        return self.P.act.do(fn, *after)

    def cp(self, q, out, a, *after):
        if q is self.P.act:
            return q.do(lambda e: e.activation(out, a, ACT.Copy), *after)
        return q.do(lambda e: e.tensor_copy(out, a), *after)

    def mm(self, out, lhsT, rhs, start, stop, *after):
        return self.P.pe.do(lambda e: e.matmul(out, lhsT, rhs, start=start, stop=stop, skip_group_check=True), *after)

    def tr(self, out, in_, *after):
        idn = self.C("ident")
        return self.P.pe.do(lambda e: e.transpose(out, in_, idn), *after)

    def C(self, name):
        s, n = CC[name]
        return self.cst[:, s:s + n]

    def kc(self, i):
        s, _ = CC["k"]
        return self.cst[:, s + i:s + i + 1]

    def pc(self, name, i=0, n=1):
        s, _ = PCOLS[name]
        return self.par[:, s + i:s + i + n]

    def split_unit(self, u):
        if u in self.wsplit or u in WHOLE or u >= self.units:
            return
        slot, b = u % RING, u % 2
        raw = self.ring[:, slot * 1024:(slot + 1) * 1024]
        hi, lo = self.wpair(b)
        free = self.wlast.get(u - 2)
        t = self.cp(self.P.act, hi, raw, self.wdma[u], free)
        v = self.tt(self.P.dve, lo, raw, hi.bitcast(F32), ALU.subtract, t, free)
        self.wsplit[u] = [t, v]
        if u + RING < self.units:
            self.load_unit(u + RING, v)

    def wpair(self, b):
        return [self.ring2[:, b * 2048 + i * 1024:b * 2048 + i * 1024 + 1024] for i in (0, 1)]

    def wblock(self, key, n=1):
        b = len(self.order)
        self.order += key if n > 1 else [key]
        u, j = divmod(b, 8)
        assert j + n <= 8 and (u in WHOLE) == (self.order[b][0] == "ada")
        if j == 0:
            self.split_unit(u)
            self.split_unit(u + 1)
        c = slice(j * 128, (j + n) * 128)
        if u in WHOLE:
            o = u % RING * 1024
            return self.ring[:, o:o + 1024][:, c], self.wdma[u]
        return [x[:, c] for x in self.wpair(u % 2)], self.wsplit[u]

    def wused(self, tok):
        b = len(self.order)
        if b % 8 == 0:
            u = b // 8 - 1
            self.wlast[u] = tok
            if u in WHOLE and u + RING < self.units:
                self.load_unit(u + RING, tok)

    def load_unit(self, u, *after):
        slot = u % RING
        self.wdma[u] = self.P.dma(self.P.sp, self.ring[:, slot * 1024:(slot + 1) * 1024],
                                  self.d["ws"][u, :, :], self.wsem[slot], *after)

    def mms(self, out, lhsT, rhs, start, stop, *after):
        self.mm(out, lhsT[0], rhs[0], start, False, *after)
        self.mm(out, lhsT[0], rhs[1], False, False)
        return self.mm(out, lhsT[1], rhs[0], False, stop)

    def split(self, hi, lo, src, tok, *after, bias=None, q=None):
        if bias is None:
            t = self.cp(self.P.act, hi, src, tok, *after)
            u = self.tt(q or self.P.dve, lo, src, hi.bitcast(F32), ALU.subtract, t, *after)
        else:
            t = self.af(hi, src, ACT.Identity, tok, *after, bias=bias)
            u = self.stt(lo, src, bias, hi.bitcast(F32), ALU.add, ALU.subtract, t, *after)
        return [t, u]

    def dense(self, keys, rhs, out, *after, each=None):
        n = len(keys)
        for i, (key, r) in enumerate(zip(keys, rhs)):
            w, wt = self.wblock(key)
            f = self.mms if isinstance(w, list) else self.mm
            t = f(out, w, r, i == 0, i == n - 1, wt, *(after if i == 0 else ()), each[i] if each else None)
            self.wused(t)
        return t

    def dump(self, name, ap, *after):
        if name in self.dumps:
            s = self.P.dsem("dump_" + name)
            t = self.P.dma(self.P.sp, self.dumps[name], ap, s, *after)
            self.final.append(t)

    def rsqrt(self, out, src, eps, scale, *after, bias=None):
        t = self.af(out, src, ACT.Ln, *after, bias=eps, scale=scale)
        return self.af(out, out, ACT.Exp, t, scale=-0.5, bias=bias)

    def build(self, stop=None):
        nc, P = self.nc, self.P
        self.final = []
        ctx = ExitStack()
        with ctx:
            self.top = 1184

            def place(name, cols, *also):
                t = [nc.alloc_sbuf_tensor_at(n, [128, cols], dt, offset=self.top)
                     for n, dt in ((name, F32), *((a, F32R) for a in also))]
                self.top += -(-cols * 4 // 32) * 32
                return t if also else t[0]
            self.cst = place("cst", NCC)
            self.par = place("par", NPC)
            self.X = place("X", NT * T).reshape([128, NT, T])
            self.H, self.HR = (x.reshape([128, NT, T]) for x in place("H", NT * T, "HR"))
            self.ring = place("ring", RING * 1024)
            self.ring2 = nc.alloc_sbuf_tensor_at("ring2", [128, 4096], F32R, offset=self.top)
            self.top += 4096 * 4
            self.ada = place("ada", 48)
            self.nst = place("nst", 608)
            self.AF = (SBUF - self.top) // 4 // 8 * 8
            self.base, self.tiles = self.top, {}
            self.ar = place("arena", self.AF)
            banks = [ctx.enter_context(nc.psum_tensor(f"b{i}", [128, 512], F32)) for i in range(8)]
            self.banks = Banks(banks)
            self.units = self.d["ws"].shape[0]
            self.wsem = [P.dsem(f"w{i}") for i in range(RING)]
            self.wdma, self.wsplit, self.wlast = {}, {}, {}
            self.body(stop)
            assert stop or len(self.order) == 8 * self.units, (len(self.order), self.units)
            P.number()
            for q in (P.pe, P.act, P.dve, P.pool, P.sp):
                q.sem = ctx.enter_context(nc.semaphore("s_" + q.name))
            for s in P.dsems:
                s.sem = ctx.enter_context(nc.semaphore("d_" + s.name))
            block = ctx.enter_context(nc.Block())

            @block.sync
            def _(e):
                P.issue(P.sp, e)
                for s in P.dsems:
                    if s.count:
                        e.wait_ge(s.sem, s.count)

            @block.gpsimd
            def _(e):
                P.issue(P.pool, e)

            @block.scalar
            def _(e):
                P.issue(P.act, e)

            @block.vector
            def _(e):
                P.issue(P.dve, e)

            @block.tensor
            def _(e):
                P.issue(P.pe, e)
        return self.order

    def pair(self, kh, kl):
        out = []
        for k in (kh, kl):
            if k not in self.tiles:
                self.tiles[k] = self.nc.alloc_sbuf_tensor_at(f"tile{int(4 * k)}", [128, T], F32R,
                                                             offset=self.base + int(1024 * k))
            out.append(self.tiles[k][:, :])
        return out

    def region(self, kb, *shape):
        n = int(np.prod(shape))
        s = int(kb * 256)
        assert s + n <= self.AF, (kb, shape, self.AF)
        a = self.ar[:, s:s + n]
        if len(shape) == 1:
            return a
        names = "abcdef"[:len(shape)]
        return a.rearrange(f"p ({' '.join(names)}) -> p {' '.join(names)}", **{x: y for x, y in zip(names[1:], shape[1:])})

    def run(self, *gens):
        gens = [[g, w, 0] for g, w in gens]
        while gens:
            for x in list(gens):
                for _ in range(x[1]):
                    try:
                        next(x[0])
                    except StopIteration:
                        gens.remove(x)
                        break

    def body(self, stop):
        P = self.P
        sp = P.sp
        s0 = P.dsem("in0")
        t_par = P.dma(sp, self.par[:, :], self.d["par"], s0)
        t_cst = P.dma(sp, self.cst[:, :], self.d["cst"], s0)
        self.t_in = t_cst
        s1 = P.dsem("in1")
        self.t_x = P.dma(sp, self.X[:, :, :], self.d["xT"], s1)
        for u in range(RING):
            self.load_unit(u)
        self.block1(stop)
        if stop and stop.startswith("b1"):
            return
        self.layers(stop)

    def ada_tiles(self, a, b):
        i, ps, fr = self.banks.take()
        for n in range(a, b):
            rhs = [self.cact[:, k:k + 1] for k in range(8)]
            t = self.dense([("ada", n, k) for k in range(8)], rhs, ps[:, n - a:n - a + 1], self.t_cact, fr)
            fr = ()
            yield
        t = self.tt(self.P.dve, self.ada[:, a:b], ps[:, 0:b - a], self.pc("b_ada", a, b - a), ALU.add, t)
        self.banks.give(i, t)
        self.t_ada = t

    def norm_stats(self, tmp, *after):
        i, ps, fr = self.banks.take()
        return {"bank": (i, ps, fr), "tmp": tmp, "after": flat(after), "mm": []}

    def norm_tile(self, st, src, tok):
        i, ps, fr = st["bank"]
        k = len(st["mm"])
        sq = st["tmp"][:, k % 2, :]
        w = st["mm"][k - 2] if k >= 2 else st["after"]
        if k % 2:
            t = self.af(sq, src, ACT.Square, tok, w)
        else:
            t = self.tt(self.P.pool, sq, src, src, ALU.mult, tok, w)
        for q in range(4):
            m = self.mm(ps[:, q:q + 1], sq[:, q * 128:q * 128 + 128], self.C("ones")[:, 0:1], k == 0 and q == 0, True,
                        t, fr)
        st["mm"].append(m)

    def norm_apply(self, st, src, dst, gain, shift=None, after=None):
        P = self.P
        i, ps, _ = st["bank"]
        r, D = self.nst[:, 0:4], self.nst[:, 8:520].rearrange("p (q t) -> p q t", q=4)
        t = self.ts(P.dve, r, ps[:, 0:4], 1.0 / (128 * len(src)), ALU.mult, 1e-6, ALU.add, st["mm"][-1])
        self.banks.give(i, t)
        t = self.af(r, r, ACT.Sqrt, t)
        t = P.dve.do(lambda e: e.reciprocal(r, r), t)
        t = self.tt(P.dve, D, self.C("ident").unsqueeze(1).broadcast_to((128, 4, 128)),
                    r.unsqueeze(2).broadcast_to((128, 4, 128)), ALU.mult, t)
        i, ps, fr = self.banks.take()
        for q in range(4):
            m = self.mm(ps[:, q * 128:q * 128 + 128], self.C("ones"), D[:, q, :], q == 0, True, t, fr)
        outs = []
        for k in range(len(src)):
            if not isinstance(dst[k], list):
                outs.append(self.stt(dst[k], src[k], gain[k], ps[:, :], ALU.mult, ALU.mult, m, after))
                continue
            x = st["tmp"][:, k % 2, :]
            u = self.stt(x, src[k], gain[k], ps[:, :], ALU.mult, ALU.mult, m, after, outs[k - 2] if k >= 2 else None)
            outs.append(self.split(*dst[k], x, u, after, bias=shift[k] if shift else None,
                                   q=P.pool if k % 2 and not shift else None))
        self.banks.give(i, P.dve.last)
        return outs

    def block1(self, stop):
        P = self.P
        dve, act, pool, sp = P.dve, P.act, P.pool, P.sp
        R = self.region
        self.cact = self.nst[:, 528:536]
        t = self.af(self.cact, self.pc("c", 0, 8), ACT.Silu, self.t_in)
        self.t_cact = t
        s = P.dsem("s5w")
        self.s5p = R(124, 4, 256)
        self.t_s5p = P.dma(sp, self.s5p, self.d["s5p"], s)
        self.run((self.ada_tiles(0, 16), 1), (self.s5_tables(), 3))
        t_ada = self.t_ada
        one_sc = self.nst[:, 536:544]
        t1 = self.ts(dve, one_sc, self.ada[:, 8:16], 1.0, ALU.add, None, None, t_ada)
        X = [self.X[:, k, :] for k in range(8)]
        Hs = self.Hs = [[self.HR[:, k, :], self.pair(0, 132.25 + 2 * k)[1]] for k in range(8)]
        st = self.norm_stats(R(126, 2, 512), self.t_tab)
        for k in range(8):
            self.norm_tile(st, X[k], self.t_x)
        t_h = self.norm_apply(st, X, Hs, [one_sc[:, k:k + 1] for k in range(8)], [self.ada[:, k:k + 1] for k in range(8)], after=self.t_tab)
        self.dump("h", self.H[:, :, :], t_h)
        if stop == "b1h":
            return
        U = R(110, 4, 8, 64)
        self.U = U
        self.t_u = []
        for n in range(4):
            i, ps, fr = self.banks.take()
            t = self.dense([("in", 14 + n, k) for k in range(8)], Hs, ps[:, :], self.t_tab, fr, each=t_h)
            t = self.cp(dve, U[:, n, :, :], ps[:, :].rearrange("p (j t) -> p t j", t=8), t)
            self.banks.give(i, t)
            self.t_u.append(t)
        self.dump("u", R(110, 2048), self.t_u)
        self.run((self.in_proj(Hs), 1), (self.s5_apply(), 4))
        self.dump("zs", R(0, 14 * 512), self.t_z)
        self.dump("ys5", R(28, 2048), self.t_os)
        if stop == "b1s5":
            return
        self.run((self.rwkv(stop), 2), (self.ada_tiles(16, 48), 1))
        self.dump("yr", self.region(0, 2048), self.t_yr)
        if stop == "b1rw":
            return
        ys = self.ysp
        each = self.t_ysp
        t_x1 = []
        st = self.norm_stats(R(120, 2, 512), self.t_yr)
        for n in range(8):
            i, ps, fr = self.banks.take()
            t = self.dense([("out", n, k) for k in range(8)], ys, ps[:, :], fr, each=each)
            t = self.stt(X[n], ps[:, :], self.ada[:, 16 + n:17 + n], X[n], ALU.mult, ALU.add, t, self.t_ada, self.t_x)
            self.banks.give(i, t)
            t_x1.append(t)
            if n:
                self.norm_tile(st, X[n - 1], t_x1[n - 1])
        self.dump("x1", self.X[:, :, :], t_x1)
        if stop == "b1x":
            return
        one_sc = self.nst[:, 536:544]
        t1 = self.ts(dve, one_sc, self.ada[:, 32:40], 1.0, ALU.add, None, None, self.t_ada, t_x1)
        self.norm_tile(st, X[7], t_x1[7])
        t_h = self.norm_apply(st, X, Hs, [one_sc[:, k:k + 1] for k in range(8)],
                              [self.ada[:, 24 + k:25 + k] for k in range(8)])
        at = [2 * i for i in range(12)] + [33 + 2 * i for i in range(38)]
        G = [self.pair(at[2 * n], at[2 * n + 1]) for n in range(DFF_T)]
        SB, GT = [R(97 + 2 * j, 512) for j in (0, 1)], [R(101 + 2 * j, 512) for j in (0, 1)]
        t_g, t_raw = [], []
        for n in range(DFF_T):
            i, ps, fr = self.banks.take()
            t = self.dense([("gate", n, k) for k in range(8)], Hs, ps[:, :], fr, each=t_h)
            ta = self.af(SB[n % 2], ps[:, :], ACT.Silu, t, t_raw[n - 2] if n >= 2 else t_x1)
            self.banks.give(i, ta)
            i, ps, fr = self.banks.take()
            t = self.dense([("up", n, k) for k in range(8)], Hs, ps[:, :], fr)
            t = self.tt(dve, GT[n % 2], ps[:, :], SB[n % 2], ALU.mult, t, ta, t_g[n - 2] if n >= 2 else t_x1)
            self.banks.give(i, t)
            t_raw.append(t)
            t_g.append(self.split(*G[n], GT[n % 2], t, t_x1, q=pool))
        self.load_lw(t)
        t_x2 = []
        st = self.norm_stats(R(120, 2, 512))
        for n in range(8):
            i, ps, fr = self.banks.take()
            t = self.dense([("down", n, k) for k in range(DFF_T)], G, ps[:, :], fr, each=t_g)
            t = self.stt(X[n], ps[:, :], self.ada[:, 40 + n:41 + n], X[n], ALU.mult, ALU.add, t)
            self.banks.give(i, t)
            t_x2.append(t)
            if n:
                self.norm_tile(st, X[n - 1], t_x2[n - 1])
        self.norm_tile(st, X[7], t_x2[7])
        self.load_layer_tables(t)
        self.t_X = self.norm_apply(st, X, X, [self.pc("fgain", k) for k in range(8)])
        self.dump("x2", self.X[:, :, :], self.t_X)

    def s5_tables(self):
        P = self.P
        dve, act, pool, sp = P.dve, P.act, P.pool, P.sp
        R = self.region
        V = lambda out, a, b, op, *w: self.tt(dve, out, a, b, op, *w)
        S = lambda out, a, s1, o1, s2, o2, *w: self.ts(dve, out, a, s1, o1, s2, o2, *w)
        sm = R(141, 24, 16)
        dt, xr, mag, xi, kf, r, sn, cs, den, pr_, cr, ci, t1, t2, t3, t4, cc, sg = (sm[:, i, :] for i in range(18))
        PR, PI = R(28, 16, 9), R(29, 16, 9)
        are, aim, ldt = self.pc("are", 0, 16), self.pc("aim", 0, 16), self.pc("ldt", 0, 16)
        a = self.af(dt, ldt, ACT.Exp, self.t_in)
        a = V(xr, dt, are, ALU.mult, a)
        b = V(xi, dt, aim, ALU.mult)
        a = self.af(mag, xr, ACT.Exp, a)
        M = 12582912.0
        b = S(kf, xi, 1.0 / (2 * math.pi), ALU.mult, M, ALU.add, b)
        b = S(kf, kf, -M, ALU.add, None, None, b)
        c1 = 6.28125
        c2 = float(np.float32(np.round((2 * math.pi - c1) * 2 ** 22) / 2 ** 22))
        c3 = float(np.float32(2 * math.pi - c1 - c2))
        b = self.stt(r, kf, -c1, xi, ALU.mult, ALU.add, b)
        b = self.stt(r, kf, -c2, r, ALU.mult, ALU.add, b)
        b = self.stt(r, kf, -c3, r, ALU.mult, ALU.add, b)
        PIF = 3.14159250
        c = S(cc, r, math.pi / 2, ALU.add, None, None, b)
        d_ = S(t1, cc, math.pi, ALU.is_gt, -2 * math.pi, ALU.mult, c)
        c = V(cc, cc, t1, ALU.add, d_)
        c = S(cc, cc, PIF, ALU.min, -PIF, ALU.max, c)
        b = S(r, r, PIF, ALU.min, -PIF, ALU.max, b)
        yield
        b = self.af(sn, r, ACT.Sin, b)
        c = self.af(cs, cc, ACT.Sin, c)
        c = V(PR[:, :, 1], mag, cs, ALU.mult, c, a)
        b = V(PI[:, :, 1], mag, sn, ALU.mult, b)
        b = dve.do(lambda e: e.memset(PR[:, :, 0], 1.0))
        b = dve.do(lambda e: e.memset(PI[:, :, 0], 0.0))
        yield
        t = V(t1, are, are, ALU.mult)
        u = V(t2, aim, aim, ALU.mult)
        t = V(den, t1, t2, ALU.add, t, u)
        t = dve.do(lambda e: e.reciprocal(den, den), t)
        w = S(pr_, PR[:, :, 1], -1.0, ALU.add, None, None, c)
        x1 = V(t1, pr_, are, ALU.mult, w)
        x2 = V(t2, PI[:, :, 1], aim, ALU.mult, b)
        x3 = V(t3, PI[:, :, 1], are, ALU.mult)
        x4 = V(t4, pr_, aim, ALU.mult)
        x1 = V(t1, t1, t2, ALU.add, x1, x2)
        x3 = V(t3, t3, t4, ALU.subtract, x3, x4)
        x1 = V(cr, t1, den, ALU.mult, x1, t)
        x3 = V(ci, t3, den, ALU.mult, x3)
        yield
        def bc(ap, n):
            return ap.unsqueeze(2).broadcast_to((128, 16, n))

        q1, q2 = sm[:, 20, :], sm[:, 21, :]
        tm = R(30, 4, 16, 4)
        last = x3
        for lo, n in ((1, 1), (2, 2), (4, 4)):
            ar_, ai_ = bc(PR[:, :, lo], n), bc(PI[:, :, lo], n)
            br_, bi_ = PR[:, :, 1:1 + n], PI[:, :, 1:1 + n]
            y = [V(tm[:, i, :, 0:n], p, q_, ALU.mult, last)
                 for i, (p, q_) in enumerate(((br_, ar_), (bi_, ai_), (br_, ai_), (bi_, ar_)))]
            y1 = V(PR[:, :, lo + 1:lo + 1 + n], tm[:, 0, :, 0:n], tm[:, 1, :, 0:n], ALU.subtract, y)
            last = V(PI[:, :, lo + 1:lo + 1 + n], tm[:, 2, :, 0:n], tm[:, 3, :, 0:n], ALU.add, y1)
            yield
        P8R, P8I = R(33.5, 8, 16), R(34, 8, 16)
        self.P8R, self.P8I = P8R, P8I
        t = self.cp(dve, P8R[:, 0, :], PR[:, :, 8], last)
        t = self.cp(dve, P8I[:, 0, :], PI[:, :, 8], t)
        tm2 = R(31, 4, 4, 16)
        for lo, n in ((1, 1), (2, 2), (4, 4)):
            def bb(ap):
                return ap.unsqueeze(1).broadcast_to((128, n, 16))
            ar_, ai_ = bb(P8R[:, lo - 1, :]), bb(P8I[:, lo - 1, :])
            br_, bi_ = P8R[:, 0:n, :], P8I[:, 0:n, :]
            y = [V(tm2[:, i, 0:n, :], p, q_, ALU.mult, t)
                 for i, (p, q_) in enumerate(((br_, ar_), (bi_, ai_), (br_, ai_), (bi_, ar_)))]
            y1 = V(P8R[:, lo:lo + n, :], tm2[:, 0, 0:n, :], tm2[:, 1, 0:n, :], ALU.subtract, y)
            t = V(P8I[:, lo:lo + n, :], tm2[:, 2, 0:n, :], tm2[:, 3, 0:n, :], ALU.add, y1)
            yield
        t_p8 = t
        BB = R(16, 2, 16, 16)
        self.BB = BB
        bt = R(18, 2, 16, 16)
        bre, bim, cre, cim = (self.s5p[:, i, :].rearrange("p (g c) -> p g c", g=16) for i in range(4))
        crb, cib = bc(cr, 16), bc(ci, 16)
        y1 = V(bt[:, 0], crb, bre, ALU.mult, x1, x3, self.t_s5p)
        y2 = V(bt[:, 1], cib, bim, ALU.mult)
        y = V(BB[:, 0], bt[:, 0], bt[:, 1], ALU.subtract, y1, y2)
        y1 = V(bt[:, 0], crb, bim, ALU.mult, y)
        y2 = V(bt[:, 1], cib, bre, ALU.mult)
        t_bb = V(BB[:, 1], bt[:, 0], bt[:, 1], ALU.add, y1, y2)
        yield
        W = R(76, 2, 16, 9, 16)
        self.W = W
        wt = R(36, 2, 16, 9, 16)

        def b4(ap, n):
            return ap.unsqueeze(3).broadcast_to((128, 16, n, 16))

        def c4(ap, n):
            return ap.unsqueeze(2).broadcast_to((128, 16, n, 16))
        VT = R(0, 2, 16, 8, 16)
        vt = R(62, 16, 8, 16)
        t = None
        tws = []
        for ri in range(2):
            (pa, ca), (pb_, cb) = (((PR, cre), (PI, cim)) if ri == 0 else ((PI, cre), (PR, cim)))
            for g in range(0, 16, 4):
                gs = slice(g, g + 4)
                w1 = V(wt[:, 0, gs], pa[:, gs].unsqueeze(3).broadcast_to((128, 4, 9, 16)),
                       ca[:, gs].unsqueeze(2).broadcast_to((128, 4, 9, 16)), ALU.mult, last, t)
                w2 = V(wt[:, 1, gs], pb_[:, gs].unsqueeze(3).broadcast_to((128, 4, 9, 16)),
                       cb[:, gs].unsqueeze(2).broadcast_to((128, 4, 9, 16)), ALU.mult, t)
                if ri == 0:
                    t = V(W[:, 0, gs], wt[:, 0, gs], wt[:, 1, gs], ALU.subtract, w1, w2)
                else:
                    t = self.stt(W[:, 1, gs].rearrange("p g d c -> p (g d c)"),
                                 wt[:, 0, gs].rearrange("p g d c -> p (g d c)"), -1.0,
                                 wt[:, 1, gs].rearrange("p g d c -> p (g d c)"), ALU.mult, ALU.subtract, w1, w2)
                tws.append(t)
                yield
        self.t_w = tws
        tv = {}
        t = t_bb
        for ri in range(2):
            br_, bi_ = BB[:, 0], BB[:, 1]
            (pa, ca), (pb_, cb) = (((PR, br_), (PI, bi_)) if ri == 0 else ((PR, bi_), (PI, br_)))
            for g in range(0, 16, 4):
                gs = slice(g, g + 4)
                w1 = V(VT[:, ri, gs], pa[:, gs, 0:8].unsqueeze(3).broadcast_to((128, 4, 8, 16)),
                       ca[:, gs].unsqueeze(2).broadcast_to((128, 4, 8, 16)), ALU.mult, t)
                w2 = V(vt[:, gs], pb_[:, gs, 0:8].unsqueeze(3).broadcast_to((128, 4, 8, 16)),
                       cb[:, gs].unsqueeze(2).broadcast_to((128, 4, 8, 16)), ALU.mult, t)
                t = V(VT[:, ri, gs], VT[:, ri, gs], vt[:, gs], ALU.subtract if ri == 0 else ALU.add, w1, w2)
                tv[ri, g] = t
                yield
        KS = R(94, 32, 240)
        t_z = pool.do(lambda e: e.memset(KS[0:16, :, 0:112], 0.0))
        t_ks = []
        for g4 in range(8):
            i, ps, fr = self.banks.take()
            for gp in range(4 * (g4 // 2), 4 * (g4 // 2) + 4):
                par = 64 * (g4 % 2)
                o = ps[0:16, (gp % 4) * 128:(gp % 4) * 128 + 128]
                for ri in range(2):
                    t = self.mm(o, BB[par:par + 64, ri, gp, :],
                                W[par:par + 64, ri, gp, 0:8, :].rearrange("p d c -> p (d c)"),
                                ri == 0, ri == 1, t_bb, tws, fr)
            g0 = 8 * (g4 // 2) + g4 % 2
            t = self.cp(act, KS[0:16, g0:g0 + 7:2, 112:240], ps[0:16, :].rearrange("p (g d) -> p g d", g=4), t)
            self.banks.give(i, t)
            t_ks.append(t)
            yield
        kd = self.d["kpad"]
        sk = P.dsem("kpad")
        t = P.dma(sp, kd.rearrange("g c n -> c g n"), KS[0:16, :, :], sk, t_ks, t_z)
        TT = R(44, 32, 128)
        self.TT = TT
        st = P.dsem("tt")
        for dl in range(8):
            t_tt = P.dma(sp, TT[16 * dl:16 * dl + 16, :, :],
                         kd[:, :, 16 * dl:16 * dl + 128].rearrange("g c n -> c g n"), st, t, tws[-1], tv[1, 12])
        self.t_tt = t_tt
        VM = R(60, 16, 2, 128)
        self.VM = VM
        t_vm = []
        for g in range(0, 16, 2):
            i, ps, fr = self.banks.take()
            for gg in (g, g + 1):
                for ri in range(2):
                    o = ((gg - g) * 2 + ri) * 128
                    t = self.tr(ps[:, o:o + 128], VT[:, ri, gg].rearrange("p d c -> p (d c)"), tv[1, 12], fr)
            t = self.cp(act if g % 4 else dve, VM[:, g:g + 2].rearrange("p a b c -> p (a b c)"), ps[:, :], t)
            self.banks.give(i, t)
            t_vm.append(t)
            yield
        self.t_vm = t_vm
        self.t_tab = [t_vm, t_p8, t_tt, t_ks]
        self.t_tab_mm = t_vm[-1]

    def in_proj(self, Hs):
        P = self.P
        ZB = self.region(0, 14, 512)
        self.ZB = ZB
        TMP = self.region(126, 2, 516)
        omm = self.nst[:, 544:558]
        t_o = self.ts(P.dve, omm, self.pc("mu", 0, 14), -1.0, ALU.mult, 1.0, ALU.add, self.t_tab, self.t_u)
        z = [P.pool.do(lambda e, j=j: e.memset(TMP[:, j, 0:1], 0.0), self.t_tab, self.t_u) for j in range(2)]
        self.t_z = []
        for m, n in enumerate([12, 13, 4, 5, 6, 7, 0, 1, 2, 3, 8, 9, 10, 11]):
            i, ps, fr = self.banks.take()
            t = self.dense([("in", n, k) for k in range(8)], Hs, ps[:, :], fr)
            tmp = TMP[:, m % 2, :]
            ta = self.af(tmp[:, 1:513], ps[:, :], ACT.Copy, t, self.t_z[m - 2] if m >= 2 else z,
                         scale=self.pc("mu", n))
            tb = self.stt(ZB[:, n, :], ps[:, :], omm[:, n:n + 1], tmp[:, 0:512], ALU.mult, ALU.add, ta, t_o, z)
            self.banks.give(i, tb)
            self.t_z.append(tb)
            yield
        self.t_hfree = t

    def s5_apply(self):
        P = self.P
        dve, act, pool, sp = P.dve, P.act, P.pool, P.sp
        R = self.region
        U, TT, VM, W = self.U, self.TT, self.VM, self.W
        UG = R(36, 32, 64)
        ud = self.d["ud"]
        s = P.dsem("ud")
        t = P.dma(sp, ud.rearrange("(gt g) c t j -> (g c) gt (t j)", gt=4),
                  U.rearrange("p a t j -> p a (t j)"), s, self.t_u)
        s = P.dsem("ug")
        for dl in range(8):
            t_ug = P.dma(sp, UG[16 * dl:16 * dl + 16, :, :], ud[:, :, 7 - dl, :].rearrange("g c j -> c g j"),
                         s, t, self.t_w, self.t_tab)
        yield
        S = R(94, 2, 16, 64)
        t_e = []
        for ri in range(2):
            for h in range(2):
                i, ps, fr = self.banks.take()
                for g in range(16 * h, 16 * h + 16):
                    gp, par = g // 2, 64 * (g % 2)
                    t = self.mm(ps[par:par + 64, (gp - 8 * h) * 64:(gp - 8 * h) * 64 + 64],
                                VM[:, gp, ri, par:par + 64], UG[:, g, :], True, True, t_ug, self.t_vm, fr)
                t = self.cp(act, S[:, ri, 8 * h:8 * h + 8, :].rearrange("p a j -> p (a j)"), ps[:, :], t)
                self.banks.give(i, t)
                t_e.append(t)
                yield
        Sv = S.rearrange("p r g (b i) -> p r g b i", i=8)
        T1, T2 = R(102, 2, 16, 8), R(103, 2, 16, 8)
        P8R, P8I = self.P8R, self.P8I
        V = lambda out, a, b, op, *w: self.tt(dve, out, a, b, op, *w)

        def cstep(dst, src, wr, wi, T1, T2, *w):
            a = V(T1[:, 0], src[:, 0], wr, ALU.mult, *w)
            a = V(T1[:, 1], src[:, 1], wr, ALU.mult)
            b = V(T2[:, 0], src[:, 1], wi, ALU.mult)
            c = V(T2[:, 1], src[:, 0], wi, ALU.mult)
            a = V(dst[:, 0], dst[:, 0], T1[:, 0], ALU.add, a)
            b = V(dst[:, 1], dst[:, 1], T1[:, 1], ALU.add)
            a = V(dst[:, 0], dst[:, 0], T2[:, 0], ALU.subtract, a, c)
            b = V(dst[:, 1], dst[:, 1], T2[:, 1], ALU.add, b)
            return b
        t = t_e
        w8r = P8R[:, 0, :].unsqueeze(2).broadcast_to((128, 16, 8))
        w8i = P8I[:, 0, :].unsqueeze(2).broadcast_to((128, 16, 8))
        for k in range(1, 8):
            t = cstep(Sv[:, :, :, :, k], Sv[:, :, :, :, k - 1], w8r, w8i, T1, T2, t)
            yield
        for b in range(1, 8):
            t = cstep(Sv[:, :, :, b, 7], Sv[:, :, :, b - 1, 7], P8R[:, 7, :], P8I[:, 7, :],
                      T1[:, :, :, 0], T2[:, :, :, 0], t)
        yield
        for k in range(7):
            wr = P8R[:, k, :].unsqueeze(2).broadcast_to((128, 16, 7))
            wi = P8I[:, k, :].unsqueeze(2).broadcast_to((128, 16, 7))
            X1, X2 = R(102, 2, 16, 7), R(103, 2, 16, 7)
            t = cstep(Sv[:, :, :, 1:8, k], Sv[:, :, :, 0:7, 7], wr, wi, X1, X2, t)
            yield
        t_s = t
        YG = UG
        t_yg = []
        for q in range(4):
            i, ps, fr = self.banks.take()
            for gp in range(8 * (q // 2), 8 * (q // 2) + 8):
                g, par = 2 * gp + q % 2, 64 * (q % 2)
                o = (gp % 8) * 64
                self.mm(ps[:, o:o + 64], TT[:, g, :], UG[:, g, :], True, False, self.t_tt, t_ug, fr)
                for ri in range(2):
                    t = self.mm(ps[:, o + 1:o + 64], W[par:par + 64, ri, gp, 1:9, :].rearrange("p d c -> p (d c)"),
                                S[par:par + 64, ri, gp, 0:63], False, ri == 1, t_s)
            g0 = 16 * (q // 2) + q % 2
            t = self.cp(act, YG[:, g0:g0 + 15:2, :], ps[:, :].rearrange("p (g j) -> p g j", g=8), t)
            self.banks.give(i, t)
            t_yg.append(t)
            yield
        yd = self.d["yd"]
        s = P.dsem("yd")
        for tau in range(8):
            t = P.dma(sp, yd[:, :, tau, :].rearrange("g c j -> c g j"), YG[16 * tau:16 * tau + 16, :, :], s, t_yg)
        YS = R(118, 4, 512)
        s = P.dsem("ys")
        t_ys = P.dma(sp, YS, yd.rearrange("(gt g) c t j -> (g c) gt (t j)", gt=4), s, t)
        yield
        Z = R(44, 4, 512)
        t_z = []
        for n in range(4):
            t = self.stt(YS[:, n, :], U[:, n].rearrange("p t j -> p (t j)"), self.pc("s5d", n), YS[:, n, :],
                         ALU.mult, ALU.add, t_ys)
            t = self.af(Z[:, n, :], YS[:, n, :], ACT.Gelu_apprx_tanh, t, t_yg)
            t_z.append(t)
        ZP = [self.pair(60 + 2 * n, 68 + 2 * n) for n in range(4)]
        t_zp = [self.split(*ZP[n], Z[:, n, :], t_z[n], t_yg) for n in range(4)]
        yield
        OZ = R(52, 4, 512)
        t_oz = []
        for n in range(4):
            i, ps, fr = self.banks.take()
            t = self.dense([("glu", n, k) for k in range(4)], ZP, ps[:, :], fr, each=t_zp)
            t = self.af(YS[:, n, :], ps[:, :], ACT.Sigmoid, t, bias=self.pc("bglu", n))
            self.banks.give(i, t)
            t = self.tt(dve, OZ[:, n, :], Z[:, n, :], YS[:, n, :], ALU.mult, t)
            t_oz.append(t)
            yield
        self.small = R(118, 2, 512)
        s = P.dsem("small")
        self.t_small = P.dma(sp, self.small, self.d["small"], s, t_oz)
        OS = R(28, 4, 512)
        dst = [OS[:, n, :].rearrange("p (j t) -> p t j", t=8) for n in range(4)]
        tmp = R(104, 3, 512)
        t_r = self.norm_r([OZ[:, n, :] for n in range(4)], t_oz, 512, tmp)
        rr = tmp[:, 2, :].rearrange("p (t j) -> p t j", t=8)
        self.t_os = [self.stt(dst[n], OZ[:, n, :].rearrange("p (t j) -> p t j", t=8), self.pc("gain", n), rr,
                              ALU.mult, ALU.mult, t_r) for n in range(4)]

    def norm_r(self, src, t_src, feats, tmp, tmp_free=()):
        P = self.P
        i, ps, fr = self.banks.take()
        mms = []
        n = len(src)
        for k in range(n):
            sq = tmp[:, k % 2, :]
            w = mms[k - 2] if k >= 2 else tmp_free
            t = self.tt(P.pool, sq, src[k], src[k], ALU.mult, t_src[k], w)
            mms.append(self.mm(ps[:, :], self.C("ones"), sq, k == 0, k == n - 1, t, fr if k == 0 else ()))
        t = self.rsqrt(tmp[:, 2, :], ps[:, :], self.kc(EPS6), 1.0 / feats, mms[-1], tmp_free)
        self.banks.give(i, t)
        return t

    def rwkv(self, stop):
        P = self.P
        dve, act, pool = P.dve, P.act, P.pool
        R = self.region
        ZB = self.ZB
        CE = math.exp(-0.5)
        V = lambda out, a, b, op, *w: self.tt(dve, out, a, b, op, *w)
        G = lambda out, a, b, op, *w: self.tt(pool, out, a, b, op, *w)
        tz, to, hf = self.t_z, self.t_os, self.t_hfree
        SG, AS = self.H[:, 0:4, :], self.H[:, 4:8, :]
        w2, g2 = self.small[:, 0, :], self.small[:, 1, :]
        t = self.af(ZB[0:64, 12, :], ZB[0:64, 12, :], ACT.Tanh, tz)
        t_gl = self.af(ZB[:, 13, :], ZB[:, 13, :], ACT.Sigmoid, tz)
        t_sg, t_as = [], []
        for n in range(4):
            i, ps, fr = self.banks.take()
            m = self.mm(ps[:, :], w2[0:64, n * 128:n * 128 + 128], ZB[0:64, 12, :], True, True, t, fr, self.t_small)
            x = self.af(SG[:, n, :], ps[:, :], ACT.Sigmoid, m, hf, bias=self.pc("w0", n))
            self.banks.give(i, x)
            t_sg.append(x)
            i, ps, fr = self.banks.take()
            m = self.mm(ps[:, :], w2[64:128, n * 128:n * 128 + 128], ZB[64:128, 12, :], True, True, fr)
            x = self.af(AS[:, n, :], ps[:, :], ACT.Sigmoid, m, hf, bias=self.pc("a0", n))
            self.banks.give(i, x)
            t_as.append(x)
            yield
        omk = self.nst[:, 560:564]
        t_omk = self.ts(dve, omk, self.pc("k_a", 0, 4), -1.0, ALU.mult, 1.0, ALU.add, to)
        AR = R(36, 4, 8, 2, 64)
        B = R(52, 4, 512)
        GC = self.nst[:, 572:604].rearrange("p (n c) -> p n c", n=4)
        E = R(68, 8, 512)
        t_ar, t_b, t_k, t_bv = [], [], [], []
        last_e = [to, None]
        RK, KK = [ZB[:, n, :] for n in range(4)], [ZB[:, 4 + n, :] for n in range(4)]
        VV = [ZB[:, 8 + n, :] for n in range(4)]
        v8 = lambda ap: ap.rearrange("p (c t) -> p c t", t=64)
        for n in range(4):
            o = 0
            cs, gam, ig, gp, x, y, z_, q = (R(68 + 16 * (n % 2), 8, 512)[:, i, :] for i in range(8))
            le = last_e[n % 2] if n >= 2 else to
            t = dve.do(lambda e, cs=cs, n=n: e.tensor_tensor_scan(out=cs, data0=self.C("scan"), data1=SG[:, n, :],
                       initial=0.0, op0=ALU.mult, op1=ALU.add), t_sg[n], le)
            tg = self.af(gam, cs, ACT.Exp, t, le, scale=-CE)
            ti = self.af(ig, cs, ACT.Exp, t, scale=CE)
            tp = G(gp, cs, SG[:, n, :], ALU.subtract, t, t_sg[n], le)
            tp = self.af(gp, gp, ACT.Exp, tp, scale=-CE)
            t_gc = self.cp(dve, GC[:, n, :], v8(gam)[:, :, 63], tg, to)
            t1 = self.ts(pool, x, KK[n], self.pc("k_k", n), ALU.mult, None, None, tz, le)
            t2 = G(y, x, x, ALU.mult, t1)
            i, ps, fr = self.banks.take()
            m = self.mm(ps[:, :], self.C("blk"), y, True, True, t2, fr)
            c = self.ts(dve, z_, ps[:, :], 2.0 ** 20, ALU.mult, 1e-24 * 2 ** 20, ALU.max, m, le)
            self.banks.give(i, c)
            c = self.af(z_, z_, ACT.Ln, c)
            c = self.af(z_, z_, ACT.Exp, c, scale=-0.5, bias=self.kc(TENLN2))
            tkk = V(x, x, z_, ALU.mult, c, t1)
            ta = self.stt(AR[:, n, :, 0, :], v8(x), -1.0, v8(gp), ALU.mult, ALU.mult, tkk, tp)
            tb = G(y, x, AS[:, n, :], ALU.mult, tkk, m, t_as[n])
            tb = V(B[:, n, :], y, ig, ALU.mult, tb, ti)
            yield
            t3 = self.ts(pool, q, AS[:, n, :], self.pc("k_a", n), ALU.mult, omk[:, n:n + 1], ALU.add, t_as[n], t_omk, le)
            t3 = G(KK[n], KK[n], q, ALU.mult, t3, t1)
            t4 = self.stt(q, RK[n], self.pc("r_k", n), KK[n], ALU.mult, ALU.mult, t3)
            i, ps, fr = self.banks.take()
            m = self.mm(ps[:, :], self.C("blk"), q, True, True, t4, fr)
            t5 = V(z_, VV[n], ps[:, :], ALU.mult, m, tkk)
            self.banks.give(i, t5)
            BVn = self.H[:, n, :]
            t6 = self.cp(pool, BVn, z_, t5, t, tp)
            tr_ = V(AR[:, n, :, 1, :], v8(RK[n]), v8(gam), ALU.mult, tg, t4)
            tk = G(KK[n], KK[n], ig, ALU.mult, t4, ti)
            t_ar += [ta, tr_]
            t_b.append(tb)
            t_k.append(tk)
            t_bv.append(t6)
            last_e[n % 2] = [t6, tk, tr_, tb, ta, t_gc, m]
            yield
        ew = [t_ar, t_b, t_k, t_bv, last_e]
        self.dump("ar", R(36, 4096), ew)
        M, LT, LL, PP, MT, KA, BR, KR = (R(x, 4, 512) for x in (68, 76, 84, 92, 100, 108, 132.25, 140.25))
        mk = lambda name: self.C(name).unsqueeze(1).broadcast_to((128, 8, 64))
        h8 = lambda ap: ap.rearrange("p (h t) -> p h t", t=64)
        tM, tMT, tLT, tKA, tBR, tKR = {}, {}, {}, {}, {}, {}
        for pp in range(2):
            for hp in (0, 64):
                i, ps, fr = self.banks.take()
                for p in range(2 * pp, 2 * pp + 2):
                    for n in range(4):
                        for par in range(2):
                            c, o = 2 * p + par, (p % 2) * 256 + n * 64
                            t = self.mm(ps[64 * par:64 * par + 64, o:o + 64], AR[hp:hp + 64, n, c, 0, :],
                                        B[hp:hp + 64, n, c * 64:c * 64 + 64], True, True, ew, fr)
                dst = M[:, 2 * pp:2 * pp + 2, :].rearrange("p q (n a t) -> p q n a t", a=2, t=64)[:, :, :, hp // 64, :]
                m4 = lambda name: self.C(name).unsqueeze(1).unsqueeze(1).broadcast_to((128, 2, 4, 64))
                t = V(dst, ps[:, :].rearrange("p (q n t) -> p q n t", q=2, t=64), m4("m2L"), ALU.mult, t)
                self.banks.give(i, t)
            for p in range(2 * pp, 2 * pp + 2):
                tM[p] = G(h8(M[:, p, :]), h8(M[:, p, :]), mk("I64"), ALU.add, t)
            yield
        for p in range(4):
            ks = []
            for hp in (0, 64):
                for which in (0, 1):
                    i, ps, fr = self.banks.take()
                    for n in range(4):
                        for par in range(2):
                            c = 2 * p + par
                            l = (B[hp:hp + 64, n, :] if which == 0 else KK[n][hp:hp + 64, :])[:, c * 64:c * 64 + 64]
                            t = self.mm(ps[64 * par:64 * par + 64, n * 128:n * 128 + 128], l,
                                        AR[hp:hp + 64, n, c, :, :].rearrange("p a t -> p (a t)"), True, True, ew, fr)
                    pv = ps[:, :].rearrange("p (n a t) -> p n a t", a=2, t=64)
                    n4 = lambda z: z[:, p, :].rearrange("p (n a t) -> p n a t", a=2, t=64)[:, :, hp // 64, :]
                    mk4 = lambda name: self.C(name).unsqueeze(1).broadcast_to((128, 4, 64))
                    a = V(n4(LT if which == 0 else KA), pv[:, :, 0, :], mk4("mSU"), ALU.mult, t)
                    b = V(n4(BR if which == 0 else KR), pv[:, :, 1, :], mk4("mIU"), ALU.mult)
                    self.banks.give(i, b)
                    ks.append(b)
                    if which == 0:
                        tLT[p, hp] = a
                yield
            tLT[p] = tLT[p, 64]
            t = G(h8(MT[:, p, :]), h8(LT[:, p, :]), mk("m2U"), ALU.mult, tLT[p])
            tMT[p] = G(h8(MT[:, p, :]), h8(MT[:, p, :]), mk("I64"), ALU.add, t)
            tKA[p] = ks[-1]
        t_gram = ks[-1]
        VTk, BTk = self.H[:, 4:8, :], R(60, 4, 512)
        t_tok = []

        def tok_tr(src, dst, *w):
            out = []
            for p in range(4):
                i, ps, fr = self.banks.take()
                for n in range(4):
                    t = self.tr(ps[:, n * 128:n * 128 + 128], src[n][:, p * 128:p * 128 + 128], w, fr)
                t = self.cp(act, dst[:, p, :], ps[:, :], t)
                self.banks.give(i, t)
                out.append(t)
            return out, t
        self.tv_, _ = tok_tr(VV, VTk, t_gram)
        yield
        self.tb_, _ = tok_tr([B[:, n, :] for n in range(4)], BTk, t_gram)
        yield
        KTk = R(16, 4, 512)
        self.tk_, _ = tok_tr(KK, KTk, t_gram, self.tv_)
        yield
        for l in range(5):
            lv = self.cst[:, CC["lvl"][0] + 64 * l:CC["lvl"][0] + 64 * l + 64].unsqueeze(1).broadcast_to((128, 8, 64))
            tP, tL = {}, {}
            for p in range(4):
                tL[p] = G(h8(LL[:, p, :]), h8(LT[:, p, :]), lv, ALU.mult, tMT[p])
            for p in range(4):
                i, ps, fr = self.banks.take()
                for h in range(8):
                    for par in (0, 64):
                        r, c = slice(par, par + 64), slice(h * 64, h * 64 + 64)
                        t = self.mm(ps[r, c], LL[r, p, c], M[r, p, c], True, True, tL[p], tM[p], fr)
                tP[p] = self.cp(act, PP[:, p, :], ps[:, :], t)
                self.banks.give(i, tP[p])
                yield
            for p in range(4):
                iM, pM, fM = self.banks.take() if l < 4 else (None, None, None)
                iT, pT, fT = self.banks.take()
                for h in range(8):
                    for par in (0, 64):
                        r, c = slice(par, par + 64), slice(h * 64, h * 64 + 64)
                        if l < 4:
                            tm = self.mm(pM[r, c], MT[r, p, c], PP[r, p, c], True, True, tP[p], fM)
                        tt_ = self.mm(pT[r, c], PP[r, p, c], MT[r, p, c], True, True, tP[p], fT)
                if l < 4:
                    tM[p] = V(M[:, p, :], M[:, p, :], pM[:, :], ALU.add, tm, tM[p])
                    self.banks.give(iM, tM[p])
                tMT[p] = V(MT[:, p, :], MT[:, p, :], pT[:, :], ALU.add, tt_, tMT[p])
                self.banks.give(iT, tMT[p])
                yield
        self.dump("mt", R(100, 2048), list(tMT.values()))
        ST, XX, UU, TS = R(76, 4, 128), R(80, 2, 512), R(84, 2, 512), R(90, 4, 64)
        Y = R(0, 4, 512)
        t0 = [tMT[3], self.tk_, self.tb_, self.tv_]
        tST = [dve.do(lambda e: e.memset(ST, 0.0), t0)]
        tS0 = tST[0]
        t_y, t_xf, t_uf = [], {}, {}
        for c in range(8):
            p, par = c // 2, 64 * (c % 2)
            r = slice(par, par + 64)
            i, ps, fr = self.banks.take()
            for h in range(8):
                hs = slice(h * 64, h * 64 + 64)
                self.mm(ps[r, hs], KA[r, p, hs], VTk[r, p, hs], h == 0, False, t0, fr)
            for n in range(4):
                t = self.mm(ps[r, n * 128:n * 128 + 128], AR[:, n, c, 0, :], ST[:, n, :], False, True, tST)
            tx = self.cp(act, XX[r, c // 2 % 2, :], ps[r, :], t, t_xf.get(c - 4), tS0)
            self.banks.give(i, tx)
            i, ps, fr = self.banks.take()
            for h in range(8):
                hs = slice(h * 64, h * 64 + 64)
                t = self.mm(ps[r, hs], MT[r, p, hs], XX[r, c // 2 % 2, hs], True, True, tx, fr)
            t_xf[c] = t
            tu = self.cp(act, UU[r, c // 2 % 2, :], ps[r, :], t, t_uf.get(c - 4), tS0)
            self.banks.give(i, tu)
            i, ps, fr = self.banks.take()
            for h in range(8):
                n, hp = h // 2, slice(64 * (h % 2), 64 * (h % 2) + 64)
                hs = slice(h * 64, h * 64 + 64)
                o = ps[hp, n * 64:n * 64 + 64]
                self.mm(o, KTk[r, p, hs], VTk[r, p, hs], h < 2, False, fr)
            for h in range(8):
                n, hp = h // 2, slice(64 * (h % 2), 64 * (h % 2) + 64)
                hs = slice(h * 64, h * 64 + 64)
                t = self.mm(ps[hp, n * 64:n * 64 + 64], BTk[r, p, hs], UU[r, c // 2 % 2, hs], False, True, tu)
            ty = []
            for hp in (0, 64):
                ty.append(V(TS[hp:hp + 64], ps[hp:hp + 64, 0:256].rearrange("p (n v) -> p n v", v=64),
                            ST[hp:hp + 64, :, hp:hp + 64], ALU.add, t, tST))
            self.banks.give(i, ty)
            i, ps, fr = self.banks.take()
            for n in range(4):
                self.mm(ps[:, n * 64:n * 64 + 64], ST[:, n, :], AR[:, n, c, 1, :], n == 0, False, fr)
            for h in range(8):
                n, hp = h // 2, slice(64 * (h % 2), 64 * (h % 2) + 64)
                hs = slice(h * 64, h * 64 + 64)
                o = ps[hp, n * 64:n * 64 + 64]
                self.mm(o, VTk[r, p, hs], KR[r, p, hs], False, False)
                t = self.mm(o, UU[r, c // 2 % 2, hs], BR[r, p, hs], False, True)
            t_uf[c] = t
            tST = [V(ST[hp:hp + 64, :, hp:hp + 64], TS[hp:hp + 64],
                     GC[hp:hp + 64, :, c].unsqueeze(2).broadcast_to((64, 4, 64)), ALU.mult, ty, t) for hp in (0, 64)]
            t = self.cp(act, Y[:, :, c * 64:c * 64 + 64], ps[:, 0:256].rearrange("p (n v) -> p n v", v=64), t, t0)
            self.banks.give(i, t)
            t_y.append(t)
            yield
        self.dump("y0", R(0, 2048), t_y)
        self.ysp = [self.pair(36 + 4 * k, 38 + 4 * k) for k in range(8)]
        self.t_ysp = [None] * 4 + [self.split(*self.ysp[4 + k], R(28, 4, 512)[:, k, :], self.t_os[k], t_y, q=pool)
                                   for k in range(4)]
        self.t_yr = []
        D = [(R(92, 512), R(94, 512), R(96, 512)), (R(68, 512), R(70, 512), R(72, 512))]
        le = [t_y, t_y]
        nb = []
        for n in range(4):
            a, b, c = D[n % 2]
            y = Y[:, n, :]
            i, ps, fr = self.banks.take()
            m = self.mm(ps[:, :], self.C("blk"), y, True, True, t_y, fr)
            t1 = self.stt(y, ps[:, :], -1.0 / 64, y, ALU.mult, ALU.add, m)
            self.banks.give(i, t1)
            t2 = self.af(a, y, ACT.Square, t1, le[n % 2])
            i, ps, fr = self.banks.take()
            m = self.mm(ps[:, :], self.C("blk"), a, True, True, t2, fr)
            t2 = self.rsqrt(b, ps[:, :], self.kc(EPSLN), 1.0 / 64, m, le[n % 2])
            self.banks.give(i, t2)
            t3 = self.stt(y, y, self.pc("lnw", n), b, ALU.mult, ALU.mult, t2, t1)
            t3 = self.stt(y, y, self.pc("lnb", n), self.H[:, n, :], ALU.add, ALU.add, t3)
            i, ps, fr = self.banks.take()
            m = self.mm(ps[:, :], g2[:, n * 128:n * 128 + 128], ZB[:, 13, :], True, True, t_gl, fr)
            t3 = V(y, y, ps[:, :], ALU.mult, m, t3)
            self.banks.give(i, t3)
            le[n % 2] = t3
            self.t_yr.append(t3)
            self.t_ysp[n] = self.split(*self.ysp[n], y, t3, t_y)
            yield

    def load_layer_tables(self, *after):
        self.c2 = self.region(24, NC2)
        s = self.P.dsem("c2")
        self.t_c2 = self.P.dma(self.P.sp, self.c2, self.d["cst2"], s, *after)

    def load_lw(self, *after):
        self.slw = self.P.dsem("lw")
        self.lw = self.region(109.5, 2560)
        self.t_lw = self.P.dma(self.P.sp, self.lw, self.d["lw"][0], self.slw, *after)

    def layers(self, stop):
        P, R = self.P, self.region
        X = [self.X[:, k, :] for k in range(8)]
        Hs = self.Hs
        t_X, self.t_end = self.t_X, self.t_X
        st = self.norm_stats(R(59, 2, 512), t_X)
        for k in range(8):
            self.norm_tile(st, X[k], t_X[k])
        for l in range(2):
            t_h = self.norm_apply(st, X, Hs, [self.pc(f"ng{l}", k) for k in range(8)])
            self.layer(l, Hs, t_h)
            Y = [self.pair(a, a + 2) for a in (85, 89, 95, 99, 103, 63, 75, 119.5, 43, 47, 51, 55)]
            each = [self.split(*Y[k], self.G[:, k, :], self.t_y[k], self.t_ysf, q=P.pool if k % 2 else None)
                    for k in range(12)]
            t_X = []
            if l == 0:
                st = self.norm_stats(R(59, 2, 512), self.t_y)
                self.t_lw = P.dma(P.sp, self.lw, self.d["lw"][1], self.slw, self.t_mla)
            so = P.dsem("out") if l == 1 else None
            for n in range(8):
                i, ps, fr = self.banks.take()
                t = self.dense([(f"o{l}", n, k) for k in range(12)], Y, ps[:, :], fr, each=each)
                u = self.tt(P.dve, X[n], ps[:, :], X[n], ALU.add, t)
                self.banks.give(i, u)
                t_X.append(u)
                if l == 1:
                    P.dma(P.sp, self.out[:, n, :], X[n], so, u)
                elif n:
                    self.norm_tile(st, X[n - 1], t_X[n - 1])
            if l == 0:
                self.norm_tile(st, X[7], t_X[7])
                self.dump("Y12", self.G, self.t_y, t)
                self.dump("l0", self.X[:, :, :], t_X)
            self.t_end = [t_X, t]
            if stop == "l0":
                return

    def layer(self, l, Hs, t_h):
        P, R = self.P, self.region
        act, dve, pool = P.act, P.dve, P.pool
        self.G = R(0, 12, 512)
        self.L = R(37, 3, 512)
        self.name = f"l{l}"
        te = self.t_end
        RT = R(33, 4, 4, 2, 16)
        cs, sn = (self.c2[:, 2048 + 64 * i:2112 + 64 * i].rearrange("p (a d) -> p a d", a=4) for i in (0, 1))
        gr = self.pc(f"gr{l}", 0, 64).rearrange("p (b d) -> p b d", b=2)
        for i, (tb, lo) in enumerate(((cs, 0), (cs, 16), (sn, 0), (sn, 16))):
            self.t_rt = self.tt(pool, RT[:, i], tb.unsqueeze(2).broadcast_to((128, 4, 2, 16)),
                                gr[:, :, lo:lo + 16].unsqueeze(1).broadcast_to((128, 4, 2, 16)), ALU.mult,
                                self.t_c2, te)
        self.RT = RT
        ST = R(35.5, 352)
        self.ST = ST
        i, pst, frs = self.banks.take()
        t_sq, self.t_l = [], []
        SQ = R(75, 3, 512)
        for n in range(3):
            b, ps, fr = self.banks.take()
            t = self.dense([(self.name, n, k) for k in range(8)], Hs, ps[:, :], fr, each=t_h)
            a = self.af(SQ[:, n, :], ps[:, :], ACT.Square, t, te)
            c = self.af(self.L[:, n, :], ps[:, :], ACT.Copy, t, te,
                        scale=self.pc(f"qan{l}", n) if n < 2 else self.pc(f"kvan{l}"))
            self.banks.give(b, a, c)
            t_sq.append(a)
            self.t_l.append(c)
        b, psr, fr = self.banks.take()
        for k in range(8):
            w, wt = self.wblock((self.name, 3, k))
            for q in range(4):
                t = self.mms(psr[:, q * 32:q * 32 + 32], self.tok(k, q), [x[:, 0:32] for x in w],
                            k == 0 and q == 0, k == 7, wt, fr)
            self.wused(t)
        self.KRt = R(35, 4, 32)
        self.t_kr = self.cp(act, self.KRt, psr[:, 0:128].rearrange("p (q d) -> p q d", q=4), t, te)
        self.banks.give(b, self.t_kr)
        for n in range(3):
            for q in range(4):
                o = (0 if n < 2 else 4) + q
                t = self.mm(pst[:, o:o + 1], SQ[:, n, q * 128:q * 128 + 128], self.C("ones")[:, 0:1],
                            n == 0 and q == 0, n > 0, t_sq[n], frs)
        a = self.ts(dve, ST[:, 0:4], pst[:, 0:4], 1.0 / 256, ALU.mult, 1e-6, ALU.add, t, te)
        a = self.ts(dve, ST[:, 4:8], pst[:, 4:8], 1.0 / 128, ALU.mult, 1e-6, ALU.add)
        self.banks.give(i, a)
        t = self.af(ST[:, 8:12], ST[:, 4:8], ACT.Sqrt, a)
        t = dve.do(lambda e: e.reciprocal(ST[:, 8:12], ST[:, 8:12]), t)
        self.t_st = t
        self.t_y = [None] * 12
        self.t_sq, self.silu_last = {}, []
        d = self.dense_rest(l)
        self.run((self.qk(l), 1), (self.take_n(d, 4), 1))
        self.run((self.heads(l), 1), (self.take_n(d, 14), 1))
        self.run((self.windows(l), 2), (d, 1))
        self.t_ysf = [self.t_mla, self.t_wt, self.t_win]
        t_s = [self.af(self.G[:, m, :], self.G[:, m, :], ACT.Silu, self.t_raw[m]) for m in (4, 5, 6, 7, 8, 9, 10, 11)]
        for j, m in enumerate((4, 5, 6, 7, 8, 9, 10, 11)):
            src = self.YC[:, m - 4, :] if m < 8 else self.SO[:, m - 8, :]
            self.t_y[m] = self.tt(dve if j % 3 else pool, self.G[:, m, :], self.G[:, m, :], src, ALU.mult, t_s[j],
                                  self.t_yc[m - 4] if m < 8 else self.t_so)

    def tok(self, k, q):
        return [x[:, q * 128:q * 128 + 128] for x in self.Hs[k]]

    def take_n(self, g, n):
        for _ in range(n):
            try:
                next(g)
            except StopIteration:
                return
            yield

    def proj(self, n):
        i, ps, fr = self.banks.take()
        t = self.dense([(self.name, n, k) for k in range(8)], self.Hs, ps[:, :], fr)
        return i, ps, t

    def dense_rest(self, l):
        P, R = self.P, self.region
        act, dve, pool = P.act, P.dve, P.pool
        te = self.t_end
        self.t_g = {}
        self.t_raw = {}
        for n in range(4):
            i, ps, t = self.proj(4 + n)
            self.t_raw[n] = self.cp(act, self.G[:, n, :], ps[:, :], t, te)
            self.banks.give(i, self.t_raw[n])
            yield
        hold = [self.banks.take() for _ in range(4)]
        for k in range(8):
            w, wt = self.wblock([(self.name, 24 + n, k) for n in range(4)], 4)
            for q in range(4):
                t = self.mms(hold[q][1][:, :], self.tok(k, q), w, k == 0, k == 7, wt, hold[q][2])
            self.wused(t)
            if k % 2:
                yield
        self.q_ps, self.t_q = hold, t
        b, ps, fr = self.banks.take()
        b2, ps2, fr2 = self.banks.take()
        for which, p_, f_ in ((28, ps, fr), (29, ps2, fr2)):
            for k in range(8):
                w, wt = self.wblock((self.name, which, k))
                for q in range(4):
                    t = self.mms(p_[:, q * 128:q * 128 + 128], self.tok(k, q), w,
                                k == 0 and q == 0, k == 7, wt, f_)
                self.wused(t)
            if which == 28:
                self.k_ps, self.t_k = (b, ps), t
                self.window_norm(l)
                yield
        self.SV = R(105.5, 4, 128)
        self.t_sv = self.cp(act, self.SV.rearrange("p q v -> p (q v)"), ps2[:, :], t, te, self.t_qkfree)
        self.banks.give(b2, self.t_sv)
        yield
        self.window_t()
        yield
        for n in range(4):
            i, ps, t = self.proj(30 + n)
            self.t_raw[8 + n] = self.cp(dve, self.G[:, 8 + n, :], ps[:, :], t, te)
            self.banks.give(i, self.t_raw[8 + n])
            yield
        self.YC = YC = R(119.5, 4, 512)
        CU = R(127.5, 516)
        CH = R(129.75, 512)
        t0 = dve.do(lambda e: e.memset(CU[:, 0:2], 0.0), te, self.t_wt)
        t_y, t_u = t0, t0
        self.t_yc = []
        for j in range(4):
            i, ps, t = self.proj(8 + j)
            ta = self.cp(act, CH, ps[:, :], t, t_u)
            self.banks.give(i, ta)
            yield
            i, ps, t = self.proj(16 + j)
            t_u = self.tt(dve, CU[:, 2:514], ps[:, :], CH, ALU.mult, t, ta, t_y)
            self.banks.give(i, t_u)
            y = YC[:, j, :]
            a = self.ts(pool, y, CU[:, 0:512], self.pc(f"cw{l}", j), ALU.mult, None, None, t_u, self.t_qkfree)
            a = self.stt(y, CU[:, 1:513], self.pc(f"cw{l}", 4 + j), y, ALU.mult, ALU.add, a)
            t_y = self.stt(y, CU[:, 2:514], self.pc(f"cw{l}", 8 + j), y, ALU.mult, ALU.add, a)
            yield
            i, ps, t = self.proj(12 + j)
            b = self.tt(dve, y, y, ps[:, :], ALU.mult, t, t_y)
            self.banks.give(i, b)
            self.t_yc.append(b)
            yield
            i, ps, t = self.proj(20 + j)
            self.t_raw[4 + j] = self.cp(act, self.G[:, 4 + j, :], ps[:, :], t, te)
            self.banks.give(i, self.t_raw[4 + j])
            yield

    def window_norm(self, l):
        P, R = self.P, self.region
        act, dve, pool = P.act, P.dve, P.pool
        te = self.t_end
        W = R(95.5, 4, 640)
        SQ = R(127.5, 640)
        S = self.ST[:, 168:208].rearrange("p (q h) -> p q h", q=4)
        bk, psk = self.k_ps
        ts_ = []
        last = te
        for q in range(4):
            psq = self.q_ps[q][1]
            a = self.af(SQ[:, 0:512], psq[:, :], ACT.Square, self.t_q, last)
            b = self.af(SQ[:, 512:640], psk[:, q * 128:q * 128 + 128], ACT.Square, self.t_k)
            last = dve.do(lambda e, q=q: e.tensor_reduce(out=S[:, q, :], in_=SQ.rearrange("p (h d) -> p h d", d=64),
                                                         op=ALU.add, axis=AX.X), a, b, te)
            ts_.append(last)
        a = self.ts(dve, S, S, 1.0 / 64, ALU.mult, 1e-6, ALU.add, ts_)
        a = self.af(S, S, ACT.Sqrt, a)
        a = dve.do(lambda e: e.reciprocal(S, S), a)
        t_w = []
        for q in range(4):
            i, psq, _ = self.q_ps[q]
            b = self.tt(dve, W[:, q, 0:512].rearrange("p (h d) -> p h d", d=64),
                        psq[:, :].rearrange("p (h d) -> p h d", d=64),
                        S[:, q, 0:8].unsqueeze(2).broadcast_to((128, 8, 64)), ALU.mult, a, te, self.t_mlaw)
            self.banks.give(i, b)
            c = self.tt(dve, W[:, q, 512:640].rearrange("p (h d) -> p h d", d=64),
                        psk[:, q * 128:q * 128 + 128].rearrange("p (h d) -> p h d", d=64),
                        S[:, q, 8:10].unsqueeze(2).broadcast_to((128, 2, 64)), ALU.mult, a)
            t_w.append(c)
        self.banks.give(bk, c)
        self.WT_, self.t_wn = W, t_w

    def window_t(self):
        l = int(self.name[1])
        self.SQT = [self.region(x, 512) for x in (37, 39, 41, 33, 107.5)]
        self.t_sqt = []
        for n in range(5):
            i, ps, fr = self.banks.take()
            for q in range(4):
                t = self.tr(ps[:, q * 128:q * 128 + 128], self.WT_[:, q, n * 128:n * 128 + 128], self.t_wn[q], fr)
            t = self.af(self.SQT[n], ps[:, :], ACT.Copy, t, self.t_mlaw,
                        scale=self.pc(f"sqn{l}" if n < 4 else f"skn{l}"))
            self.banks.give(i, t)
            self.t_sqt.append(t)
        self.t_wt = t

    def qk(self, l):
        P, R = self.P, self.region
        act, dve, pool = P.act, P.dve, P.pool
        L, lw, ST, RT = self.L, self.lw, self.ST, self.RT
        te = self.t_end
        KT, QT, MV = R(43, 8, 512), R(59, 8, 512), R(87, 4, 512)
        self.KT, self.QT, self.MV = KT, QT, MV
        gcol = [self.pc(f"kn{l}"), self.pc(f"qn{l}")]
        KQ = [R(75 + 6 * b, 2, 8, 96) for b in range(2)]
        SQ = [R(95 + 6 * b, 2, 8, 96) for b in range(2)]
        T4 = R(119.5, 4, 2, 8, 16)
        self.t_mv, self.t_kt = [], []
        free = [te, te]
        t_t4 = te
        pend = None

        def transposes(q, kq, t):
            out = []
            for w in range(2):
                for hh in range(2):
                    i, ps, fr = self.banks.take()
                    for h in range(4):
                        m = self.tr(ps[0:96, h * 128:h * 128 + 128], kq[:, w, 4 * hh + h, :], t, fr)
                    dst = (KT, QT)[w][0:96, 4 * hh:4 * hh + 4, q * 128:q * 128 + 128]
                    src = ps[0:96, :].rearrange("p (h t) -> p h t", h=4)
                    if hh:
                        e_ = self.af(dst, src, ACT.Copy, m, te, scale=gcol[w][0:96])
                    else:
                        e_ = self.ts(dve, dst, src, gcol[w][0:96], ALU.mult, None, None, m, te)
                    self.banks.give(i, e_)
                    out.append(e_)
            self.t_kt += out
            return m
        for q in range(4):
            b = q % 2
            kq, sq = KQ[b], SQ[b]
            tok = slice(q * 128, q * 128 + 128)
            hold = []
            for hh in range(2):
                i, ps, fr = self.banks.take()
                self.mm(ps[:, 0:384], L[:, 0, tok], lw[:, hh * 384:hh * 384 + 384], True, False, self.t_l, self.t_lw, fr)
                t = self.mm(ps[:, 0:384], L[:, 1, tok], lw[:, 768 + hh * 384:1152 + hh * 384], False, True)
                hold.append((i, ps))
            ik, psk, fr = self.banks.take()
            tk = self.mm(psk[:, :], L[:, 2, tok], lw[:, 1536:2048], True, True, fr)
            iv, psv, fr = self.banks.take()
            tv = self.mm(psv[:, :], L[:, 2, tok], lw[:, 2048:2560], True, True, fr)
            h96 = lambda ps: ps[:, 0:384].rearrange("p (h d) -> p h d", h=4)
            a = [self.af(sq[:, 1, 4 * hh:4 * hh + 4, :], h96(hold[hh][1]), ACT.Square, t, free[b]) for hh in range(2)]
            a.append(self.af(sq[:, 0, :, 0:64], psk[:, :].rearrange("p (h d) -> p h d", d=64), ACT.Square, tk, free[b], self.t_st,
                             scale=ST[:, 8 + q:9 + q]))
            u = self.af(MV[:, q, :], psv[:, :], ACT.Copy, tv, self.t_st, te, scale=ST[:, 8 + q:9 + q])
            self.banks.give(iv, u)
            self.t_mv.append(u)
            a.append(self.tt(pool, sq[:, 0, :, 64:96], self.KRt[:, q, :].unsqueeze(1).broadcast_to((128, 8, 32)),
                             self.KRt[:, q, :].unsqueeze(1).broadcast_to((128, 8, 32)), ALU.mult, self.t_kr, free[b]))
            yield
            s_ = ST[:, 16 + 16 * q:32 + 16 * q].rearrange("p (w h) -> p w h", w=2)
            v = ST[:, 104 + 16 * q:120 + 16 * q].rearrange("p (w h) -> p w h", w=2)
            c = dve.do(lambda e, sq=sq, s_=s_: e.tensor_reduce(out=s_, in_=sq, op=ALU.add, axis=AX.X), a)
            em = ST[:, 12 + q:13 + q]
            c1 = self.ts(dve, em, ST[:, q:q + 1], 1e-6, ALU.mult, None, None, c)
            c2_ = self.ts(dve, s_[:, 0], s_[:, 0], 1.0 / 96, ALU.mult, 1e-6, ALU.add, c)
            c3 = self.ts(dve, s_[:, 1], s_[:, 1], 1.0 / 96, ALU.mult, em, ALU.add, c1, c)
            c = self.af(v, s_, ACT.Sqrt, c2_, c3)
            c = dve.do(lambda e, v=v: e.reciprocal(v, v), c)
            d_ = self.ts(dve, s_[:, 0], v[:, 0], ST[:, 8 + q:9 + q], ALU.mult, None, None, c)
            bc = lambda ap, n: ap.unsqueeze(2).broadcast_to((128, ap.shape[1], n))
            w1 = [self.tt(dve, kq[:, 1, 4 * hh:4 * hh + 4, :], h96(hold[hh][1]), bc(v[:, 1, 4 * hh:4 * hh + 4], 96),
                          ALU.mult, c, free[b]) for hh in range(2)]
            w2 = self.tt(dve, kq[:, 0, :, 0:64], psk[:, :].rearrange("p (h d) -> p h d", d=64), bc(s_[:, 0], 64),
                         ALU.mult, d_, free[b])
            w3 = self.tt(pool, kq[:, 0, :, 64:96], self.KRt[:, q, :].unsqueeze(1).broadcast_to((128, 8, 32)),
                         bc(v[:, 0], 32), ALU.mult, c, free[b])
            self.banks.give(hold[0][0], w1[0])
            self.banks.give(hold[1][0], w1[1])
            self.banks.give(ik, w2, a)
            yield
            x1, x2 = kq[:, :, :, 64:80], kq[:, :, :, 80:96]
            rt = lambda i: RT[:, i, q].unsqueeze(2).broadcast_to((128, 2, 8, 16))
            m1 = self.tt(pool, T4[:, 0], x1, rt(0), ALU.mult, w1, w3, self.t_rt, t_t4)
            m2 = self.tt(pool, T4[:, 1], x2, rt(3), ALU.mult)
            m3 = self.tt(pool, T4[:, 2], x2, rt(1), ALU.mult)
            m4 = self.tt(pool, T4[:, 3], x1, rt(2), ALU.mult)
            m2 = self.tt(dve, x1, T4[:, 0], T4[:, 1], ALU.subtract, m4)
            m4 = self.tt(dve, x2, T4[:, 2], T4[:, 3], ALU.add, m4)
            t_t4 = m4
            if pend:
                m = transposes(*pend)
                free[1 - b] = [m]
            pend = (q, kq, [m2, m4, w2])
            yield
        m = transposes(*pend)
        self.t_qkfree = [m, m4]
        self.t_mlaw = [self.t_qkfree, a]
        self.t_silu = [self.af(self.G[:, n, :], self.G[:, n, :], ACT.Silu, self.t_raw[n]) for n in range(4)]
        yield

    def heads(self, l):
        P, R = self.P, self.region
        act, dve, pool = P.act, P.dve, P.pool
        KT, QT, MV = self.KT, self.QT, self.MV
        PB = [R(75, 1280), R(80, 1280)]
        PT = [R(109.5, 1280), R(114.5, 1280)]
        sc = 96.0 ** -0.5
        off = {3: 0, 2: 512, 0: 896, 1: 1024}
        n_ = lambda q: 128 * (q + 1)
        poff = {0: 0, 1: 512, 3: 896, 2: 1024}
        S2 = self.ST[:, 208:272].rearrange("p (b k q) -> p b k q", b=2, k=8)
        t_tr, t_pv, tp = {}, {}, {}
        te = [self.t_end, self.t_qkfree]

        def A(h):
            b = h % 2
            mx, nm, rs, rc = (S2[:, b, k, :] for k in range(4))
            banks = [self.banks.take() for _ in range(3)]
            where = {3: (0, 0), 2: (1, 0), 0: (1, 384), 1: (2, 0)}
            tm = []
            first = set()
            for q in (3, 2, 0, 1):
                bi, o = where[q]
                i, ps, fr = banks[bi]
                n = n_(q)
                t = self.mm(ps[:, o:o + n], QT[0:96, h, q * 128:q * 128 + 128], KT[0:96, h, 0:n], True, True,
                            self.t_kt, fr)
                if q == 2:
                    continue
                for qq in ((2, 0) if q == 0 else (q,)):
                    bi, o = where[qq]
                    ps, n = banks[bi][1], n_(qq)
                    u = self.tt(dve, ps[:, o + n - 128:o + n], ps[:, o + n - 128:o + n], self.C("caus"), ALU.add, t)
                    tm.append(dve.do(lambda e, o_=mx[:, qq:qq + 1], a=ps[:, o:o + n]:
                                     e.tensor_reduce(out=o_, in_=a, op=ALU.max, axis=AX.X), u, t_tr.get(h - 2)))
            t = self.ts(dve, nm, mx, -sc, ALU.mult, None, None, tm)
            te_ = {}
            for q in (3, 2, 0, 1):
                bi, o = where[q]
                ps, n = banks[bi][1], n_(q)
                te_[q] = self.af(PB[b][:, off[q]:off[q] + n], ps[:, o:o + n], ACT.Exp, t, t_tr.get(h - 2, te),
                                 bias=nm[:, q:q + 1], scale=sc, acc=rs[:, q:q + 1])
            for bi, qs in ((0, (3,)), (1, (2, 0)), (2, (1,))):
                self.banks.give(banks[bi][0], [te_[q] for q in qs])
            t = dve.do(lambda e: e.reciprocal(rc, rs), list(te_.values()))
            tp[h] = {q: self.ts(pool, PB[b][:, off[q]:off[q] + n_(q)], PB[b][:, off[q]:off[q] + n_(q)],
                                rc[:, q:q + 1], ALU.mult, None, None, t) for q in (0, 1, 2, 3)}

        def B(h):
            b = h % 2
            ev = []
            for js in ((0,), (1, 3), (2,)):
                i, ps, fr = self.banks.take()
                o = 0
                for j in js:
                    for q in range(j, 4):
                        t = self.tr(ps[:, o:o + 128], PB[b][:, off[q] + j * 128:off[q] + j * 128 + 128], tp[h][3], fr)
                        o += 128
                e_ = self.cp(act if js == (0,) else dve, PT[b][:, poff[js[0]]:poff[js[0]] + o], ps[:, 0:o], t,
                             t_pv.get(h - 2, te))
                self.banks.give(i, e_)
                ev.append(e_)
            t_tr[h] = t
            self.evs[h] = ev

        def C(h):
            b = h % 2
            i, ps, fr = self.banks.take()
            r = slice(64 * b, 64 * b + 64)
            for j in (0, 1, 2, 3):
                t = self.mm(ps[r, j * 128:512], MV[:, j, 64 * h:64 * h + 64],
                            PT[b][:, poff[j]:poff[j] + 512 - 128 * j], j == 0, j == 3, self.evs[h], self.t_mv, fr)
            t_pv[h] = t
            g = self.G[r, h // 2, :]
            t = self.tt(dve, g, ps[r, :], g, ALU.mult, t, self.t_silu[h // 2])
            self.banks.give(i, t)
            self.t_y[h // 2] = [self.t_y[h // 2], t]
        self.evs = {}
        for s in range(10):
            if s < 8:
                A(s)
                yield
            if 1 <= s < 9:
                B(s - 1)
                yield
            if s >= 2:
                C(s - 2)
                yield
        self.t_mla = [t_tr[7], t_pv[7]]

    def windows(self, l):
        P, R = self.P, self.region
        act, dve, pool = P.act, P.dve, P.pool
        SQT, SV = self.SQT, self.SV
        ZZ = [R(43, 8, 256), R(51, 8, 256)]
        PP = [R(75, 2, 2, 512), R(59, 2, 2, 512)]
        self.SO = R(67, 4, 512)
        al = self.c2[:, 0:2048].rearrange("p (h k) -> p h k", h=8)
        sink = self.pc(f"sink{l}", 0, 8)
        S = self.ST[:, 272:352].rearrange("p (b k h) -> p b k h", b=2, k=5)
        tp, ev, t_tr, t_pv = {}, {}, {}, {}
        tm = self.t_mla
        self.t_so = []

        def A(n):
            b = n % 2
            Z = ZZ[b]
            mx, nm, rs, es, rc = (S[:, b, k, :] for k in range(5))
            lo = 128 if n == 0 else 0
            w = 256 - lo
            k0 = (n - 1) * 128 + lo
            tz = []
            for g in range(2):
                for jj in range(2):
                    i, ps, fr = self.banks.take()
                    for x in range(2):
                        j = 2 * jj + x
                        t = self.mm(ps[:, x * 256 + lo:x * 256 + 256], SQT[j][64 * g:64 * g + 64, n * 128:n * 128 + 128],
                                    SQT[4][64 * g:64 * g + 64, k0:k0 + w], True, True, self.t_sqt, fr)
                    h0 = 4 * jj + g
                    t = self.stt(Z[:, h0:h0 + 3:2, lo:256], ps[:, :].rearrange("p (x k) -> p x k", x=2)[:, :, lo:256],
                                 0.125, al[:, h0:h0 + 3:2, lo:256], ALU.mult, ALU.add, t, self.t_c2, t_tr.get(n - 2, tm))
                    self.banks.give(i, t)
                    tz.append(t)
            yield
            t = dve.do(lambda e, lo=lo: e.tensor_reduce(out=mx, in_=Z[:, :, lo:256], op=ALU.max, axis=AX.X), tz)
            t = self.tt(dve, mx, mx, sink, ALU.max, t)
            ta = self.ts(dve, nm, mx, -1.0, ALU.mult, None, None, t)
            tb = self.tt(dve, es, sink, mx, ALU.subtract, t)
            te = [self.af(Z[:, h, lo:256], Z[:, h, lo:256], ACT.Exp, ta, tz, bias=nm[:, h:h + 1], acc=rs[:, h:h + 1])
                  for h in range(8)]
            tb = self.af(es, es, ACT.Exp, tb)
            t = self.tt(dve, rc, rs, es, ALU.add, te, tb)
            t = dve.do(lambda e: e.reciprocal(rc, rc), t)
            tp[n] = self.tt(pool, Z[:, :, lo:256], Z[:, :, lo:256], rc.unsqueeze(2).broadcast_to((128, 8, w)),
                            ALU.mult, t, te)
            yield

        def B(n):
            b = n % 2
            Z, PT = ZZ[b], PP[b]
            lo = 128 if n == 0 else 0
            for g in range(2):
                for kb in range(lo // 128, 2):
                    i, ps, fr = self.banks.take()
                    for j in range(4):
                        t = self.tr(ps[:, j * 128:j * 128 + 128], Z[:, 2 * j + g, kb * 128:kb * 128 + 128], tp[n], fr)
                    e_ = self.cp(act if kb else dve, PT[:, g, kb, :], ps[:, :], t, t_pv.get(n - 2, tm))
                    self.banks.give(i, e_)
                    ev.setdefault(n, []).append(e_)
            t_tr[n] = t

        def C(n):
            PT = PP[n % 2]
            i, ps, fr = self.banks.take()
            kbs = range(1 if n == 0 else 0, 2)
            for g in range(2):
                for kb in kbs:
                    t = self.mm(ps[64 * g:64 * g + 64, :], SV[:, n - 1 + kb, 64 * g:64 * g + 64], PT[:, g, kb, :],
                                kb == kbs[0], kb == 1, ev[n], self.t_sv, fr)
            t_pv[n] = t
            t = self.cp(act, self.SO[:, :, n * 128:n * 128 + 128], ps[:, :].rearrange("p (j q) -> p j q", j=4), t, tm)
            self.banks.give(i, t)
            self.t_so.append(t)
        for s in range(6):
            if s < 4:
                yield from A(s)
            if 1 <= s < 5:
                B(s - 1)
                yield
            if s >= 2:
                C(s - 2)
                yield
        self.t_win = [t_tr[3], t_pv[3]]


def _cols(a, n):
    return np.asarray(a, np.float32).reshape(n, 128).T


def _pad(a, rows):
    out = np.zeros((rows,) + a.shape[1:], np.float32)
    out[:a.shape[0]] = a
    return out


SW = [0, 4, 1, 5, 2, 6, 3, 7]


def _heads(a, axis):
    a = np.moveaxis(a, axis, 0)
    a = a.reshape((8, 64) + a.shape[1:])[SW].reshape((512,) + a.shape[1:])
    return np.moveaxis(a, 0, axis)


def _weights(inp):
    W = {"ada": inp["w_ada"][0], "in": inp["w_in"][0], "glu": inp["s5_w_glu"][0], "out": inp["w_out"][0],
         "gate": inp["ffn_w_gate"][0], "up": inp["ffn_w_up"][0], "down": inp["ffn_w_down"][0]}
    for l in range(2):
        w = inp["w_in_2"][l]
        o = np.cumsum([0, 256, 128, 32, 512, 512, 512, 512, 512, 512, 128, 128, 512])
        part = [w[:, o[i]:o[i + 1]] for i in range(12)]
        rope = np.zeros((1024, 128), np.float32)
        rope[:, :32] = part[2]
        W[f"l{l}"] = np.concatenate([part[0], part[1], rope, part[3], part[4], part[5], part[6], part[7],
                                     _heads(part[8], 1), part[9], part[10], _heads(part[11], 1)], 1)
        wo = inp["w_out_2"][l]
        W[f"o{l}"] = np.concatenate([wo[:1024], _heads(wo[1024:], 0)], 0)
    return W


def _arrays(inp):
    f = lambda n: np.asarray(inp[n], np.float32)
    par = np.zeros((128, NPC), np.float32)

    def put(name, a):
        s, n = PCOLS[name]
        par[:a.shape[0], s:s + n] = a
    put("b_ada", _cols(f("b_ada")[0], 48))
    put("mu", _cols(f("mu_shift")[0], 14))
    for name, src in (("w0", "rw_w0"), ("a0", "rw_a0"), ("k_k", "rw_k_k"), ("k_a", "rw_k_a"), ("lnw", "rw_lnx_w"),
                      ("lnb", "rw_lnx_b"), ("bglu", "s5_b_glu"), ("gain", "s5_gain")):
        put(name, _cols(f(src)[0], 4))
    put("r_k", _cols(f("rw_r_k")[0].reshape(512), 4))
    put("s5d", _cols(f("s5_d")[0].reshape(512), 4))
    put("fgain", _cols(f("final_gain"), 8))
    put("c", _cols(f("c")[0], 8))
    put("are", f("s5_a_re")[0].reshape(16, 128).T)
    put("aim", f("s5_a_im")[0].reshape(16, 128).T)
    put("ldt", np.repeat(f("s5_log_dt")[0].reshape(16, 2), 64, axis=1).T)
    for l in range(2):
        put(f"ng{l}", _cols(f("norm_g_2")[l], 8))
        put(f"qan{l}", _cols(f("mla_q_a_norm_2")[l], 2))
        put(f"kvan{l}", _cols(f("mla_kv_a_norm_2")[l], 1))
        for name, src in (("qn", "mla_q_norm_2"), ("kn", "mla_k_norm_2")):
            put(f"{name}{l}", np.concatenate([f(src)[l][:64], np.ones(32, np.float32)])[:, None])
        both = np.concatenate([f("mla_k_norm_2")[l][64:], f("mla_q_norm_2")[l][64:]])
        put(f"gr{l}", np.broadcast_to(both[None, :], (128, 64)))
        put(f"cw{l}", np.concatenate([_cols(f("conv_w_2")[l][w], 4) for w in range(3)], 1))
        put(f"sqn{l}", np.tile(f("swa_q_norm_2")[l], 2)[:, None])
        put(f"skn{l}", np.tile(f("swa_k_norm_2")[l], 2)[:, None])
        put(f"sink{l}", np.broadcast_to(f("swa_sinks_2")[l][SW][None, :], (128, 8)))
    cst, cst2 = constants()
    b = lambda a: a.reshape(16, 128, 16).transpose(1, 0, 2).reshape(128, 256)
    bt = lambda a: b(a.transpose(0, 2, 1))
    s5p = np.stack([b(f("s5_b_re")[0]), b(f("s5_b_im")[0]), bt(f("s5_c_re")[0]), bt(f("s5_c_im")[0])], 1)
    small = np.stack([np.concatenate([f("rw_w2")[0], f("rw_a2")[0]], 0), f("rw_g2")[0]], 1)
    lw = []
    for l in range(2):
        qb, kvb = f("mla_w_qb_2")[l], f("mla_w_kvb_2")[l].reshape(128, 8, 128)
        lw.append(np.concatenate([qb[0:128], qb[128:256], kvb[:, :, :64].reshape(128, 512),
                                  kvb[:, :, 64:].reshape(128, 512)], 1))
    xT = f("x")[0].T.reshape(8, 128, 512).transpose(1, 0, 2)
    out = {"par": par, "cst": cst, "cst2": cst2, "s5p": s5p, "small": small, "lw": np.stack(lw), "xT": xT}
    return {k: np.ascontiguousarray(v) for k, v in out.items()}


def _program(nc, stop=None, dump_shapes=None):
    shapes = {"par": [128, NPC], "cst": [128, NCC], "cst2": [128, NC2], "s5p": [128, 4, 256],
              "small": [128, 2, 512], "lw": [2, 128, 2560], "xT": [128, 8, 512], "ws": [UNITS, 128, 1024]}
    d = {n: nc.dram_tensor("in_" + n, s, F32, kind="ExternalInput").ap() for n, s in shapes.items()}
    for n, s in (("kpad", [32, 16, 240]), ("ud", [32, 16, 8, 64]), ("yd", [32, 16, 8, 64])):
        d[n] = nc.dram_tensor("scr_" + n, s, F32).ap()
    out = nc.dram_tensor("outT", [128, 8, 512], F32, kind="ExternalOutput").ap()
    dumps = {n: nc.dram_tensor("dump_" + n, s, F32, kind="ExternalOutput").ap() for n, s in (dump_shapes or {}).items()}
    return Kern(nc, d, out, dumps).build(stop)


def _stream(W, order):
    ws = np.zeros((UNITS, 128, 8, 128), np.float32)
    for b, (name, n, k) in enumerate(order):
        ws[b // 8, :, b % 8, :] = W[name][k * 128:k * 128 + 128, n * 128:n * 128 + 128]
    return ws.reshape(UNITS, 128, 1024)


def kernel(**inputs):
    import concourse.bacc as _bacc
    from concourse.bass_utils import run_bass_kernel_spmd as _run

    nc = _bacc.Bacc("TRN2", target_bir_lowering=False, num_devices=1, dynamic_dma_scratch_size=1024)
    order = _program(nc)
    inp = {k: np.asarray(v) for k, v in inputs.items()}
    arrays = {"in_" + k: v for k, v in _arrays(inp).items()}
    arrays["in_ws"] = _stream(_weights(inp), order)
    r = _run(nc, [arrays], core_ids=[0])
    got = r.results[0]["outT"]
    return np.ascontiguousarray(got.transpose(2, 1, 0).reshape(1, 512, 1024))
```

```python
import math

import numpy as np
import concourse.bass as bass
from concourse import mybir
from contextlib import ExitStack

F32 = mybir.dt.float32
F32R = mybir.dt.float32r
ALU = mybir.AluOpType
ACT = mybir.ActivationFunctionType
AX = mybir.AxisListType

T = 512
NT = 8
DFF_T = 22
RING = 4
UNITS = 234
SBUF = 229344
ORDER = "si" * 3 + "s" * 4 + "ssi" * 8 + "s" * 4 + "i" * 3
WHOLE = set(range(16)) | set(range(36, 68))


class Tok:
    __slots__ = ("queue", "signals", "value")

    def __init__(self, queue):
        self.queue, self.signals, self.value = queue, False, None


class Queue:

    def __init__(self, name):
        self.name, self.items, self.sem, self.last = name, [], None, None

    def do(self, fn, *after):
        tok = Tok(self)
        waits = []
        for a in flat(after):
            a.signals = True
            waits.append(a)
        self.items.append((fn, waits, tok))
        self.last = tok
        return tok


class DmaTok(Tok):
    __slots__ = ("dsem",)


def flat(x):
    if x is None:
        return []
    if isinstance(x, Tok):
        return [x]
    out = []
    for y in x:
        out += flat(y)
    return out


class DmaSem:

    def __init__(self, prog, name):
        self.name, self.count, self.sem = name, 0, None
        prog.dsems.append(self)


class Prog:
    def __init__(self):
        self.pe, self.act, self.dve, self.pool, self.sp = (Queue(n) for n in ("pe", "act", "dve", "pool", "sp"))
        self.dsems = []

    def dsem(self, name):
        return DmaSem(self, name)

    def dma(self, queue, out, in_, dsem, *after):
        tok = DmaTok(queue)
        dsem.count += 16
        tok.dsem, tok.value = dsem, dsem.count
        waits = []
        for a in flat(after):
            a.signals = True
            waits.append(a)
        queue.items.append((lambda e: e.dma_start(out, in_), waits, tok))
        return tok

    def number(self):
        for q in (self.pe, self.act, self.dve, self.pool, self.sp):
            n = 0
            for _, _, tok in q.items:
                if not isinstance(tok, DmaTok) and tok.signals:
                    n += 1
                    tok.value = n

    def issue(self, q, eng):
        seen = {}
        for fn, waits, tok in q.items:
            for w in waits:
                sem = w.dsem.sem if isinstance(w, DmaTok) else w.queue.sem
                name = w.dsem.name if isinstance(w, DmaTok) else w.queue.name
                if seen.get(name, 0) < w.value:
                    eng.wait_ge(sem, w.value)
                    seen[name] = w.value
            ins = fn(eng)
            if isinstance(tok, DmaTok):
                ins.then_inc(tok.dsem.sem, 16)
            elif tok.signals:
                ins.then_inc(q.sem, 1)


class Banks:

    def __init__(self, aps):
        self.aps = aps
        self.free = [(i, []) for i in range(len(aps))]

    def take(self):
        i, toks = self.free.pop(0)
        return i, self.aps[i], toks

    def give(self, i, *toks):
        self.free.append((i, flat(toks)))


PCOLS = {}


def _pcols():
    at = 0
    for name, n in [("b_ada", 48), ("mu", 14), ("w0", 4), ("a0", 4), ("k_k", 4), ("k_a", 4), ("r_k", 4),
                    ("lnw", 4), ("lnb", 4), ("s5d", 4), ("bglu", 4), ("gain", 4), ("fgain", 8), ("c", 8),
                    ("are", 16), ("aim", 16), ("ldt", 16),
                    ("ng0", 8), ("ng1", 8), ("qan0", 2), ("qan1", 2), ("kvan0", 1), ("kvan1", 1),
                    ("qn0", 1), ("qn1", 1), ("kn0", 1), ("kn1", 1), ("cw0", 12), ("cw1", 12),
                    ("sqn0", 1), ("sqn1", 1), ("skn0", 1), ("skn1", 1), ("sink0", 8), ("sink1", 8),
                    ("gr0", 64), ("gr1", 64)]:
        PCOLS[name] = (at, n)
        at += n
    return at


NPC = _pcols()
CC = {}


def _ccols():
    at = 0
    for name, n in [("ident", 128), ("ones", 128), ("blk", 128), ("caus", 128), ("scan", 512),
                    ("I64", 64), ("m2L", 64), ("m2U", 64), ("mSU", 64), ("mIU", 64), ("lvl", 320), ("k", 8)]:
        CC[name] = (at, n)
        at += n
    return at


NCC = _ccols()
NC2 = 2176
EPS6, EPSLN, TENLN2, C1E24, HPI = range(5)


def constants():
    c = np.zeros((128, NCC), np.float32)

    def put(name, a):
        s, n = CC[name]
        c[:, s:s + n] = a
    i = np.arange(128)
    put("ident", np.eye(128))
    put("ones", 1.0)
    put("blk", (i[:, None] // 64) == (i[None, :] // 64))
    put("caus", np.where(i[None, :] > i[:, None], -1e30, 0.0))
    put("scan", (np.arange(512) % 64 != 0)[None, :].astype(np.float32))
    a, b = (i % 64)[:, None], np.arange(64)[None, :]
    put("I64", a == b)
    put("m2L", (a // 2 == b // 2) & (a > b))
    put("m2U", (a // 2 == b // 2) & (a < b))
    put("mSU", a < b)
    put("mIU", a <= b)
    lv = [((a // (2 * m)) == (b // (2 * m))) & ((a // m) < (b // m)) for m in (2, 4, 8, 16, 32)]
    put("lvl", np.concatenate(lv, 1))
    put("k", np.array([1e-6, 64e-5, 10 * math.log(2), 1e-24 * 2 ** 20, math.pi / 2, 0, 0, 0])[None, :])
    d = np.zeros((128, NC2), np.float32)
    q, k = i[:, None], np.arange(256)[None, :]
    dist = 128 + q - k
    ok = (dist >= 0) & (dist < 128)
    al = []
    for h in (0, 4, 1, 5, 2, 6, 3, 7):
        slope = np.float32(2.0 ** (-(h + 1)))
        al.append(np.where(ok, -slope * dist.astype(np.float32), np.float32(-1e30)))
    d[:, 0:2048] = np.concatenate(al, 1)
    half = 16
    inv = np.power(np.float32(10000.0), -np.arange(half, dtype=np.float32) / half).astype(np.float32)
    ang = (np.arange(512, dtype=np.float32)[:, None] * inv[None, :]).astype(np.float32)
    by_token = lambda a: a.reshape(4, 128, 16).transpose(1, 0, 2).reshape(128, 64)
    d[:, 2048:2112], d[:, 2112:2176] = by_token(np.cos(ang)), by_token(np.sin(ang))
    return c, d


class Kern:
    def __init__(self, nc, d, out, dumps=None):
        self.nc, self.d, self.out, self.dumps = nc, d, out, dumps or {}
        self.P = Prog()
        self.order = []

    def tt(self, q, out, a, b, op, *after):
        if q is self.P.pool:
            after += (q.last,)
        return q.do(lambda e: e.tensor_tensor(out=out, in0=a, in1=b, op=op), *after)

    def ts(self, q, out, a, s1, op0, s2, op1, *after):
        if q is self.P.pool:
            after += (q.last,)
        if s2 is None:
            return q.do(lambda e: e.tensor_scalar(out=out, in0=a, scalar1=s1, scalar2=None, op0=op0), *after)
        return q.do(lambda e: e.tensor_scalar(out=out, in0=a, scalar1=s1, scalar2=s2, op0=op0, op1=op1), *after)

    def stt(self, out, a, s, b, op0, op1, *after):
        return self.P.dve.do(lambda e: e.scalar_tensor_tensor(out=out, in0=a, scalar=s, in1=b, op0=op0, op1=op1), *after)

    def af(self, out, a, f, *after, bias=None, scale=1.0, acc=None):
        def fn(e):
            kw = {}
            if bias is not None:
                kw["bias"] = bias
            if acc is not None:
                kw["accum_out"] = acc
            return e.activation(out, a, f, scale=scale, **kw)
        return self.P.act.do(fn, *after)

    def cp(self, q, out, a, *after):
        if q is self.P.act:
            return q.do(lambda e: e.activation(out, a, ACT.Copy), *after)
        return q.do(lambda e: e.tensor_copy(out, a), *after)

    def mm(self, out, lhsT, rhs, start, stop, *after):
        return self.P.pe.do(lambda e: e.matmul(out, lhsT, rhs, start=start, stop=stop, skip_group_check=True), *after)

    def tr(self, out, in_, *after):
        idn = self.C("ident")
        return self.P.pe.do(lambda e: e.transpose(out, in_, idn), *after)

    def C(self, name):
        s, n = CC[name]
        return self.cst[:, s:s + n]

    def kc(self, i):
        s, _ = CC["k"]
        return self.cst[:, s + i:s + i + 1]

    def pc(self, name, i=0, n=1):
        s, _ = PCOLS[name]
        return self.par[:, s + i:s + i + n]

    def split_unit(self, u):
        if u in self.wsplit or u in WHOLE or u >= self.units:
            return
        slot, b = u % RING, u % 2
        raw = self.ring[:, slot * 1024:(slot + 1) * 1024]
        hi, lo = self.wpair(b)
        free = self.wlast.get(u - 2)
        t = self.cp(self.P.act, hi, raw, self.wdma[u], free)
        v = self.tt(self.P.dve, lo, raw, hi.bitcast(F32), ALU.subtract, t, free)
        self.wsplit[u] = [t, v]
        if u + RING < self.units:
            self.load_unit(u + RING, v)

    def wpair(self, b):
        return [self.ring2[:, b * 2048 + i * 1024:b * 2048 + i * 1024 + 1024] for i in (0, 1)]

    def wblock(self, key, n=1):
        b = len(self.order)
        self.order += key if n > 1 else [key]
        u, j = divmod(b, 8)
        assert j + n <= 8 and (u in WHOLE) == (self.order[b][0] == "ada")
        if j == 0:
            self.split_unit(u)
            self.split_unit(u + 1)
        c = slice(j * 128, (j + n) * 128)
        if u in WHOLE:
            o = u % RING * 1024
            return self.ring[:, o:o + 1024][:, c], self.wdma[u]
        return [x[:, c] for x in self.wpair(u % 2)], self.wsplit[u]

    def wused(self, tok):
        b = len(self.order)
        if b % 8 == 0:
            u = b // 8 - 1
            self.wlast[u] = tok
            if u in WHOLE and u + RING < self.units:
                self.load_unit(u + RING, tok)

    def load_unit(self, u, *after):
        slot = u % RING
        self.wdma[u] = self.P.dma(self.P.sp, self.ring[:, slot * 1024:(slot + 1) * 1024],
                                  self.d["ws"][u, :, :], self.wsem[slot], *after)

    def mms(self, out, lhsT, rhs, start, stop, *after):
        self.mm(out, lhsT[0], rhs[0], start, False, *after)
        self.mm(out, lhsT[0], rhs[1], False, False)
        return self.mm(out, lhsT[1], rhs[0], False, stop)

    def split(self, hi, lo, src, tok, *after, bias=None, q=None):
        if bias is None:
            t = self.cp(self.P.act, hi, src, tok, *after)
            u = self.tt(q or self.P.dve, lo, src, hi.bitcast(F32), ALU.subtract, t, *after)
        else:
            t = self.af(hi, src, ACT.Identity, tok, *after, bias=bias)
            u = self.stt(lo, src, bias, hi.bitcast(F32), ALU.add, ALU.subtract, t, *after)
        return [t, u]

    def dense(self, keys, rhs, out, *after, each=None, start=True, stop=True):
        n = len(keys)
        for i, (key, r) in enumerate(zip(keys, rhs)):
            w, wt = self.wblock(key)
            f = self.mms if isinstance(w, list) else self.mm
            t = f(out, w, r, start and i == 0, stop and i == n - 1, wt, *(after if i == 0 else ()), each[i] if each else None)
            self.wused(t)
        return t

    def dump(self, name, ap, *after):
        if name in self.dumps:
            s = self.P.dsem("dump_" + name)
            t = self.P.dma(self.P.sp, self.dumps[name], ap, s, *after)
            self.final.append(t)

    def rsqrt(self, out, src, eps, scale, *after, bias=None):
        t = self.af(out, src, ACT.Ln, *after, bias=eps, scale=scale)
        return self.af(out, out, ACT.Exp, t, scale=-0.5, bias=bias)

    def build(self, stop=None):
        nc, P = self.nc, self.P
        self.final = []
        ctx = ExitStack()
        with ctx:
            self.top = 1184

            def place(name, cols, *also):
                t = [nc.alloc_sbuf_tensor_at(n, [128, cols], dt, offset=self.top)
                     for n, dt in ((name, F32), *((a, F32R) for a in also))]
                self.top += -(-cols * 4 // 32) * 32
                return t if also else t[0]
            self.cst = place("cst", NCC)
            self.par = place("par", NPC)
            self.X = place("X", NT * T).reshape([128, NT, T])
            self.H, self.HR = (x.reshape([128, NT, T]) for x in place("H", NT * T, "HR"))
            self.ring = place("ring", RING * 1024)
            self.ring2 = nc.alloc_sbuf_tensor_at("ring2", [128, 4096], F32R, offset=self.top)
            self.top += 4096 * 4
            self.ada = place("ada", 48)
            self.nst = place("nst", 608)
            self.AF = (SBUF - self.top) // 4 // 8 * 8
            self.base, self.tiles = self.top, {}
            self.ar = place("arena", self.AF)
            banks = [ctx.enter_context(nc.psum_tensor(f"b{i}", [128, 512], F32)) for i in range(8)]
            self.banks = Banks(banks)
            self.units = self.d["ws"].shape[0]
            self.wsem = [P.dsem(f"w{i}") for i in range(RING)]
            self.t_spread = None
            self.wdma, self.wsplit, self.wlast = {}, {}, {}
            self.body(stop)
            assert stop or len(self.order) == 8 * self.units, (len(self.order), self.units)
            P.number()
            for q in (P.pe, P.act, P.dve, P.pool, P.sp):
                q.sem = ctx.enter_context(nc.semaphore("s_" + q.name))
            for s in P.dsems:
                s.sem = ctx.enter_context(nc.semaphore("d_" + s.name))
            block = ctx.enter_context(nc.Block())

            @block.sync
            def _(e):
                P.issue(P.sp, e)
                for s in P.dsems:
                    if s.count:
                        e.wait_ge(s.sem, s.count)

            @block.gpsimd
            def _(e):
                P.issue(P.pool, e)

            @block.scalar
            def _(e):
                P.issue(P.act, e)

            @block.vector
            def _(e):
                P.issue(P.dve, e)

            @block.tensor
            def _(e):
                P.issue(P.pe, e)
        return self.order

    def pair(self, kh, kl):
        out = []
        for k in (kh, kl):
            if k not in self.tiles:
                self.tiles[k] = self.nc.alloc_sbuf_tensor_at(f"tile{int(4 * k)}", [128, T], F32R,
                                                             offset=self.base + int(1024 * k))
            out.append(self.tiles[k][:, :])
        return out

    def region(self, kb, *shape):
        n = int(np.prod(shape))
        s = int(kb * 256)
        assert s + n <= self.AF, (kb, shape, self.AF)
        a = self.ar[:, s:s + n]
        if len(shape) == 1:
            return a
        names = "abcdef"[:len(shape)]
        return a.rearrange(f"p ({' '.join(names)}) -> p {' '.join(names)}", **{x: y for x, y in zip(names[1:], shape[1:])})

    def run(self, *gens):
        gens = [[g, w, 0] for g, w in gens]
        while gens:
            for x in list(gens):
                for _ in range(x[1]):
                    try:
                        next(x[0])
                    except StopIteration:
                        gens.remove(x)
                        break

    def body(self, stop):
        P = self.P
        sp = P.sp
        s0 = P.dsem("in0")
        t_par = P.dma(sp, self.par[:, :], self.d["par"], s0)
        t_cst = P.dma(sp, self.cst[:, :], self.d["cst"], s0)
        self.t_in = t_cst
        s1 = P.dsem("in1")
        for u in range(RING):
            self.load_unit(u)
        self.t_x = P.dma(sp, self.X[:, :, :], self.d["xT"], s1)
        self.block1(stop)
        if stop and stop.startswith("b1"):
            return
        self.layers(stop)

    def ada_tiles(self, a, b):
        i, ps, fr = self.banks.take()
        for n in range(a, b):
            rhs = [self.cact[:, k:k + 1] for k in range(8)]
            t = self.dense([("ada", n, k) for k in range(8)], rhs, ps[:, n - a:n - a + 1], self.t_cact, fr)
            fr = ()
            yield
        t = self.tt(self.P.dve, self.ada[:, a:b], ps[:, 0:b - a], self.pc("b_ada", a, b - a), ALU.add, t)
        self.banks.give(i, t)
        self.t_ada = t

    def ada_columns(self, a, b):
        P = self.P
        acc = [self.region(122, 1024), self.region(126, 1024)]
        i, ps, fr = self.banks.take()
        last = {}
        for g, n in enumerate(range(a, b, 8)):
            x = acc[g % 2]
            for k in range(8):
                w, wt = self.wblock([("ada", n + j, k) for j in range(8)], 8)
                c = self.cact[:, k:k + 1]
                if k == 0:
                    t = self.ts(P.dve, x, w, c, ALU.mult, None, None, wt, last.get(g - 2, self.t_z))
                else:
                    t = self.stt(x, w, c, x, ALU.mult, ALU.add, wt, t)
                self.wused(t)
                yield
            for j in range(8):
                m = self.mm(ps[:, n - a + j:n - a + j + 1], x[:, j * 128:j * 128 + 128], self.C("ones")[:, 0:1],
                            g == 0 and j == 0, True, t, fr)
            last[g] = m
            yield
        t = self.tt(P.dve, self.ada[:, a:b], ps[:, 0:b - a], self.pc("b_ada", a, b - a), ALU.add, m)
        self.banks.give(i, t)
        self.t_ada = t

    def norm_stats(self, tmp, *after):
        return {"tmp": tmp, "after": flat(after), "sums": []}

    def norm_tile(self, st, src, tok, gain=None):
        k = len(st["sums"])
        acc = st["tmp"][:, 2, :]
        sq = st["tmp"][:, k % 2, :] if k else acc
        w = st["sums"][k - 2] if k > 2 else st["after"]
        t = self.af(sq, src, ACT.Square, tok, w, scale=1.0 if gain is None else gain)
        if k:
            t = self.tt(self.P.dve, acc, acc, sq, ALU.add, t, st["sums"][-1])
        st["sums"].append(t)

    def token_sums(self, st):
        i, ps, fr = self.banks.take()
        for q in range(4):
            m = self.mm(ps[:, q:q + 1], st["tmp"][:, 2, q * 128:q * 128 + 128], self.C("ones")[:, 0:1], q == 0, True,
                        st["sums"][-1], fr)
        return i, ps, m

    def spread(self, r, t):
        D = self.nst[:, 8:520].rearrange("p (q t) -> p q t", q=4)
        t = self.tt(self.P.dve, D, self.C("ident").unsqueeze(1).broadcast_to((128, 4, 128)),
                    r.unsqueeze(2).broadcast_to((128, 4, 128)), ALU.mult, t, self.t_spread)
        i, ps, fr = self.banks.take()
        for q in range(4):
            m = self.mm(ps[:, q * 128:q * 128 + 128], self.C("ones"), D[:, q, :], q == 0, True, t, fr)
        self.t_spread = m
        return i, ps, m

    def norm_two(self, st, st2, src, gain, dst, gain2):
        P = self.P
        r, r2, e = self.nst[:, 0:4], self.nst[:, 4:8], self.nst[:, 604:608]
        i, ps, m = self.token_sums(st)
        i2, ps2, m2 = self.token_sums(st2)
        t = self.ts(P.dve, r, ps[:, 0:4], 1.0 / 1024, ALU.mult, 1e-6, ALU.add, m)
        self.banks.give(i, t)
        t = self.af(r, r, ACT.Sqrt, t)
        t = P.dve.do(lambda q: q.reciprocal(r, r), t)
        u = self.tt(P.dve, e, r, r, ALU.mult, t)
        u = self.tt(P.dve, r2, ps2[:, 0:4], e, ALU.mult, u, m2)
        self.banks.give(i2, u)
        u = self.ts(P.dve, r2, r2, 1.0 / 1024, ALU.mult, 1e-6, ALU.add, u)
        u = self.af(r2, r2, ACT.Sqrt, u)
        i, ps, m = self.spread(r, t)
        u = P.dve.do(lambda q: q.reciprocal(r2, r2), u)
        i2, ps2, m2 = self.spread(r2, u)
        xs, outs = [], []
        for k in range(8):
            xs.append(self.stt(src[k], src[k], gain[k], ps[:, :], ALU.mult, ALU.mult, m))
            x = st["tmp"][:, k % 2, :]
            u = self.stt(x, src[k], gain2[k], ps2[:, :], ALU.mult, ALU.mult, m2, xs[k], outs[k - 2] if k >= 2 else None)
            outs.append(self.split(*dst[k], x, u, q=P.pool if k % 2 else None))
        self.banks.give(i, u)
        self.banks.give(i2, u)
        return xs, outs

    def norm_apply(self, st, src, dst, gain, shift=None, after=None):
        P = self.P
        i, ps, m = self.token_sums(st)
        r = self.nst[:, 0:4]
        t = self.ts(P.dve, r, ps[:, 0:4], 1.0 / (128 * len(src)), ALU.mult, 1e-6, ALU.add, m)
        self.banks.give(i, t)
        t = self.af(r, r, ACT.Sqrt, t)
        t = P.dve.do(lambda e: e.reciprocal(r, r), t)
        i, ps, m = self.spread(r, t)
        outs = []
        for k in range(len(src)):
            if not isinstance(dst[k], list):
                outs.append(self.stt(dst[k], src[k], gain[k], ps[:, :], ALU.mult, ALU.mult, m, after))
                continue
            x = st["tmp"][:, k % 2, :]
            u = self.stt(x, src[k], gain[k], ps[:, :], ALU.mult, ALU.mult, m, after, outs[k - 2] if k >= 2 else None)
            outs.append(self.split(*dst[k], x, u, after, bias=shift[k] if shift else None,
                                   q=P.pool if k % 2 and not shift else None))
        self.banks.give(i, P.dve.last)
        return outs

    def block1(self, stop):
        P = self.P
        dve, act, pool, sp = P.dve, P.act, P.pool, P.sp
        R = self.region
        self.cact = self.nst[:, 528:536]
        t = self.af(self.cact, self.pc("c", 0, 8), ACT.Silu, self.t_in)
        self.t_cact = t
        s = P.dsem("s5w")
        self.s5p = R(124, 4, 256)
        self.t_s5p = P.dma(sp, self.s5p, self.d["s5p"], s)
        X = [self.X[:, k, :] for k in range(8)]
        Hs = self.Hs = [[self.HR[:, k, :], self.pair(0, 132.25 + 2 * k)[1]] for k in range(8)]
        st = self.norm_stats(R(104, 3, 512))
        self.run((self.ada_tiles(0, 16), 1), (self.s5_tables(), 3),
                 ((self.norm_tile(st, X[k], self.t_x) for k in range(8)), 1))
        one_sc = self.nst[:, 536:544]
        self.ts(dve, one_sc, self.ada[:, 8:16], 1.0, ALU.add, None, None, self.t_ada)
        t_h = self.norm_apply(st, X, Hs, [one_sc[:, k:k + 1] for k in range(8)], [self.ada[:, k:k + 1] for k in range(8)])
        if stop == "b1h":
            return
        U = R(110, 4, 8, 64)
        self.U = U
        self.t_u = []
        for n in range(4):
            i, ps, fr = self.banks.take()
            t = self.dense([("in", 14 + n, k) for k in range(8)], Hs, ps[:, :], fr, each=t_h)
            t = self.cp(dve, U[:, n, :, :], ps[:, :].rearrange("p (j t) -> p t j", t=8), t)
            self.banks.give(i, t)
            self.t_u.append(t)
        self.s5_matrices()
        self.dump("u", R(110, 2048), self.t_u)
        parts = {"i": self.in_proj(Hs), "s": self.s5_apply()}
        for c in ORDER:
            next(parts[c], None)
        self.run((parts["i"], 1), (parts["s"], 1))
        self.dump("zs", R(0, 14 * 512), self.t_z)
        self.dump("ys5", R(28, 2048), self.t_os)
        if stop == "b1s5":
            return
        self.run((self.rwkv(stop), 2), (self.ada_columns(16, 48), 1))
        self.dump("yr", self.region(0, 2048), self.t_yr)
        if stop == "b1rw":
            return
        ys = self.ysp
        each = self.t_ysp
        t_x1 = []
        st = self.norm_stats(R(120, 3, 512), self.t_yr, self.t_ada)
        for n in range(8):
            i, ps, fr = self.banks.take()
            t = self.dense([("out", n, k) for k in range(8)], ys, ps[:, :], fr, each=each)
            t = self.stt(X[n], ps[:, :], self.ada[:, 16 + n:17 + n], X[n], ALU.mult, ALU.add, t, self.t_ada, self.t_x)
            self.banks.give(i, t)
            t_x1.append(t)
            if n:
                self.norm_tile(st, X[n - 1], t_x1[n - 1])
        self.dump("x1", self.X[:, :, :], t_x1)
        if stop == "b1x":
            return
        one_sc = self.nst[:, 536:544]
        t1 = self.ts(dve, one_sc, self.ada[:, 32:40], 1.0, ALU.add, None, None, self.t_ada, t_x1)
        self.norm_tile(st, X[7], t_x1[7])
        t_h = self.norm_apply(st, X, Hs, [one_sc[:, k:k + 1] for k in range(8)],
                              [self.ada[:, 24 + k:25 + k] for k in range(8)])
        at = [2 * i for i in range(12)] + [33 + 2 * i for i in range(38)]
        G = [self.pair(at[2 * n], at[2 * n + 1]) for n in range(DFF_T)]
        SB, GT = [R(97 + 2 * j, 512) for j in (0, 1)], [R(101 + 2 * j, 512) for j in (0, 1)]
        t_g, t_raw = [], []
        for n in range(DFF_T):
            i, ps, fr = self.banks.take()
            t = self.dense([("gate", n, k) for k in range(8)], Hs, ps[:, :], fr, each=t_h)
            ta = self.af(SB[n % 2], ps[:, :], ACT.Silu, t, t_raw[n - 2] if n >= 2 else t_x1)
            self.banks.give(i, ta)
            i, ps, fr = self.banks.take()
            t = self.dense([("up", n, k) for k in range(8)], Hs, ps[:, :], fr)
            t = self.tt(dve, GT[n % 2], ps[:, :], SB[n % 2], ALU.mult, t, ta, t_g[n - 2] if n >= 2 else t_x1)
            self.banks.give(i, t)
            t_raw.append(t)
            t_g.append(self.split(*G[n], GT[n % 2], t, t_x1, q=pool))
        self.load_lw(t)
        t_x2 = []
        st, st2 = self.norm_stats(R(120, 3, 512), t_h, self.t_z), self.norm_stats(R(126, 3, 512), t_h, self.t_z)
        for n in range(8):
            i, ps, fr = self.banks.take()
            t = self.dense([("down", n, k) for k in range(DFF_T)], G, ps[:, :], fr, each=t_g)
            t = self.stt(X[n], ps[:, :], self.ada[:, 40 + n:41 + n], X[n], ALU.mult, ALU.add, t)
            self.banks.give(i, t)
            t_x2.append(t)
            if n:
                self.norm_tile(st, X[n - 1], t_x2[n - 1])
                self.norm_tile(st2, X[n - 1], t_x2[n - 1], self.pc("fgain", n - 1))
        self.norm_tile(st, X[7], t_x2[7])
        self.norm_tile(st2, X[7], t_x2[7], self.pc("fgain", 7))
        self.load_layer_tables(t)
        self.t_X, self.t_h0 = self.norm_two(st, st2, X, [self.pc("fgain", k) for k in range(8)], Hs,
                                            [self.pc("ng0", k) for k in range(8)])
        self.dump("x2", self.X[:, :, :], self.t_X)

    def s5_tables(self):
        P = self.P
        dve, act, pool, sp = P.dve, P.act, P.pool, P.sp
        R = self.region
        V = lambda out, a, b, op, *w: self.tt(dve, out, a, b, op, *w)
        S = lambda out, a, s1, o1, s2, o2, *w: self.ts(dve, out, a, s1, o1, s2, o2, *w)
        sm = R(130.5, 24, 16)
        dt, xr, mag, xi, kf, r, sn, cs, den, pr_, cr, ci, t1, t2, t3, t4, cc, sg = (sm[:, i, :] for i in range(18))
        PR, PI = R(28, 16, 9), R(29, 16, 9)
        are, aim, ldt = self.pc("are", 0, 16), self.pc("aim", 0, 16), self.pc("ldt", 0, 16)
        a = self.af(dt, ldt, ACT.Exp, self.t_in)
        a = V(xr, dt, are, ALU.mult, a)
        b = V(xi, dt, aim, ALU.mult)
        a = self.af(mag, xr, ACT.Exp, a)
        M = 12582912.0
        b = S(kf, xi, 1.0 / (2 * math.pi), ALU.mult, M, ALU.add, b)
        b = S(kf, kf, -M, ALU.add, None, None, b)
        c1 = 6.28125
        c2 = float(np.float32(np.round((2 * math.pi - c1) * 2 ** 22) / 2 ** 22))
        c3 = float(np.float32(2 * math.pi - c1 - c2))
        b = self.stt(r, kf, -c1, xi, ALU.mult, ALU.add, b)
        b = self.stt(r, kf, -c2, r, ALU.mult, ALU.add, b)
        b = self.stt(r, kf, -c3, r, ALU.mult, ALU.add, b)
        PIF = 3.14159250
        c = S(cc, r, math.pi / 2, ALU.add, None, None, b)
        d_ = S(t1, cc, math.pi, ALU.is_gt, -2 * math.pi, ALU.mult, c)
        c = V(cc, cc, t1, ALU.add, d_)
        c = S(cc, cc, PIF, ALU.min, -PIF, ALU.max, c)
        b = S(r, r, PIF, ALU.min, -PIF, ALU.max, b)
        yield
        b = self.af(sn, r, ACT.Sin, b)
        c = self.af(cs, cc, ACT.Sin, c)
        c = V(PR[:, :, 1], mag, cs, ALU.mult, c, a)
        b = V(PI[:, :, 1], mag, sn, ALU.mult, b)
        b = dve.do(lambda e: e.memset(PR[:, :, 0], 1.0))
        b = dve.do(lambda e: e.memset(PI[:, :, 0], 0.0))
        yield
        t = V(t1, are, are, ALU.mult)
        u = V(t2, aim, aim, ALU.mult)
        t = V(den, t1, t2, ALU.add, t, u)
        t = dve.do(lambda e: e.reciprocal(den, den), t)
        w = S(pr_, PR[:, :, 1], -1.0, ALU.add, None, None, c)
        x1 = V(t1, pr_, are, ALU.mult, w)
        x2 = V(t2, PI[:, :, 1], aim, ALU.mult, b)
        x3 = V(t3, PI[:, :, 1], are, ALU.mult)
        x4 = V(t4, pr_, aim, ALU.mult)
        x1 = V(t1, t1, t2, ALU.add, x1, x2)
        x3 = V(t3, t3, t4, ALU.subtract, x3, x4)
        x1 = V(cr, t1, den, ALU.mult, x1, t)
        x3 = V(ci, t3, den, ALU.mult, x3)
        yield
        def bc(ap, n):
            return ap.unsqueeze(2).broadcast_to((128, 16, n))

        q1, q2 = sm[:, 20, :], sm[:, 21, :]
        tm = R(30, 4, 16, 4)
        last = x3
        for lo, n in ((1, 1), (2, 2), (4, 4)):
            ar_, ai_ = bc(PR[:, :, lo], n), bc(PI[:, :, lo], n)
            br_, bi_ = PR[:, :, 1:1 + n], PI[:, :, 1:1 + n]
            y = [V(tm[:, i, :, 0:n], p, q_, ALU.mult, last)
                 for i, (p, q_) in enumerate(((br_, ar_), (bi_, ai_), (br_, ai_), (bi_, ar_)))]
            y1 = V(PR[:, :, lo + 1:lo + 1 + n], tm[:, 0, :, 0:n], tm[:, 1, :, 0:n], ALU.subtract, y)
            last = V(PI[:, :, lo + 1:lo + 1 + n], tm[:, 2, :, 0:n], tm[:, 3, :, 0:n], ALU.add, y1)
            yield
        P8R, P8I = R(33.5, 8, 16), R(34, 8, 16)
        self.P8R, self.P8I = P8R, P8I
        t = self.cp(dve, P8R[:, 0, :], PR[:, :, 8], last)
        t = self.cp(dve, P8I[:, 0, :], PI[:, :, 8], t)
        tm2 = R(31, 4, 4, 16)
        for lo, n in ((1, 1), (2, 2), (4, 4)):
            def bb(ap):
                return ap.unsqueeze(1).broadcast_to((128, n, 16))
            ar_, ai_ = bb(P8R[:, lo - 1, :]), bb(P8I[:, lo - 1, :])
            br_, bi_ = P8R[:, 0:n, :], P8I[:, 0:n, :]
            y = [V(tm2[:, i, 0:n, :], p, q_, ALU.mult, t)
                 for i, (p, q_) in enumerate(((br_, ar_), (bi_, ai_), (br_, ai_), (bi_, ar_)))]
            y1 = V(P8R[:, lo:lo + n, :], tm2[:, 0, 0:n, :], tm2[:, 1, 0:n, :], ALU.subtract, y)
            t = V(P8I[:, lo:lo + n, :], tm2[:, 2, 0:n, :], tm2[:, 3, 0:n, :], ALU.add, y1)
            yield
        t_p8 = t
        BB = R(16, 2, 16, 16)
        self.BB = BB
        bt = R(18, 2, 16, 16)
        bre, bim, cre, cim = (self.s5p[:, i, :].rearrange("p (g c) -> p g c", g=16) for i in range(4))
        crb, cib = bc(cr, 16), bc(ci, 16)
        y1 = V(bt[:, 0], crb, bre, ALU.mult, x1, x3, self.t_s5p)
        y2 = V(bt[:, 1], cib, bim, ALU.mult)
        y = V(BB[:, 0], bt[:, 0], bt[:, 1], ALU.subtract, y1, y2)
        y1 = V(bt[:, 0], crb, bim, ALU.mult, y)
        y2 = V(bt[:, 1], cib, bre, ALU.mult)
        t_bb = V(BB[:, 1], bt[:, 0], bt[:, 1], ALU.add, y1, y2)
        yield
        W = R(76, 2, 16, 9, 16)
        self.W = W
        wt = R(36, 2, 16, 9, 16)

        def b4(ap, n):
            return ap.unsqueeze(3).broadcast_to((128, 16, n, 16))

        def c4(ap, n):
            return ap.unsqueeze(2).broadcast_to((128, 16, n, 16))
        VT = R(0, 2, 16, 8, 16)
        vt = R(62, 16, 8, 16)
        t = None
        tws = []
        for ri in range(2):
            (pa, ca), (pb_, cb) = (((PR, cre), (PI, cim)) if ri == 0 else ((PI, cre), (PR, cim)))
            for g in range(0, 16, 4):
                gs = slice(g, g + 4)
                w1 = V(wt[:, 0, gs], pa[:, gs].unsqueeze(3).broadcast_to((128, 4, 9, 16)),
                       ca[:, gs].unsqueeze(2).broadcast_to((128, 4, 9, 16)), ALU.mult, last, t)
                w2 = V(wt[:, 1, gs], pb_[:, gs].unsqueeze(3).broadcast_to((128, 4, 9, 16)),
                       cb[:, gs].unsqueeze(2).broadcast_to((128, 4, 9, 16)), ALU.mult, t)
                if ri == 0:
                    t = V(W[:, 0, gs], wt[:, 0, gs], wt[:, 1, gs], ALU.subtract, w1, w2)
                else:
                    t = self.stt(W[:, 1, gs].rearrange("p g d c -> p (g d c)"),
                                 wt[:, 0, gs].rearrange("p g d c -> p (g d c)"), -1.0,
                                 wt[:, 1, gs].rearrange("p g d c -> p (g d c)"), ALU.mult, ALU.subtract, w1, w2)
                tws.append(t)
                yield
        self.t_w = tws
        tv = {}
        t = t_bb
        for ri in range(2):
            br_, bi_ = BB[:, 0], BB[:, 1]
            (pa, ca), (pb_, cb) = (((PR, br_), (PI, bi_)) if ri == 0 else ((PR, bi_), (PI, br_)))
            for g in range(0, 16, 4):
                gs = slice(g, g + 4)
                w1 = V(VT[:, ri, gs], pa[:, gs, 0:8].unsqueeze(3).broadcast_to((128, 4, 8, 16)),
                       ca[:, gs].unsqueeze(2).broadcast_to((128, 4, 8, 16)), ALU.mult, t)
                w2 = V(vt[:, gs], pb_[:, gs, 0:8].unsqueeze(3).broadcast_to((128, 4, 8, 16)),
                       cb[:, gs].unsqueeze(2).broadcast_to((128, 4, 8, 16)), ALU.mult, t)
                t = V(VT[:, ri, gs], VT[:, ri, gs], vt[:, gs], ALU.subtract if ri == 0 else ALU.add, w1, w2)
                tv[ri, g] = t
                yield
        self.tb = BB, W, VT, t_bb, tws, tv, t_p8

    def s5_matrices(self):
        P = self.P
        dve, act, pool, sp = P.dve, P.act, P.pool, P.sp
        R = self.region
        BB, W, VT, t_bb, tws, tv, t_p8 = self.tb
        KS = R(36, 32, 240)
        t_z = pool.do(lambda e: e.memset(KS[0:16, :, 0:112], 0.0), tws, tv[1, 12])
        t_ks = []
        for g4 in range(8):
            i, ps, fr = self.banks.take()
            for gp in range(4 * (g4 // 2), 4 * (g4 // 2) + 4):
                par = 64 * (g4 % 2)
                o = ps[0:16, (gp % 4) * 128:(gp % 4) * 128 + 128]
                for ri in range(2):
                    t = self.mm(o, BB[par:par + 64, ri, gp, :],
                                W[par:par + 64, ri, gp, 0:8, :].rearrange("p d c -> p (d c)"),
                                ri == 0, ri == 1, t_bb, tws, fr)
            g0 = 8 * (g4 // 2) + g4 % 2
            t = self.cp(act, KS[0:16, g0:g0 + 7:2, 112:240], ps[0:16, :].rearrange("p (g d) -> p g d", g=4), t, tv[1, 12])
            self.banks.give(i, t)
            t_ks.append(t)
        kd = self.d["kpad"]
        sk = P.dsem("kpad")
        t_kd = P.dma(sp, kd.rearrange("g c n -> c g n"), KS[0:16, :, :], sk, t_ks, t_z)
        TT = R(44, 32, 128)
        self.TT = TT
        self.stt_, self.t_kd = P.dsem("tt"), [t_kd, tws[-1], tv[1, 12]]
        VM = R(60, 16, 2, 128)
        self.VM = VM
        t_vm = []
        for g in range(0, 16, 2):
            i, ps, fr = self.banks.take()
            for gg in (g, g + 1):
                for ri in range(2):
                    o = ((gg - g) * 2 + ri) * 128
                    t = self.tr(ps[:, o:o + 128], VT[:, ri, gg].rearrange("p d c -> p (d c)"), tv[1, 12], fr)
            t = self.cp(act if g % 4 else dve, VM[:, g:g + 2].rearrange("p a b c -> p (a b c)"), ps[:, :], t, t_kd)
            self.banks.give(i, t)
            t_vm.append(t)
        self.t_vm = t_vm
        self.t_tab = [t_vm, t_p8, t_kd, t_ks]
        self.t_tabc = [t_vm, t_ks, tws, tv[1, 12]]
        self.t_tab_mm = t_vm[-1]

    def in_proj(self, Hs):
        P = self.P
        ZB = self.region(0, 14, 512)
        self.ZB = ZB
        TMP = self.region(126, 2, 516)
        omm = self.nst[:, 544:558]
        t_o = self.ts(P.dve, omm, self.pc("mu", 0, 14), -1.0, ALU.mult, 1.0, ALU.add, self.t_tabc, self.t_u)
        z = [P.pool.do(lambda e, j=j: e.memset(TMP[:, j, 0:1], 0.0), self.t_tabc, self.t_u) for j in range(2)]
        self.t_z = []
        for m, n in enumerate([12, 13, 4, 5, 6, 7, 0, 1, 2, 3, 8, 9, 10, 11]):
            i, ps, fr = self.banks.take()
            t = self.dense([("in", n, k) for k in range(8)], Hs, ps[:, :], fr)
            tmp = TMP[:, m % 2, :]
            ta = self.af(tmp[:, 1:513], ps[:, :], ACT.Copy, t, self.t_z[m - 2] if m >= 2 else z,
                         scale=self.pc("mu", n))
            tb = self.stt(ZB[:, n, :], ps[:, :], omm[:, n:n + 1], tmp[:, 0:512], ALU.mult, ALU.add, ta, t_o, z)
            self.banks.give(i, tb)
            self.t_z.append(tb)
            yield
        self.t_hfree = t

    def s5_apply(self):
        P = self.P
        dve, act, pool, sp = P.dve, P.act, P.pool, P.sp
        R = self.region
        U, TT, VM, W = self.U, self.TT, self.VM, self.W
        UG = R(36, 32, 64)
        ud = self.d["ud"]
        s = P.dsem("ud")
        t = P.dma(sp, ud.rearrange("(gt g) c t j -> (g c) gt (t j)", gt=4),
                  U.rearrange("p a t j -> p a (t j)"), s, self.t_u)
        s = P.dsem("ug")
        yield
        for dl in range(8):
            if dl == 4:
                yield
            t_ug = P.dma(sp, UG[16 * dl:16 * dl + 16, :, :], ud[:, :, 7 - dl, :].rearrange("g c j -> c g j"),
                         s, t, self.t_w, self.t_tab)
        yield
        S = R(94, 2, 16, 64)
        t_e = []
        for ri in range(2):
            for h in range(2):
                i, ps, fr = self.banks.take()
                for g in range(16 * h, 16 * h + 16):
                    gp, par = g // 2, 64 * (g % 2)
                    t = self.mm(ps[par:par + 64, (gp - 8 * h) * 64:(gp - 8 * h) * 64 + 64],
                                VM[:, gp, ri, par:par + 64], UG[:, g, :], True, True, t_ug, self.t_vm, fr)
                t = self.cp(act, S[:, ri, 8 * h:8 * h + 8, :].rearrange("p a j -> p (a j)"), ps[:, :], t)
                self.banks.give(i, t)
                t_e.append(t)
                yield
        Sv = S.rearrange("p r g (b i) -> p r g b i", i=8)
        T1, T2 = R(102, 2, 16, 8), R(103, 2, 16, 8)
        P8R, P8I = self.P8R, self.P8I
        V = lambda out, a, b, op, *w: self.tt(dve, out, a, b, op, *w)

        def cstep(dst, src, wr, wi, T1, T2, *w):
            a = V(T1[:, 0], src[:, 0], wr, ALU.mult, *w)
            a = V(T1[:, 1], src[:, 1], wr, ALU.mult)
            b = V(T2[:, 0], src[:, 1], wi, ALU.mult)
            c = V(T2[:, 1], src[:, 0], wi, ALU.mult)
            a = V(dst[:, 0], dst[:, 0], T1[:, 0], ALU.add, a)
            b = V(dst[:, 1], dst[:, 1], T1[:, 1], ALU.add)
            a = V(dst[:, 0], dst[:, 0], T2[:, 0], ALU.subtract, a, c)
            b = V(dst[:, 1], dst[:, 1], T2[:, 1], ALU.add, b)
            return b
        t = t_e
        w8r = P8R[:, 0, :].unsqueeze(2).broadcast_to((128, 16, 8))
        w8i = P8I[:, 0, :].unsqueeze(2).broadcast_to((128, 16, 8))
        for k in range(1, 8):
            for dl in (2 * k - 2, 2 * k - 1) if k <= 4 else ():
                self.t_tt = P.dma(sp, TT[16 * dl:16 * dl + 16, :, :],
                                  self.d["kpad"][:, :, 16 * dl:16 * dl + 128].rearrange("g c n -> c g n"),
                                  self.stt_, self.t_kd)
            t = cstep(Sv[:, :, :, :, k], Sv[:, :, :, :, k - 1], w8r, w8i, T1, T2, t)
            yield
        for b in range(1, 8):
            t = cstep(Sv[:, :, :, b, 7], Sv[:, :, :, b - 1, 7], P8R[:, 7, :], P8I[:, 7, :],
                      T1[:, :, :, 0], T2[:, :, :, 0], t)
        yield
        for k in range(7):
            wr = P8R[:, k, :].unsqueeze(2).broadcast_to((128, 16, 7))
            wi = P8I[:, k, :].unsqueeze(2).broadcast_to((128, 16, 7))
            X1, X2 = R(102, 2, 16, 7), R(103, 2, 16, 7)
            t = cstep(Sv[:, :, :, 1:8, k], Sv[:, :, :, 0:7, 7], wr, wi, X1, X2, t)
            yield
        t_s = t
        YG = UG
        t_yg = []
        for q in range(4):
            i, ps, fr = self.banks.take()
            for gp in range(8 * (q // 2), 8 * (q // 2) + 8):
                g, par = 2 * gp + q % 2, 64 * (q % 2)
                o = (gp % 8) * 64
                self.mm(ps[:, o:o + 64], TT[:, g, :], UG[:, g, :], True, False, self.t_tt, t_ug, fr)
                for ri in range(2):
                    t = self.mm(ps[:, o + 1:o + 64], W[par:par + 64, ri, gp, 1:9, :].rearrange("p d c -> p (d c)"),
                                S[par:par + 64, ri, gp, 0:63], False, ri == 1, t_s)
            g0 = 16 * (q // 2) + q % 2
            t = self.cp(act, YG[:, g0:g0 + 15:2, :], ps[:, :].rearrange("p (g j) -> p g j", g=8), t)
            self.banks.give(i, t)
            t_yg.append(t)
            yield
        yd = self.d["yd"]
        s = P.dsem("yd")
        for tau in range(8):
            t = P.dma(sp, yd[:, :, tau, :].rearrange("g c j -> c g j"), YG[16 * tau:16 * tau + 16, :, :], s, t_yg)
        YS = R(118, 4, 512)
        s = P.dsem("ys")
        t_ys = P.dma(sp, YS, yd.rearrange("(gt g) c t j -> (g c) gt (t j)", gt=4), s, t)
        yield
        Z = R(44, 4, 512)
        t_z = []
        for n in range(4):
            t = self.stt(YS[:, n, :], U[:, n].rearrange("p t j -> p (t j)"), self.pc("s5d", n), YS[:, n, :],
                         ALU.mult, ALU.add, t_ys)
            t = self.af(Z[:, n, :], YS[:, n, :], ACT.Gelu_apprx_tanh, t, t_yg)
            t_z.append(t)
        ZP = [self.pair(60 + 2 * n, 68 + 2 * n) for n in range(4)]
        t_zp = [self.split(*ZP[n], Z[:, n, :], t_z[n], t_yg) for n in range(4)]
        yield
        OZ = R(52, 4, 512)
        t_oz = []
        for n in range(4):
            i, ps, fr = self.banks.take()
            t = self.dense([("glu", n, k) for k in range(4)], ZP, ps[:, :], fr, each=t_zp)
            t = self.af(YS[:, n, :], ps[:, :], ACT.Sigmoid, t, bias=self.pc("bglu", n))
            self.banks.give(i, t)
            t = self.tt(dve, OZ[:, n, :], Z[:, n, :], YS[:, n, :], ALU.mult, t)
            t_oz.append(t)
            yield
        self.small = R(118, 2, 512)
        s = P.dsem("small")
        self.t_small = P.dma(sp, self.small, self.d["small"], s, t_oz)
        OS = R(28, 4, 512)
        dst = [OS[:, n, :].rearrange("p (j t) -> p t j", t=8) for n in range(4)]
        tmp = R(104, 3, 512)
        t_r = self.norm_r([OZ[:, n, :] for n in range(4)], t_oz, 512, tmp)
        rr = tmp[:, 2, :].rearrange("p (t j) -> p t j", t=8)
        self.t_os = [self.stt(dst[n], OZ[:, n, :].rearrange("p (t j) -> p t j", t=8), self.pc("gain", n), rr,
                              ALU.mult, ALU.mult, t_r) for n in range(4)]

    def norm_r(self, src, t_src, feats, tmp, tmp_free=()):
        P = self.P
        i, ps, fr = self.banks.take()
        mms = []
        n = len(src)
        for k in range(n):
            sq = tmp[:, k % 2, :]
            w = mms[k - 2] if k >= 2 else tmp_free
            t = self.tt(P.pool, sq, src[k], src[k], ALU.mult, t_src[k], w)
            mms.append(self.mm(ps[:, :], self.C("ones"), sq, k == 0, k == n - 1, t, fr if k == 0 else ()))
        t = self.rsqrt(tmp[:, 2, :], ps[:, :], self.kc(EPS6), 1.0 / feats, mms[-1], tmp_free)
        self.banks.give(i, t)
        return t

    def rwkv(self, stop):
        P = self.P
        dve, act, pool = P.dve, P.act, P.pool
        R = self.region
        ZB = self.ZB
        CE = math.exp(-0.5)
        V = lambda out, a, b, op, *w: self.tt(dve, out, a, b, op, *w)
        G = lambda out, a, b, op, *w: self.tt(pool, out, a, b, op, *w)
        tz, to, hf = self.t_z, self.t_os, self.t_hfree
        SG, AS = self.H[:, 0:4, :], self.H[:, 4:8, :]
        w2, g2 = self.small[:, 0, :], self.small[:, 1, :]
        t = self.af(ZB[0:64, 12, :], ZB[0:64, 12, :], ACT.Tanh, tz)
        t_gl = self.af(ZB[:, 13, :], ZB[:, 13, :], ACT.Sigmoid, tz)
        t_sg, t_as = [], []
        for n in range(4):
            i, ps, fr = self.banks.take()
            m = self.mm(ps[:, :], w2[0:64, n * 128:n * 128 + 128], ZB[0:64, 12, :], True, True, t, fr, self.t_small)
            x = self.af(SG[:, n, :], ps[:, :], ACT.Sigmoid, m, hf, bias=self.pc("w0", n))
            self.banks.give(i, x)
            t_sg.append(x)
            i, ps, fr = self.banks.take()
            m = self.mm(ps[:, :], w2[64:128, n * 128:n * 128 + 128], ZB[64:128, 12, :], True, True, fr)
            x = self.af(AS[:, n, :], ps[:, :], ACT.Sigmoid, m, hf, bias=self.pc("a0", n))
            self.banks.give(i, x)
            t_as.append(x)
            yield
        omk = self.nst[:, 560:564]
        t_omk = self.ts(dve, omk, self.pc("k_a", 0, 4), -1.0, ALU.mult, 1.0, ALU.add, to)
        AR = R(36, 4, 8, 2, 64)
        B = R(52, 4, 512)
        GC = self.nst[:, 572:604].rearrange("p (n c) -> p n c", n=4)
        E = R(68, 8, 512)
        t_ar, t_b, t_k, t_bv = [], [], [], []
        last_e = [to, None]
        RK, KK = [ZB[:, n, :] for n in range(4)], [ZB[:, 4 + n, :] for n in range(4)]
        VV = [ZB[:, 8 + n, :] for n in range(4)]
        v8 = lambda ap: ap.rearrange("p (c t) -> p c t", t=64)
        for half in range(2):
            W = []
            for n in (2 * half, 2 * half + 1):
                W.append((n, [R(68 + 16 * (n % 2), 8, 512)[:, i, :] for i in range(8)], last_e[n % 2] if half else to, {}))
            for n, (cs, gam, ig, gp, x, y, z_, q), le, t in W:
                t["cs"] = dve.do(lambda e, cs=cs, n=n: e.tensor_tensor_scan(out=cs, data0=self.C("scan"),
                                 data1=SG[:, n, :], initial=0.0, op0=ALU.mult, op1=ALU.add), t_sg[n], le)
                t["x"] = self.ts(dve, x, KK[n], self.pc("k_k", n), ALU.mult, None, None, tz, le)
                t["y"] = G(y, x, x, ALU.mult, t["x"])
            for n, (cs, gam, ig, gp, x, y, z_, q), le, t in W:
                t["g"] = self.af(gam, cs, ACT.Exp, t["cs"], le, scale=-CE)
                t["ig"] = self.af(ig, cs, ACT.Exp, t["cs"], le, scale=CE)
                t["gp"] = G(gp, cs, SG[:, n, :], ALU.subtract, t["cs"], t_sg[n], le)
                i, ps, fr = self.banks.take()
                m = self.mm(ps[:, :], self.C("blk"), y, True, True, t["y"], fr)
                c = self.ts(dve, z_, ps[:, :], 2.0 ** 20, ALU.mult, 1e-24 * 2 ** 20, ALU.max, m, le)
                self.banks.give(i, c)
                t["z"], t["m"] = c, m
            yield
            for n, (cs, gam, ig, gp, x, y, z_, q), le, t in W:
                t["gp"] = self.af(gp, gp, ACT.Exp, t["gp"], scale=-CE)
                t["q"] = self.ts(dve, q, AS[:, n, :], self.pc("k_a", n), ALU.mult, omk[:, n:n + 1], ALU.add,
                                 t_as[n], t_omk, le)
                t["gc"] = self.cp(dve, GC[:, n, :], v8(gam)[:, :, 63], t["g"], to)
            for n, (cs, gam, ig, gp, x, y, z_, q), le, t in W:
                t["z"] = self.af(z_, z_, ACT.Ln, t["z"])
                t["k"] = G(KK[n], KK[n], q, ALU.mult, t["q"], t["x"])
            for n, (cs, gam, ig, gp, x, y, z_, q), le, t in W:
                t["z"] = self.af(z_, z_, ACT.Exp, t["z"], scale=-0.5, bias=self.kc(TENLN2))
            yield
            for n, (cs, gam, ig, gp, x, y, z_, q), le, t in W:
                t["rk"] = self.stt(q, RK[n], self.pc("r_k", n), KK[n], ALU.mult, ALU.mult, t["k"])
                i, ps, fr = self.banks.take()
                m = self.mm(ps[:, :], self.C("blk"), q, True, True, t["rk"], fr)
                t["bv"] = (i, ps, m)
                t["r"] = V(AR[:, n, :, 1, :], v8(RK[n]), v8(gam), ALU.mult, t["g"], t["rk"])
            for n, (cs, gam, ig, gp, x, y, z_, q), le, t in W:
                t["kk"] = V(x, x, z_, ALU.mult, t["z"], t["y"])
                t["y"] = G(y, x, AS[:, n, :], ALU.mult, t["kk"], t["m"], t_as[n])
                t["a"] = self.stt(AR[:, n, :, 0, :], v8(x), -1.0, v8(gp), ALU.mult, ALU.mult, t["kk"], t["gp"])
            yield
            for n, (cs, gam, ig, gp, x, y, z_, q), le, t in W:
                i, ps, m = t["bv"]
                t["bv"] = V(self.H[:, n, :], VV[n], ps[:, :], ALU.mult, m, t["gp"], t["cs"])
                self.banks.give(i, t["bv"])
                t["b"] = V(B[:, n, :], y, ig, ALU.mult, t["y"], t["ig"])
                t["kg"] = G(KK[n], KK[n], ig, ALU.mult, t["rk"], t["ig"])
                t_ar += [t["a"], t["r"]]
                t_b.append(t["b"])
                t_k.append(t["kg"])
                t_bv.append(t["bv"])
                last_e[n % 2] = [t["kg"], t["b"], t["a"], t["r"], t["bv"], t["gc"]]
            yield
        ew = [t_ar, t_b, t_k, t_bv, last_e]
        self.dump("ar", R(36, 4096), ew)
        M, LT, LL, PP, MT, KA, BR, KR = (R(x, 4, 512) for x in (68, 76, 84, 92, 100, 108, 132.25, 140.25))
        mk = lambda name: self.C(name).unsqueeze(1).broadcast_to((128, 8, 64))
        h8 = lambda ap: ap.rearrange("p (h t) -> p h t", t=64)
        tM, tMT, tLT, tKA, tBR, tKR = {}, {}, {}, {}, {}, {}
        for pp in range(2):
            for hp in (0, 64):
                i, ps, fr = self.banks.take()
                for p in range(2 * pp, 2 * pp + 2):
                    for n in range(4):
                        for par in range(2):
                            c, o = 2 * p + par, (p % 2) * 256 + n * 64
                            t = self.mm(ps[64 * par:64 * par + 64, o:o + 64], AR[hp:hp + 64, n, c, 0, :],
                                        B[hp:hp + 64, n, c * 64:c * 64 + 64], True, True, ew, fr)
                dst = M[:, 2 * pp:2 * pp + 2, :].rearrange("p q (n a t) -> p q n a t", a=2, t=64)[:, :, :, hp // 64, :]
                m4 = lambda name: self.C(name).unsqueeze(1).unsqueeze(1).broadcast_to((128, 2, 4, 64))
                t = V(dst, ps[:, :].rearrange("p (q n t) -> p q n t", q=2, t=64), m4("m2L"), ALU.mult, t)
                self.banks.give(i, t)
            for p in range(2 * pp, 2 * pp + 2):
                tM[p] = G(h8(M[:, p, :]), h8(M[:, p, :]), mk("I64"), ALU.add, t)
            yield
        for p in range(4):
            ks = []
            for hp in (0, 64):
                for which in (0, 1):
                    i, ps, fr = self.banks.take()
                    for n in range(4):
                        for par in range(2):
                            c = 2 * p + par
                            l = (B[hp:hp + 64, n, :] if which == 0 else KK[n][hp:hp + 64, :])[:, c * 64:c * 64 + 64]
                            t = self.mm(ps[64 * par:64 * par + 64, n * 128:n * 128 + 128], l,
                                        AR[hp:hp + 64, n, c, :, :].rearrange("p a t -> p (a t)"), True, True, ew, fr)
                    pv = ps[:, :].rearrange("p (n a t) -> p n a t", a=2, t=64)
                    n4 = lambda z: z[:, p, :].rearrange("p (n a t) -> p n a t", a=2, t=64)[:, :, hp // 64, :]
                    mk4 = lambda name: self.C(name).unsqueeze(1).broadcast_to((128, 4, 64))
                    a = V(n4(LT if which == 0 else KA), pv[:, :, 0, :], mk4("mSU"), ALU.mult, t)
                    b = V(n4(BR if which == 0 else KR), pv[:, :, 1, :], mk4("mIU"), ALU.mult)
                    self.banks.give(i, b)
                    ks.append(b)
                    if which == 0:
                        tLT[p, hp] = a
                yield
            tLT[p] = tLT[p, 64]
            t = G(h8(MT[:, p, :]), h8(LT[:, p, :]), mk("m2U"), ALU.mult, tLT[p])
            tMT[p] = G(h8(MT[:, p, :]), h8(MT[:, p, :]), mk("I64"), ALU.add, t)
            tKA[p] = ks[-1]
        t_gram = ks[-1]
        VTk, BTk = self.H[:, 4:8, :], R(60, 4, 512)
        t_tok = []

        def tok_tr(src, dst, *w):
            out = []
            for p in range(4):
                i, ps, fr = self.banks.take()
                for n in range(4):
                    t = self.tr(ps[:, n * 128:n * 128 + 128], src[n][:, p * 128:p * 128 + 128], w, fr)
                t = self.cp(act, dst[:, p, :], ps[:, :], t)
                self.banks.give(i, t)
                out.append(t)
            return out, t
        self.tv_, _ = tok_tr(VV, VTk, t_gram)
        yield
        self.tb_, _ = tok_tr([B[:, n, :] for n in range(4)], BTk, t_gram)
        yield
        KTk = R(16, 4, 512)
        self.tk_, _ = tok_tr(KK, KTk, t_gram, self.tv_)
        yield
        for l in range(5):
            lv = self.cst[:, CC["lvl"][0] + 64 * l:CC["lvl"][0] + 64 * l + 64].unsqueeze(1).broadcast_to((128, 8, 64))
            tP, tL = {}, {}
            for p in range(4):
                tL[p] = G(h8(LL[:, p, :]), h8(LT[:, p, :]), lv, ALU.mult, tMT[p])
            for p in range(4):
                i, ps, fr = self.banks.take()
                for h in range(8):
                    for par in (0, 64):
                        r, c = slice(par, par + 64), slice(h * 64, h * 64 + 64)
                        t = self.mm(ps[r, c], LL[r, p, c], M[r, p, c], True, True, tL[p], tM[p], fr)
                tP[p] = self.cp(act, PP[:, p, :], ps[:, :], t)
                self.banks.give(i, tP[p])
                yield
            for p in range(4):
                iM, pM, fM = self.banks.take() if l < 4 else (None, None, None)
                iT, pT, fT = self.banks.take()
                for h in range(8):
                    for par in (0, 64):
                        r, c = slice(par, par + 64), slice(h * 64, h * 64 + 64)
                        if l < 4:
                            tm = self.mm(pM[r, c], MT[r, p, c], PP[r, p, c], True, True, tP[p], fM)
                        tt_ = self.mm(pT[r, c], PP[r, p, c], MT[r, p, c], True, True, tP[p], fT)
                if l < 4:
                    tM[p] = V(M[:, p, :], M[:, p, :], pM[:, :], ALU.add, tm, tM[p])
                    self.banks.give(iM, tM[p])
                tMT[p] = V(MT[:, p, :], MT[:, p, :], pT[:, :], ALU.add, tt_, tMT[p])
                self.banks.give(iT, tMT[p])
                yield
        self.dump("mt", R(100, 2048), list(tMT.values()))
        ST, XX, UU, TS = R(76, 4, 128), R(80, 2, 512), R(84, 2, 512), R(90, 4, 64)
        Y = R(0, 4, 512)
        t0 = [tMT[3], self.tk_, self.tb_, self.tv_]
        tST = [dve.do(lambda e: e.memset(ST, 0.0), t0)]
        tS0 = tST[0]
        t_y, t_xf, t_uf = [], {}, {}
        def kav(c):
            p, r = c // 2, slice(64 * (c % 2), 64 * (c % 2) + 64)
            i, ps, fr = self.banks.take()
            for h in range(8):
                hs = slice(h * 64, h * 64 + 64)
                self.mm(ps[r, hs], KA[r, p, hs], VTk[r, p, hs], h == 0, False, t0, fr)
            return i, ps
        nxt = kav(0)
        hv = lambda h: (h // 2, slice(64 * (h % 2), 64 * (h % 2) + 64), slice(h * 64, h * 64 + 64))
        for c in range(8):
            p, par = c // 2, 64 * (c % 2)
            r = slice(par, par + 64)
            i, ps = nxt
            for n in range(4):
                t = self.mm(ps[r, n * 128:n * 128 + 128], AR[:, n, c, 0, :], ST[:, n, :], False, True, tST)
            tx = self.cp(act, XX[r, c // 2 % 2, :], ps[r, :], t, t_xf.get(c - 4), tS0)
            self.banks.give(i, tx)
            i_s, ps_s, fr = self.banks.take()
            for h in range(8):
                n, hp, hs = hv(h)
                self.mm(ps_s[hp, n * 64:n * 64 + 64], KTk[r, p, hs], VTk[r, p, hs], h < 2, False, fr)
            i_y, ps_y, fr = self.banks.take()
            for n in range(4):
                t_sy = self.mm(ps_y[:, n * 64:n * 64 + 64], ST[:, n, :], AR[:, n, c, 1, :], n == 0, False, fr)
            for h in range(8):
                n, hp, hs = hv(h)
                self.mm(ps_y[hp, n * 64:n * 64 + 64], VTk[r, p, hs], KR[r, p, hs], False, False)
            i, ps, fr = self.banks.take()
            for h in range(8):
                hs = slice(h * 64, h * 64 + 64)
                t = self.mm(ps[r, hs], MT[r, p, hs], XX[r, c // 2 % 2, hs], True, True, tx, fr)
            t_xf[c] = t
            tu = self.cp(act, UU[r, c // 2 % 2, :], ps[r, :], t, t_uf.get(c - 4), tS0)
            self.banks.give(i, tu)
            if c < 7:
                nxt = kav(c + 1)
            for h in range(8):
                n, hp, hs = hv(h)
                t = self.mm(ps_s[hp, n * 64:n * 64 + 64], BTk[r, p, hs], UU[r, c // 2 % 2, hs], False, True, tu)
            ty = []
            for hp in (0, 64):
                ty.append(V(TS[hp:hp + 64], ps_s[hp:hp + 64, 0:256].rearrange("p (n v) -> p n v", v=64),
                            ST[hp:hp + 64, :, hp:hp + 64], ALU.add, t, tST))
            self.banks.give(i_s, ty)
            tST = [V(ST[hp:hp + 64, :, hp:hp + 64], TS[hp:hp + 64],
                     GC[hp:hp + 64, :, c].unsqueeze(2).broadcast_to((64, 4, 64)), ALU.mult, ty, t_sy) for hp in (0, 64)]
            for h in range(8):
                n, hp, hs = hv(h)
                t = self.mm(ps_y[hp, n * 64:n * 64 + 64], UU[r, c // 2 % 2, hs], BR[r, p, hs], False, True)
            t_uf[c] = t
            t = self.cp(act, Y[:, :, c * 64:c * 64 + 64], ps_y[:, 0:256].rearrange("p (n v) -> p n v", v=64), t, t0)
            self.banks.give(i_y, t)
            t_y.append(t)
            yield
        self.dump("y0", R(0, 2048), t_y)
        self.ysp = [self.pair(36 + 4 * k, 38 + 4 * k) for k in range(8)]
        self.t_ysp = [None] * 4 + [self.split(*self.ysp[4 + k], R(28, 4, 512)[:, k, :], self.t_os[k], t_y, q=pool)
                                   for k in range(4)]
        Q, B_ = [R(92 + 2 * n, 512) for n in range(4)], [R(68 + 2 * n, 512) for n in range(4)]
        y = [Y[:, n, :] for n in range(4)]
        u, v = [], []
        for n in range(4):
            i, ps, fr = self.banks.take()
            m = self.mm(ps[:, :], self.C("blk"), y[n], True, True, t_y, fr)
            u.append(self.stt(y[n], ps[:, :], -1.0 / 64, y[n], ALU.mult, ALU.add, m))
            self.banks.give(i, u[n])
            v.append(self.af(Q[n], y[n], ACT.Square, u[n]))
        yield
        for n in range(4):
            i, ps, fr = self.banks.take()
            m = self.mm(ps[:, :], self.C("blk"), Q[n], True, True, v[n], fr)
            v[n] = self.af(B_[n], ps[:, :], ACT.Ln, m, t_y, bias=self.kc(EPSLN), scale=1.0 / 64)
            self.banks.give(i, v[n])
        yield
        for n in range(4):
            v[n] = self.af(B_[n], B_[n], ACT.Exp, v[n], scale=-0.5)
            i, ps, fr = self.banks.take()
            m = self.mm(ps[:, :], g2[:, n * 128:n * 128 + 128], ZB[:, 13, :], True, True, t_gl, fr)
            t = self.stt(y[n], y[n], self.pc("lnw", n), B_[n], ALU.mult, ALU.mult, v[n], u[n])
            t = self.stt(y[n], y[n], self.pc("lnb", n), self.H[:, n, :], ALU.add, ALU.add, t)
            t = V(y[n], y[n], ps[:, :], ALU.mult, m, t)
            self.banks.give(i, t)
            u[n] = t
        self.t_yr = u
        for n in range(4):
            self.t_ysp[n] = self.split(*self.ysp[n], y[n], u[n], t_y)
        yield

    def load_layer_tables(self, *after):
        self.c2 = self.region(24, NC2)
        s = self.P.dsem("c2")
        self.t_c2 = self.P.dma(self.P.sp, self.c2, self.d["cst2"], s, *after)

    def load_lw(self, *after):
        self.slw = self.P.dsem("lw")
        self.lw = self.region(109.5, 2560)
        self.t_lw = self.P.dma(self.P.sp, self.lw, self.d["lw"][0], self.slw, *after)

    def layers(self, stop):
        P, R = self.P, self.region
        X = [self.X[:, k, :] for k in range(8)]
        Hs = self.Hs
        t_X, self.t_end = self.t_X, [self.t_X, self.t_h0]
        for l in range(2):
            t_h = self.t_h0 if l == 0 else self.norm_apply(st, X, Hs, [self.pc("ng1", k) for k in range(8)])
            self.layer(l, Hs, t_h)
            Y, each = self.Y, self.t_ysp
            t_X = []
            if l == 0:
                st = self.norm_stats(R(67, 3, 512), self.t_y)
            so = P.dsem("out") if l == 1 else None
            for n in range(8):
                if n < 4:
                    i, ps = self.begun[n]
                    t = self.dense([(f"o{l}", n, k) for k in range(4, 12)], Y[4:], ps[:, :], each=each[4:], start=False)
                else:
                    i, ps, fr = self.banks.take()
                    t = self.dense([(f"o{l}", n, k) for k in range(12)], Y, ps[:, :], fr, each=each)
                u = self.tt(P.dve, X[n], ps[:, :], X[n], ALU.add, t)
                self.banks.give(i, u)
                t_X.append(u)
                if l == 1:
                    P.dma(P.sp, self.out[:, n, :], X[n], so, u)
                elif n:
                    self.norm_tile(st, X[n - 1], t_X[n - 1])
            if l == 0:
                self.norm_tile(st, X[7], t_X[7])
                self.t_lw = P.dma(P.sp, self.lw, self.d["lw"][1], self.slw, t)
                self.dump("Y12", self.G, self.t_y, t)
                self.dump("l0", self.X[:, :, :], t_X)
            self.t_end = [t_X, t]
            if stop == "l0":
                return

    def layer(self, l, Hs, t_h):
        P, R = self.P, self.region
        act, dve, pool = P.act, P.dve, P.pool
        self.G = R(0, 12, 512)
        self.L = R(37, 3, 512)
        self.name = f"l{l}"
        te = self.t_end
        RT = R(33, 4, 4, 2, 16)
        cs, sn = (self.c2[:, 2048 + 64 * i:2112 + 64 * i].rearrange("p (a d) -> p a d", a=4) for i in (0, 1))
        gr = self.pc(f"gr{l}", 0, 64).rearrange("p (b d) -> p b d", b=2)
        for i, (tb, lo) in enumerate(((cs, 0), (cs, 16), (sn, 0), (sn, 16))):
            self.t_rt = self.tt(pool, RT[:, i], tb.unsqueeze(2).broadcast_to((128, 4, 2, 16)),
                                gr[:, :, lo:lo + 16].unsqueeze(1).broadcast_to((128, 4, 2, 16)), ALU.mult,
                                self.t_c2, te)
        self.RT = RT
        ST = R(35.5, 352)
        self.ST = ST
        i, pst, frs = self.banks.take()
        t_sq, self.t_l = [], []
        SQ = R(75, 3, 512)
        for n in range(3):
            b, ps, fr = self.banks.take()
            t = self.dense([(self.name, n, k) for k in range(8)], Hs, ps[:, :], fr, each=t_h)
            a = self.af(SQ[:, n, :], ps[:, :], ACT.Square, t, te)
            c = self.af(self.L[:, n, :], ps[:, :], ACT.Copy, t, te,
                        scale=self.pc(f"qan{l}", n) if n < 2 else self.pc(f"kvan{l}"))
            self.banks.give(b, a, c)
            t_sq.append(a)
            self.t_l.append(c)
        b, ps, fr = self.banks.take()
        for k in range(8):
            w, wt = self.wblock((self.name, 3, k))
            t = self.mms(ps[0:32, :], [x[:, 0:32] for x in w], Hs[k], k == 0, k == 7, wt, fr)
            self.wused(t)
        KRf = R(81, 512)[0:32]
        t_kr = self.cp(act, KRf, ps[0:32, :], t, te)
        self.banks.give(b, t_kr)
        for n in range(3):
            for q in range(4):
                o = (0 if n < 2 else 4) + q
                t = self.mm(pst[:, o:o + 1], SQ[:, n, q * 128:q * 128 + 128], self.C("ones")[:, 0:1],
                            n == 0 and q == 0, n > 0, t_sq[n], frs)
        a = self.ts(dve, ST[:, 0:4], pst[:, 0:4], 1.0 / 256, ALU.mult, 1e-6, ALU.add, t, te)
        a = self.ts(dve, ST[:, 4:8], pst[:, 4:8], 1.0 / 128, ALU.mult, 1e-6, ALU.add)
        self.banks.give(i, a)
        t = self.af(ST[:, 8:12], ST[:, 4:8], ACT.Sqrt, a)
        t = dve.do(lambda e: e.reciprocal(ST[:, 8:12], ST[:, 8:12]), t)
        self.t_st = t
        b, ps, fr = self.banks.take()
        for q in range(4):
            t = P.pe.do(lambda e, q=q, ps=ps: e.transpose(ps[:, q * 32:q * 32 + 32], KRf[:, q * 128:q * 128 + 128],
                                                          self.C("ident")[0:32, 0:32]), t_kr, fr)
        self.KRt = R(35, 4, 32)
        self.t_kr = self.cp(act, self.KRt, ps[:, 0:128].rearrange("p (q d) -> p q d", q=4), t, te)
        self.banks.give(b, self.t_kr)
        self.t_y = [None] * 12
        self.Y = [self.pair(*a) for a in ((83, 85), (87, 89), (91, 93), (95, 97), (99, 101), (109.5, 111.5), (113.5, 115.5),
                                          (117.5, 103), (43, 45), (47, 49), (51, 53), (55, 57))]
        self.t_ysp = [None] * 12
        self.t_sq, self.silu_last = {}, []
        d = self.dense_rest(l)
        self.run((self.qk(l), 1), (self.take_n(d, 4), 1))
        self.run((self.heads(l), 1), (self.take_n(d, 20), 1))
        for m in range(4):
            self.out_split(m, self.t_mla, self.t_wt)
        self.run((self.windows(l), 2), (d, 1))
        self.gated(range(8, 12), lambda m: self.SO[:, m - 8, :], self.t_so, self.t_win)

    def out_split(self, m, *after):
        self.t_ysp[m] = self.split(*self.Y[m], self.G[:, m, :], self.t_y[m], *after, q=self.P.pool if m % 2 else None)

    def gated(self, ms, src, tok, *after):
        t = [self.af(self.G[:, m, :], self.G[:, m, :], ACT.Silu, self.t_raw[m]) for m in ms]
        for j, m in enumerate(ms):
            self.t_y[m] = self.tt(self.P.dve, self.G[:, m, :], self.G[:, m, :], src(m), ALU.mult, t[j], tok)
            self.out_split(m, *after)

    def tok(self, k, q):
        return [x[:, q * 128:q * 128 + 128] for x in self.Hs[k]]

    def take_n(self, g, n):
        for _ in range(n):
            try:
                next(g)
            except StopIteration:
                return
            yield

    def proj(self, n):
        i, ps, fr = self.banks.take()
        t = self.dense([(self.name, n, k) for k in range(8)], self.Hs, ps[:, :], fr)
        return i, ps, t

    def dense_rest(self, l):
        P, R = self.P, self.region
        act, dve, pool = P.act, P.dve, P.pool
        te = self.t_end
        self.t_g = {}
        self.t_raw = {}
        for n in range(4):
            i, ps, t = self.proj(4 + n)
            self.t_raw[n] = self.cp(act, self.G[:, n, :], ps[:, :], t, te)
            self.banks.give(i, self.t_raw[n])
            yield
        hold = [self.banks.take() for _ in range(4)]
        for k in range(8):
            w, wt = self.wblock([(self.name, 24 + n, k) for n in range(4)], 4)
            for q in range(4):
                t = self.mms(hold[q][1][:, :], self.tok(k, q), w, k == 0, k == 7, wt, hold[q][2])
            self.wused(t)
            if k % 2:
                yield
        self.q_ps, self.t_q = hold, t
        kv = [self.banks.take() for _ in range(2)]
        for k in range(8):
            w, wt = self.wblock([(self.name, 28, k), (self.name, 29, k)], 2)
            for q in range(4):
                _, ps, fr = kv[q // 2]
                t = self.mms(ps[:, q % 2 * 256:q % 2 * 256 + 256], self.tok(k, q), w, k == 0 and q % 2 == 0, k == 7,
                             wt, fr)
            self.wused(t)
        self.kv_ps = [x[1][:, :].rearrange("p (q w d) -> p q w d", q=2, w=2) for x in kv]
        self.t_k = t
        self.SV = R(105.5, 4, 128)
        self.t_sv = [self.cp(act, self.SV[:, 2 * j:2 * j + 2, :], self.kv_ps[j][:, :, 1, :], t, te, self.t_qkfree)
                     for j in range(2)]
        self.window_norm(l)
        for x in kv:
            self.banks.give(x[0], self.t_sv, self.t_wn)
        yield
        self.window_t()
        yield
        for n in range(4):
            i, ps, t = self.proj(30 + n)
            self.t_raw[8 + n] = self.cp(dve, self.G[:, 8 + n, :], ps[:, :], t, te)
            self.banks.give(i, self.t_raw[8 + n])
            yield
        self.YC = YC = R(119.5, 4, 512)
        CU = R(127.5, 516)
        CH = R(129.75, 512)
        t0 = dve.do(lambda e: e.memset(CU[:, 0:2], 0.0), te, self.t_wt)
        t_y, t_u = t0, t0
        self.t_yc = []
        for j in range(4):
            i, ps, t = self.proj(8 + j)
            ta = self.cp(act, CH, ps[:, :], t, t_u)
            self.banks.give(i, ta)
            yield
            i, ps, t = self.proj(16 + j)
            t_u = self.tt(dve, CU[:, 2:514], ps[:, :], CH, ALU.mult, t, ta, t_y)
            self.banks.give(i, t_u)
            y = YC[:, j, :]
            a = self.ts(pool, y, CU[:, 0:512], self.pc(f"cw{l}", j), ALU.mult, None, None, t_u, self.t_qkfree)
            a = self.stt(y, CU[:, 1:513], self.pc(f"cw{l}", 4 + j), y, ALU.mult, ALU.add, a)
            t_y = self.stt(y, CU[:, 2:514], self.pc(f"cw{l}", 8 + j), y, ALU.mult, ALU.add, a)
            yield
            i, ps, t = self.proj(12 + j)
            b = self.tt(dve, y, y, ps[:, :], ALU.mult, t, t_y)
            self.banks.give(i, b)
            self.t_yc.append(b)
            yield
            i, ps, t = self.proj(20 + j)
            self.t_raw[4 + j] = self.cp(act, self.G[:, 4 + j, :], ps[:, :], t, te)
            self.banks.give(i, self.t_raw[4 + j])
            yield
        self.gated(range(4, 8), lambda m: YC[:, m - 4, :], self.t_yc, self.t_mla, self.t_wt)
        yield
        self.begun = []
        for n in range(4):
            i, ps, fr = self.banks.take()
            self.dense([(f"o{l}", n, k) for k in range(4)], self.Y[:4], ps[:, :], fr, each=self.t_ysp[:4], stop=False)
            self.begun.append((i, ps))
            yield

    def window_norm(self, l):
        P, R = self.P, self.region
        act, dve, pool = P.act, P.dve, P.pool
        te = self.t_end
        W = R(95.5, 4, 640)
        SQ = R(127.5, 640)
        S = self.ST[:, 168:208].rearrange("p (q h) -> p q h", q=4)
        psk = lambda q: self.kv_ps[q // 2][:, q % 2, 0, :]
        ts_ = []
        last = te
        for q in range(4):
            psq = self.q_ps[q][1]
            a = self.af(SQ[:, 0:512], psq[:, :], ACT.Square, self.t_q, last)
            b = self.af(SQ[:, 512:640], psk(q), ACT.Square, self.t_k)
            last = dve.do(lambda e, q=q: e.tensor_reduce(out=S[:, q, :], in_=SQ.rearrange("p (h d) -> p h d", d=64),
                                                         op=ALU.add, axis=AX.X), a, b, te)
            ts_.append(last)
        a = self.ts(dve, S, S, 1.0 / 64, ALU.mult, 1e-6, ALU.add, ts_)
        a = self.af(S, S, ACT.Sqrt, a)
        a = dve.do(lambda e: e.reciprocal(S, S), a)
        t_w = []
        for q in range(4):
            i, psq, _ = self.q_ps[q]
            b = self.tt(dve, W[:, q, 0:512].rearrange("p (h d) -> p h d", d=64),
                        psq[:, :].rearrange("p (h d) -> p h d", d=64),
                        S[:, q, 0:8].unsqueeze(2).broadcast_to((128, 8, 64)), ALU.mult, a, te, self.t_mlaw)
            self.banks.give(i, b)
            c = self.tt(dve, W[:, q, 512:640].rearrange("p (h d) -> p h d", d=64),
                        psk(q).rearrange("p (h d) -> p h d", d=64),
                        S[:, q, 8:10].unsqueeze(2).broadcast_to((128, 2, 64)), ALU.mult, a)
            t_w.append(c)
        self.WT_, self.t_wn = W, t_w

    def window_t(self):
        l = int(self.name[1])
        self.SQT = [self.region(x, 512) for x in (37, 39, 41, 33, 107.5)]
        self.t_sqt = []
        for n in range(5):
            i, ps, fr = self.banks.take()
            for q in range(4):
                t = self.tr(ps[:, q * 128:q * 128 + 128], self.WT_[:, q, n * 128:n * 128 + 128], self.t_wn[q], fr)
            t = self.af(self.SQT[n], ps[:, :], ACT.Copy, t, self.t_mlaw,
                        scale=self.pc(f"sqn{l}" if n < 4 else f"skn{l}"))
            self.banks.give(i, t)
            self.t_sqt.append(t)
        self.t_wt = t

    def qk(self, l):
        P, R = self.P, self.region
        act, dve, pool = P.act, P.dve, P.pool
        L, lw, ST, RT = self.L, self.lw, self.ST, self.RT
        te = self.t_end
        KT, QT, MV = R(43, 8, 512), R(59, 8, 512), R(87, 4, 512)
        self.KT, self.QT, self.MV = KT, QT, MV
        gcol = [self.pc(f"kn{l}"), self.pc(f"qn{l}")]
        KQ = [R(75 + 6 * b, 2, 8, 96) for b in range(2)]
        SQ = [R(95 + 6 * b, 2, 8, 96) for b in range(2)]
        T4 = R(119.5, 4, 2, 8, 16)
        self.t_mv, self.t_kt = [], []
        free = [te, te]
        t_t4 = te
        pend = None

        def transposes(q, kq, t):
            out = []
            for w in range(2):
                for hh in range(2):
                    i, ps, fr = self.banks.take()
                    for h in range(4):
                        m = self.tr(ps[0:96, h * 128:h * 128 + 128], kq[:, w, 4 * hh + h, :], t, fr)
                    dst = (KT, QT)[w][0:96, 4 * hh:4 * hh + 4, q * 128:q * 128 + 128]
                    src = ps[0:96, :].rearrange("p (h t) -> p h t", h=4)
                    if hh:
                        e_ = self.af(dst, src, ACT.Copy, m, te, scale=gcol[w][0:96])
                    else:
                        e_ = self.ts(dve, dst, src, gcol[w][0:96], ALU.mult, None, None, m, te)
                    self.banks.give(i, e_)
                    out.append(e_)
            self.t_kt += out
            return m
        for q in range(4):
            b = q % 2
            kq, sq = KQ[b], SQ[b]
            tok = slice(q * 128, q * 128 + 128)
            hold = []
            for hh in range(2):
                i, ps, fr = self.banks.take()
                self.mm(ps[:, 0:384], L[:, 0, tok], lw[:, hh * 384:hh * 384 + 384], True, False, self.t_l, self.t_lw, fr)
                t = self.mm(ps[:, 0:384], L[:, 1, tok], lw[:, 768 + hh * 384:1152 + hh * 384], False, True)
                hold.append((i, ps))
            ik, psk, fr = self.banks.take()
            tk = self.mm(psk[:, :], L[:, 2, tok], lw[:, 1536:2048], True, True, fr)
            iv, psv, fr = self.banks.take()
            tv = self.mm(psv[:, :], L[:, 2, tok], lw[:, 2048:2560], True, True, fr)
            h96 = lambda ps: ps[:, 0:384].rearrange("p (h d) -> p h d", h=4)
            a = [self.af(sq[:, 1, 4 * hh:4 * hh + 4, :], h96(hold[hh][1]), ACT.Square, t, free[b]) for hh in range(2)]
            a.append(self.af(sq[:, 0, :, 0:64], psk[:, :].rearrange("p (h d) -> p h d", d=64), ACT.Square, tk, free[b], self.t_st,
                             scale=ST[:, 8 + q:9 + q]))
            u = self.af(MV[:, q, :], psv[:, :], ACT.Copy, tv, self.t_st, te, scale=ST[:, 8 + q:9 + q])
            self.banks.give(iv, u)
            self.t_mv.append(u)
            a.append(self.tt(pool, sq[:, 0, :, 64:96], self.KRt[:, q, :].unsqueeze(1).broadcast_to((128, 8, 32)),
                             self.KRt[:, q, :].unsqueeze(1).broadcast_to((128, 8, 32)), ALU.mult, self.t_kr, free[b]))
            yield
            s_ = ST[:, 16 + 16 * q:32 + 16 * q].rearrange("p (w h) -> p w h", w=2)
            v = ST[:, 104 + 16 * q:120 + 16 * q].rearrange("p (w h) -> p w h", w=2)
            c = dve.do(lambda e, sq=sq, s_=s_: e.tensor_reduce(out=s_, in_=sq, op=ALU.add, axis=AX.X), a)
            em = ST[:, 12 + q:13 + q]
            c1 = self.ts(dve, em, ST[:, q:q + 1], 1e-6, ALU.mult, None, None, c)
            c2_ = self.ts(dve, s_[:, 0], s_[:, 0], 1.0 / 96, ALU.mult, 1e-6, ALU.add, c)
            c3 = self.ts(dve, s_[:, 1], s_[:, 1], 1.0 / 96, ALU.mult, em, ALU.add, c1, c)
            c = self.af(v, s_, ACT.Sqrt, c2_, c3)
            c = dve.do(lambda e, v=v: e.reciprocal(v, v), c)
            d_ = self.ts(dve, s_[:, 0], v[:, 0], ST[:, 8 + q:9 + q], ALU.mult, None, None, c)
            bc = lambda ap, n: ap.unsqueeze(2).broadcast_to((128, ap.shape[1], n))
            w1 = [self.tt(dve, kq[:, 1, 4 * hh:4 * hh + 4, :], h96(hold[hh][1]), bc(v[:, 1, 4 * hh:4 * hh + 4], 96),
                          ALU.mult, c, free[b]) for hh in range(2)]
            w2 = self.tt(dve, kq[:, 0, :, 0:64], psk[:, :].rearrange("p (h d) -> p h d", d=64), bc(s_[:, 0], 64),
                         ALU.mult, d_, free[b])
            w3 = self.tt(pool, kq[:, 0, :, 64:96], self.KRt[:, q, :].unsqueeze(1).broadcast_to((128, 8, 32)),
                         bc(v[:, 0], 32), ALU.mult, c, free[b])
            self.banks.give(hold[0][0], w1[0])
            self.banks.give(hold[1][0], w1[1])
            self.banks.give(ik, w2, a)
            yield
            x1, x2 = kq[:, :, :, 64:80], kq[:, :, :, 80:96]
            rt = lambda i: RT[:, i, q].unsqueeze(2).broadcast_to((128, 2, 8, 16))
            m1 = self.tt(pool, T4[:, 0], x1, rt(0), ALU.mult, w1, w3, self.t_rt, t_t4)
            m2 = self.tt(pool, T4[:, 1], x2, rt(3), ALU.mult)
            m3 = self.tt(pool, T4[:, 2], x2, rt(1), ALU.mult)
            m4 = self.tt(pool, T4[:, 3], x1, rt(2), ALU.mult)
            m2 = self.tt(dve, x1, T4[:, 0], T4[:, 1], ALU.subtract, m4)
            m4 = self.tt(dve, x2, T4[:, 2], T4[:, 3], ALU.add, m4)
            t_t4 = m4
            if pend:
                m = transposes(*pend)
                free[1 - b] = [m]
            pend = (q, kq, [m2, m4, w2])
            yield
        m = transposes(*pend)
        self.t_qkfree = [m, m4]
        self.t_mlaw = [self.t_qkfree, a]
        self.t_silu = [self.af(self.G[:, n, :], self.G[:, n, :], ACT.Silu, self.t_raw[n]) for n in range(4)]
        yield

    def heads(self, l):
        P, R = self.P, self.region
        act, dve, pool = P.act, P.dve, P.pool
        KT, QT, MV = self.KT, self.QT, self.MV
        PB = [R(75, 1280), R(80, 1280)]
        PT = [R(109.5, 1280), R(114.5, 1280)]
        sc = 96.0 ** -0.5
        off = {3: 0, 2: 512, 0: 896, 1: 1024}
        n_ = lambda q: 128 * (q + 1)
        poff = {0: 0, 1: 512, 3: 896, 2: 1024}
        S2 = self.ST[:, 208:272].rearrange("p (b k q) -> p b k q", b=2, k=8)
        t_tr, t_pv, tp = {}, {}, {}
        te = [self.t_end, self.t_qkfree]

        def A(h):
            b = h % 2
            mx, nm, rs, rc = (S2[:, b, k, :] for k in range(4))
            banks = [self.banks.take() for _ in range(3)]
            where = {3: (0, 0), 2: (1, 0), 0: (1, 384), 1: (2, 0)}
            tm = []
            first = set()
            for q in (3, 2, 0, 1):
                bi, o = where[q]
                i, ps, fr = banks[bi]
                n = n_(q)
                t = self.mm(ps[:, o:o + n], QT[0:96, h, q * 128:q * 128 + 128], KT[0:96, h, 0:n], True, True,
                            self.t_kt, fr)
                if q == 2:
                    continue
                for qq in ((2, 0) if q == 0 else (q,)):
                    bi, o = where[qq]
                    ps, n = banks[bi][1], n_(qq)
                    u = self.tt(dve, ps[:, o + n - 128:o + n], ps[:, o + n - 128:o + n], self.C("caus"), ALU.add, t)
                    tm.append(dve.do(lambda e, o_=mx[:, qq:qq + 1], a=ps[:, o:o + n]:
                                     e.tensor_reduce(out=o_, in_=a, op=ALU.max, axis=AX.X), u, t_tr.get(h - 2)))
            t = self.ts(dve, nm, mx, -sc, ALU.mult, None, None, tm)
            te_ = {}
            for q in (3, 2, 0, 1):
                bi, o = where[q]
                ps, n = banks[bi][1], n_(q)
                te_[q] = self.af(PB[b][:, off[q]:off[q] + n], ps[:, o:o + n], ACT.Exp, t, t_tr.get(h - 2, te),
                                 bias=nm[:, q:q + 1], scale=sc, acc=rs[:, q:q + 1])
            for bi, qs in ((0, (3,)), (1, (2, 0)), (2, (1,))):
                self.banks.give(banks[bi][0], [te_[q] for q in qs])
            t = dve.do(lambda e: e.reciprocal(rc, rs), list(te_.values()))
            tp[h] = {q: self.ts(pool, PB[b][:, off[q]:off[q] + n_(q)], PB[b][:, off[q]:off[q] + n_(q)],
                                rc[:, q:q + 1], ALU.mult, None, None, t) for q in (0, 1, 2, 3)}

        def B(h):
            b = h % 2
            ev = []
            for js in ((0,), (1, 3), (2,)):
                i, ps, fr = self.banks.take()
                o = 0
                for j in js:
                    for q in range(j, 4):
                        t = self.tr(ps[:, o:o + 128], PB[b][:, off[q] + j * 128:off[q] + j * 128 + 128], tp[h][3], fr)
                        o += 128
                e_ = self.cp(act if js == (0,) else dve, PT[b][:, poff[js[0]]:poff[js[0]] + o], ps[:, 0:o], t,
                             t_pv.get(h - 2, te))
                self.banks.give(i, e_)
                ev.append(e_)
            t_tr[h] = t
            self.evs[h] = ev

        def C(h):
            b = h % 2
            i, ps, fr = self.banks.take()
            r = slice(64 * b, 64 * b + 64)
            for j in (0, 1, 2, 3):
                t = self.mm(ps[r, j * 128:512], MV[:, j, 64 * h:64 * h + 64],
                            PT[b][:, poff[j]:poff[j] + 512 - 128 * j], j == 0, j == 3, self.evs[h], self.t_mv, fr)
            t_pv[h] = t
            g = self.G[r, h // 2, :]
            t = self.tt(dve, g, ps[r, :], g, ALU.mult, t, self.t_silu[h // 2])
            self.banks.give(i, t)
            self.t_y[h // 2] = [self.t_y[h // 2], t]
        self.evs = {}
        for s in range(10):
            if s < 8:
                A(s)
                yield
            if 1 <= s < 9:
                B(s - 1)
                yield
            if s >= 2:
                C(s - 2)
                yield
        self.t_mla = [t_tr[7], t_pv[7]]

    def windows(self, l):
        P, R = self.P, self.region
        act, dve, pool = P.act, P.dve, P.pool
        SQT, SV = self.SQT, self.SV
        ZZ = [R(43, 8, 256), R(51, 8, 256)]
        PP = [R(75, 2, 2, 512), R(59, 2, 2, 512)]
        self.SO = R(67, 4, 512)
        al = self.c2[:, 0:2048].rearrange("p (h k) -> p h k", h=8)
        sink = self.pc(f"sink{l}", 0, 8)
        S = self.ST[:, 272:352].rearrange("p (b k h) -> p b k h", b=2, k=5)
        tp, ev, t_tr, t_pv = {}, {}, {}, {}
        tm = self.t_mla
        self.t_so = []

        def A(n):
            b = n % 2
            Z = ZZ[b]
            mx, nm, rs, es, rc = (S[:, b, k, :] for k in range(5))
            lo = 128 if n == 0 else 0
            w = 256 - lo
            k0 = (n - 1) * 128 + lo
            tz = []
            for g in range(2):
                for jj in range(2):
                    i, ps, fr = self.banks.take()
                    for x in range(2):
                        j = 2 * jj + x
                        t = self.mm(ps[:, x * 256 + lo:x * 256 + 256], SQT[j][64 * g:64 * g + 64, n * 128:n * 128 + 128],
                                    SQT[4][64 * g:64 * g + 64, k0:k0 + w], True, True, self.t_sqt, fr)
                    h0 = 4 * jj + g
                    t = self.stt(Z[:, h0:h0 + 3:2, lo:256], ps[:, :].rearrange("p (x k) -> p x k", x=2)[:, :, lo:256],
                                 0.125, al[:, h0:h0 + 3:2, lo:256], ALU.mult, ALU.add, t, self.t_c2, t_tr.get(n - 2, tm))
                    self.banks.give(i, t)
                    tz.append(t)
            yield
            t = dve.do(lambda e, lo=lo: e.tensor_reduce(out=mx, in_=Z[:, :, lo:256], op=ALU.max, axis=AX.X), tz)
            t = self.tt(dve, mx, mx, sink, ALU.max, t)
            ta = self.ts(dve, nm, mx, -1.0, ALU.mult, None, None, t)
            tb = self.tt(dve, es, sink, mx, ALU.subtract, t)
            te = [self.af(Z[:, h, lo:256], Z[:, h, lo:256], ACT.Exp, ta, tz, bias=nm[:, h:h + 1], acc=rs[:, h:h + 1])
                  for h in range(8)]
            tb = self.af(es, es, ACT.Exp, tb)
            t = self.tt(dve, rc, rs, es, ALU.add, te, tb)
            t = dve.do(lambda e: e.reciprocal(rc, rc), t)
            tp[n] = self.tt(pool, Z[:, :, lo:256], Z[:, :, lo:256], rc.unsqueeze(2).broadcast_to((128, 8, w)),
                            ALU.mult, t, te)
            yield

        def B(n):
            b = n % 2
            Z, PT = ZZ[b], PP[b]
            lo = 128 if n == 0 else 0
            for g in range(2):
                for kb in range(lo // 128, 2):
                    i, ps, fr = self.banks.take()
                    for j in range(4):
                        t = self.tr(ps[:, j * 128:j * 128 + 128], Z[:, 2 * j + g, kb * 128:kb * 128 + 128], tp[n], fr)
                    e_ = self.cp(act if kb else dve, PT[:, g, kb, :], ps[:, :], t, t_pv.get(n - 2, tm))
                    self.banks.give(i, e_)
                    ev.setdefault(n, []).append(e_)
            t_tr[n] = t

        def C(n):
            PT = PP[n % 2]
            i, ps, fr = self.banks.take()
            kbs = range(1 if n == 0 else 0, 2)
            for g in range(2):
                for kb in kbs:
                    t = self.mm(ps[64 * g:64 * g + 64, :], SV[:, n - 1 + kb, 64 * g:64 * g + 64], PT[:, g, kb, :],
                                kb == kbs[0], kb == 1, ev[n], self.t_sv, fr)
            t_pv[n] = t
            t = self.cp(act, self.SO[:, :, n * 128:n * 128 + 128], ps[:, :].rearrange("p (j q) -> p j q", j=4), t, tm)
            self.banks.give(i, t)
            self.t_so.append(t)
        for s in range(6):
            if s < 4:
                yield from A(s)
            if 1 <= s < 5:
                B(s - 1)
                yield
            if s >= 2:
                C(s - 2)
                yield
        self.t_win = [t_tr[3], t_pv[3]]


def _cols(a, n):
    return np.asarray(a, np.float32).reshape(n, 128).T


def _pad(a, rows):
    out = np.zeros((rows,) + a.shape[1:], np.float32)
    out[:a.shape[0]] = a
    return out


SW = [0, 4, 1, 5, 2, 6, 3, 7]


def _heads(a, axis):
    a = np.moveaxis(a, axis, 0)
    a = a.reshape((8, 64) + a.shape[1:])[SW].reshape((512,) + a.shape[1:])
    return np.moveaxis(a, 0, axis)


def _weights(inp):
    W = {"ada": inp["w_ada"][0], "in": inp["w_in"][0], "glu": inp["s5_w_glu"][0], "out": inp["w_out"][0],
         "gate": inp["ffn_w_gate"][0], "up": inp["ffn_w_up"][0], "down": inp["ffn_w_down"][0]}
    for l in range(2):
        w = inp["w_in_2"][l]
        o = np.cumsum([0, 256, 128, 32, 512, 512, 512, 512, 512, 512, 128, 128, 512])
        part = [w[:, o[i]:o[i + 1]] for i in range(12)]
        rope = np.zeros((1024, 128), np.float32)
        rope[:, :32] = part[2]
        W[f"l{l}"] = np.concatenate([part[0], part[1], rope, part[3], part[4], part[5], part[6], part[7],
                                     _heads(part[8], 1), part[9], part[10], _heads(part[11], 1)], 1)
        wo = inp["w_out_2"][l]
        W[f"o{l}"] = np.concatenate([wo[:1024], _heads(wo[1024:], 0)], 0)
    return W


def _arrays(inp):
    f = lambda n: np.asarray(inp[n], np.float32)
    par = np.zeros((128, NPC), np.float32)

    def put(name, a):
        s, n = PCOLS[name]
        par[:a.shape[0], s:s + n] = a
    put("b_ada", _cols(f("b_ada")[0], 48))
    put("mu", _cols(f("mu_shift")[0], 14))
    for name, src in (("w0", "rw_w0"), ("a0", "rw_a0"), ("k_k", "rw_k_k"), ("k_a", "rw_k_a"), ("lnw", "rw_lnx_w"),
                      ("lnb", "rw_lnx_b"), ("bglu", "s5_b_glu"), ("gain", "s5_gain")):
        put(name, _cols(f(src)[0], 4))
    put("r_k", _cols(f("rw_r_k")[0].reshape(512), 4))
    put("s5d", _cols(f("s5_d")[0].reshape(512), 4))
    put("fgain", _cols(f("final_gain"), 8))
    put("c", _cols(f("c")[0], 8))
    put("are", f("s5_a_re")[0].reshape(16, 128).T)
    put("aim", f("s5_a_im")[0].reshape(16, 128).T)
    put("ldt", np.repeat(f("s5_log_dt")[0].reshape(16, 2), 64, axis=1).T)
    for l in range(2):
        put(f"ng{l}", _cols(f("norm_g_2")[l], 8))
        put(f"qan{l}", _cols(f("mla_q_a_norm_2")[l], 2))
        put(f"kvan{l}", _cols(f("mla_kv_a_norm_2")[l], 1))
        for name, src in (("qn", "mla_q_norm_2"), ("kn", "mla_k_norm_2")):
            put(f"{name}{l}", np.concatenate([f(src)[l][:64], np.ones(32, np.float32)])[:, None])
        both = np.concatenate([f("mla_k_norm_2")[l][64:], f("mla_q_norm_2")[l][64:]])
        put(f"gr{l}", np.broadcast_to(both[None, :], (128, 64)))
        put(f"cw{l}", np.concatenate([_cols(f("conv_w_2")[l][w], 4) for w in range(3)], 1))
        put(f"sqn{l}", np.tile(f("swa_q_norm_2")[l], 2)[:, None])
        put(f"skn{l}", np.tile(f("swa_k_norm_2")[l], 2)[:, None])
        put(f"sink{l}", np.broadcast_to(f("swa_sinks_2")[l][SW][None, :], (128, 8)))
    cst, cst2 = constants()
    b = lambda a: a.reshape(16, 128, 16).transpose(1, 0, 2).reshape(128, 256)
    bt = lambda a: b(a.transpose(0, 2, 1))
    s5p = np.stack([b(f("s5_b_re")[0]), b(f("s5_b_im")[0]), bt(f("s5_c_re")[0]), bt(f("s5_c_im")[0])], 1)
    small = np.stack([np.concatenate([f("rw_w2")[0], f("rw_a2")[0]], 0), f("rw_g2")[0]], 1)
    lw = []
    for l in range(2):
        qb, kvb = f("mla_w_qb_2")[l], f("mla_w_kvb_2")[l].reshape(128, 8, 128)
        lw.append(np.concatenate([qb[0:128], qb[128:256], kvb[:, :, :64].reshape(128, 512),
                                  kvb[:, :, 64:].reshape(128, 512)], 1))
    xT = f("x")[0].T.reshape(8, 128, 512).transpose(1, 0, 2)
    out = {"par": par, "cst": cst, "cst2": cst2, "s5p": s5p, "small": small, "lw": np.stack(lw), "xT": xT}
    return {k: np.ascontiguousarray(v) for k, v in out.items()}


def _program(nc, stop=None, dump_shapes=None):
    shapes = {"par": [128, NPC], "cst": [128, NCC], "cst2": [128, NC2], "s5p": [128, 4, 256],
              "small": [128, 2, 512], "lw": [2, 128, 2560], "xT": [128, 8, 512], "ws": [UNITS, 128, 1024]}
    d = {n: nc.dram_tensor("in_" + n, s, F32, kind="ExternalInput").ap() for n, s in shapes.items()}
    for n, s in (("kpad", [32, 16, 240]), ("ud", [32, 16, 8, 64]), ("yd", [32, 16, 8, 64])):
        d[n] = nc.dram_tensor("scr_" + n, s, F32).ap()
    out = nc.dram_tensor("outT", [128, 8, 512], F32, kind="ExternalOutput").ap()
    dumps = {n: nc.dram_tensor("dump_" + n, s, F32, kind="ExternalOutput").ap() for n, s in (dump_shapes or {}).items()}
    return Kern(nc, d, out, dumps).build(stop)


def _stream(W, order):
    ws = np.zeros((UNITS, 128, 8, 128), np.float32)
    for b, (name, n, k) in enumerate(order):
        ws[b // 8, :, b % 8, :] = W[name][k * 128:k * 128 + 128, n * 128:n * 128 + 128]
    return ws.reshape(UNITS, 128, 1024)


def kernel(**inputs):
    import concourse.bacc as _bacc
    from concourse.bass_utils import run_bass_kernel_spmd as _run

    nc = _bacc.Bacc("TRN2", target_bir_lowering=False, num_devices=1, dynamic_dma_scratch_size=1024)
    order = _program(nc)
    inp = {k: np.asarray(v) for k, v in inputs.items()}
    arrays = {"in_" + k: v for k, v in _arrays(inp).items()}
    arrays["in_ws"] = _stream(_weights(inp), order)
    r = _run(nc, [arrays], core_ids=[0])
    got = r.results[0]["outT"]
    return np.ascontiguousarray(got.transpose(2, 1, 0).reshape(1, 512, 1024))
```
